# Optimizing a Trainium2 kernel written in Bass

```python
import jax, jax.numpy as jnp
from jax import lax
import numpy as np
import math

D_MODEL = 1024
BATCH = 1
SEQ = 512
DEPTH = 1

EPS = 1e-6
N_MOD = 6
CONV_WIDTH = D_MODEL
CONV_KERNEL = 31
MLSTM_HEADS = 4
MLSTM_HEAD_DIM = D_MODEL // MLSTM_HEADS
MLSTM_WIDTH = MLSTM_HEADS * MLSTM_HEAD_DIM
QK_CONV = 4
CHUNK = 64
D_FF = ((8 * D_MODEL + 3 * 256 - 1) // (3 * 256)) * 256

N_GLU = 2 * CONV_WIDTH
N_QK = 2 * MLSTM_WIDTH
N_V = MLSTM_WIDTH
N_O = MLSTM_WIDTH
N_IF = 2 * MLSTM_HEADS
N_MERGE = 2 * D_MODEL
N_IN = N_GLU + N_QK + N_V + N_O + N_IF + N_MERGE
IN_SPLITS = (N_GLU, N_GLU + N_QK, N_GLU + N_QK + N_V, N_GLU + N_QK + N_V + N_O,
             N_GLU + N_QK + N_V + N_O + N_IF)
F_BIAS_OFFSET = N_GLU + N_QK + N_V + N_O + MLSTM_HEADS


def rms_norm(x, g):
    xf = x.astype(jnp.float32)
    y = xf * lax.rsqrt(jnp.mean(xf * xf, axis=-1, keepdims=True) + EPS)
    return (y * g.astype(jnp.float32)).astype(x.dtype)

def layer_norm(x, g, b):
    xf = x.astype(jnp.float32)
    mu = jnp.mean(xf, axis=-1, keepdims=True)
    var = jnp.mean(jnp.square(xf - mu), axis=-1, keepdims=True)
    y = (xf - mu) * lax.rsqrt(var + EPS)
    return (y * g.astype(jnp.float32) + b.astype(jnp.float32)).astype(x.dtype)

def causal_depthwise_conv(x, w, b):
    k = w.shape[0]
    y = lax.conv_general_dilated(
        x, w[:, None, :].astype(x.dtype), window_strides=(1,), padding=((k - 1, 0),),
        dimension_numbers=("NWC", "WIO", "NWC"), feature_group_count=x.shape[-1])
    return y + b

def mlstm_chunkwise(q, k, v, i_pre, f_pre):
    bsz, nh, s, dh = q.shape
    nc = s // CHUNK

    def to_chunks(t):
        return jnp.moveaxis(t.reshape(t.shape[:2] + (nc, CHUNK) + t.shape[3:]), 2, 0)

    log_f = jax.nn.log_sigmoid(f_pre)
    xs = (to_chunks(q), to_chunks(k), to_chunks(v), to_chunks(i_pre), to_chunks(log_f))
    causal = jnp.tril(jnp.ones((CHUNK, CHUNK), dtype=bool))

    def step(carry, inp):
        c_st, n_st, m_st = carry
        qc, kc, vc, ic, lfc = inp
        b = jnp.cumsum(lfc, axis=-1)
        d_log = jnp.where(causal, b[..., :, None] - b[..., None, :] + ic[..., None, :], -jnp.inf)
        inter_log = b + m_st[..., None]
        m_t = jnp.maximum(inter_log, jnp.max(d_log, axis=-1))
        dmat = jnp.exp(d_log - m_t[..., None])
        inter_w = jnp.exp(inter_log - m_t)
        sc = jnp.einsum("bhtd,bhsd->bhts", qc, kc) * dmat
        num = (jnp.einsum("bhts,bhse->bhte", sc, vc)
               + inter_w[..., None] * jnp.einsum("bhtd,bhde->bhte", qc, c_st))
        qn = jnp.sum(sc, axis=-1) + inter_w * jnp.einsum("bhtd,bhd->bht", qc, n_st)
        h = num / jnp.maximum(jnp.abs(qn), jnp.exp(-m_t))[..., None]
        b_last = b[..., -1]
        a = b_last[..., None] - b + ic
        m_new = jnp.maximum(b_last + m_st, jnp.max(a, axis=-1))
        decay = jnp.exp(b_last + m_st - m_new)
        w = jnp.exp(a - m_new[..., None])
        c_new = decay[..., None, None] * c_st + jnp.einsum("bhs,bhsd,bhse->bhde", w, kc, vc)
        n_new = decay[..., None] * n_st + jnp.einsum("bhs,bhsd->bhd", w, kc)
        return (c_new, n_new, m_new), h

    init = (jnp.zeros((bsz, nh, dh, dh), jnp.float32),
            jnp.zeros((bsz, nh, dh), jnp.float32),
            jnp.zeros((bsz, nh), jnp.float32))
    _, h = lax.scan(step, init, xs)
    return jnp.moveaxis(h, 0, 2).reshape(bsz, nh, s, dh)

def first_inputs(seed: int = 0) -> dict:
    key = jax.random.key(seed)
    ks = jax.random.split(key, 24)
    f32 = jnp.float32

    def nrm(k, shape, scale):
        return jax.random.normal(k, shape, f32) * scale

    x = jax.random.normal(ks[0], (BATCH, SEQ, D_MODEL), f32)
    c = jax.random.normal(ks[1], (BATCH, D_MODEL), f32)
    w_ada = nrm(ks[2], (DEPTH, D_MODEL, N_MOD * D_MODEL), 0.5 * D_MODEL ** -0.5)
    b_ada = nrm(ks[3], (DEPTH, N_MOD * D_MODEL), 0.02)
    norm_mix_g = 1.0 + nrm(ks[4], (DEPTH, D_MODEL), 0.1)
    w_in = nrm(ks[5], (DEPTH, D_MODEL, N_IN), D_MODEL ** -0.5)
    f_bias = jnp.linspace(3.0, 6.0, MLSTM_HEADS, dtype=f32)
    b_in = nrm(ks[6], (DEPTH, N_IN), 0.02)
    b_in = b_in.at[:, F_BIAS_OFFSET:F_BIAS_OFFSET + MLSTM_HEADS].add(f_bias)
    conv_dw_w = nrm(ks[7], (DEPTH, CONV_KERNEL, CONV_WIDTH), CONV_KERNEL ** -0.5)
    conv_dw_b = nrm(ks[8], (DEPTH, CONV_WIDTH), 0.02)
    conv_ln_g = 1.0 + nrm(ks[9], (DEPTH, CONV_WIDTH), 0.1)
    conv_ln_b = nrm(ks[10], (DEPTH, CONV_WIDTH), 0.02)
    w_conv_pw = nrm(ks[11], (DEPTH, CONV_WIDTH, D_MODEL), CONV_WIDTH ** -0.5)
    b_conv_pw = nrm(ks[12], (DEPTH, D_MODEL), 0.02)
    qk_conv_w = nrm(ks[13], (DEPTH, QK_CONV, N_QK), QK_CONV ** -0.5)
    qk_conv_b = nrm(ks[14], (DEPTH, N_QK), 0.02)
    mlstm_norm_g = 1.0 + nrm(ks[15], (DEPTH, MLSTM_WIDTH), 0.1)
    w_out = nrm(ks[16], (DEPTH, D_MODEL, D_MODEL), D_MODEL ** -0.5)
    norm_ffn_g = 1.0 + nrm(ks[17], (DEPTH, D_MODEL), 0.1)
    w_ffn_up = nrm(ks[18], (DEPTH, D_MODEL, 2 * D_FF), D_MODEL ** -0.5)
    w_ffn_down = nrm(ks[19], (DEPTH, D_FF, D_MODEL), D_FF ** -0.5)
    final_norm_g = 1.0 + nrm(ks[20], (D_MODEL,), 0.1)
    return {"x": x, "c": c, "w_ada": w_ada, "b_ada": b_ada, "norm_mix_g": norm_mix_g,
            "w_in": w_in, "b_in": b_in, "conv_dw_w": conv_dw_w, "conv_dw_b": conv_dw_b,
            "conv_ln_g": conv_ln_g, "conv_ln_b": conv_ln_b, "w_conv_pw": w_conv_pw,
            "b_conv_pw": b_conv_pw, "qk_conv_w": qk_conv_w, "qk_conv_b": qk_conv_b,
            "mlstm_norm_g": mlstm_norm_g, "w_out": w_out, "norm_ffn_g": norm_ffn_g,
            "w_ffn_up": w_ffn_up, "w_ffn_down": w_ffn_down, "final_norm_g": final_norm_g}

def first_block(x, c, w_ada, b_ada, norm_mix_g, w_in, b_in, conv_dw_w, conv_dw_b,
              conv_ln_g, conv_ln_b, w_conv_pw, b_conv_pw, qk_conv_w, qk_conv_b,
              mlstm_norm_g, w_out, norm_ffn_g, w_ffn_up, w_ffn_down, final_norm_g):
    bsz, s, _ = x.shape
    for l in range(DEPTH):
        mod = jnp.einsum("bd,de->be", jax.nn.silu(c), w_ada[l]) + b_ada[l]
        sh1, sc1, g1, sh2, sc2, g2 = jnp.split(mod[:, None, :], N_MOD, axis=-1)

        h = rms_norm(x, norm_mix_g[l]) * (1.0 + sc1) + sh1
        proj = jnp.einsum("bsd,de->bse", h, w_in[l]) + b_in[l]
        glu_in, qk_in, v, o_pre, if_pre, merge_pre = jnp.split(proj, IN_SPLITS, axis=-1)

        a = glu_in[..., :CONV_WIDTH] * jax.nn.sigmoid(glu_in[..., CONV_WIDTH:])
        a = causal_depthwise_conv(a, conv_dw_w[l], conv_dw_b[l])
        a = jax.nn.silu(layer_norm(a, conv_ln_g[l], conv_ln_b[l]))
        y_conv = jnp.einsum("bsc,cd->bsd", a, w_conv_pw[l]) + b_conv_pw[l]

        qk = jax.nn.silu(causal_depthwise_conv(qk_in, qk_conv_w[l], qk_conv_b[l]))
        q, k = jnp.split(qk, 2, axis=-1)

        def heads(t):
            return t.reshape(bsz, s, MLSTM_HEADS, MLSTM_HEAD_DIM).transpose(0, 2, 1, 3).astype(jnp.float32)

        gates = jnp.moveaxis(if_pre, -1, 1).astype(jnp.float32)
        hm = mlstm_chunkwise(heads(q), heads(k) * (MLSTM_HEAD_DIM ** -0.5), heads(v),
                             gates[:, :MLSTM_HEADS], gates[:, MLSTM_HEADS:])
        mu = jnp.mean(hm, axis=-1, keepdims=True)
        var = jnp.mean(jnp.square(hm - mu), axis=-1, keepdims=True)
        hm = ((hm - mu) * lax.rsqrt(var + EPS)).transpose(0, 2, 1, 3).reshape(bsz, s, MLSTM_WIDTH)
        hm = (hm * mlstm_norm_g[l].astype(jnp.float32)).astype(x.dtype)
        y_mlstm = jax.nn.sigmoid(o_pre) * hm

        g_conv, g_mlstm = jnp.split(jax.nn.sigmoid(merge_pre), 2, axis=-1)
        y = jnp.einsum("bsd,de->bse", g_conv * y_conv + g_mlstm * y_mlstm, w_out[l])
        x = x + g1 * y

        h = rms_norm(x, norm_ffn_g[l]) * (1.0 + sc2) + sh2
        gt, up = jnp.split(jnp.einsum("bsd,df->bsf", h, w_ffn_up[l]), 2, axis=-1)
        x = x + g2 * jnp.einsum("bsf,fd->bsd", jax.nn.silu(gt) * up, w_ffn_down[l])
    return rms_norm(x, final_norm_g)


DEPTH_2 = 2

N_MEM = 256
HEAD_DIM = 64
MIX_WIDTH = 3 * D_MODEL // 4
MIX_HEADS = MIX_WIDTH // HEAD_DIM
MEM_HEADS = 4
MEM_WIDTH = MEM_HEADS * HEAD_DIM
NSA_KV_GROUPS = 4
NSA_GROUP_SIZE = MIX_HEADS // NSA_KV_GROUPS
KV_WIDTH = NSA_KV_GROUPS * HEAD_DIM
CMP_BLOCK = 32
CMP_STRIDE = 16
CMP_HIDDEN = 2 * HEAD_DIM
SEL_BLOCK = 64
SEL_TOPN = 16
WINDOW = 512
NSA_Q_BLOCK = 64
FORCE_SCORE = 1.0e4
NSA_IN = MIX_WIDTH + 6 * KV_WIDTH + 3 * MIX_HEADS + MEM_WIDTH
DECAY_LORA = 64
ICLR_LORA = 64
GATE_LORA = 160
RW_SHIFT = 3 * MIX_WIDTH + DECAY_LORA + ICLR_LORA + GATE_LORA
RW_IN = RW_SHIFT + MEM_WIDTH
GN_EPS = 64e-5
FFN_HIDDEN = -(-8 * D_MODEL // (3 * 256)) * 256
N_NSA = (DEPTH_2 + 1) // 2
N_RWKV = DEPTH_2 // 2
RMS_EPS = 1e-6
NEG_INF = -1e30


def _rmsnorm(x, g):
    xf = x.astype(jnp.float32)
    y = xf * lax.rsqrt(jnp.mean(xf * xf, axis=-1, keepdims=True) + RMS_EPS)
    return (y * g.astype(jnp.float32)).astype(x.dtype)

def _split(x, sizes):
    idx = [int(i) for i in np.cumsum(sizes)[:-1]]
    return jnp.split(x, idx, axis=-1)

def _alibi_slopes(n):
    def pow2(m):
        start = 2.0 ** (-8.0 / m)
        return [start ** (i + 1) for i in range(m)]
    c = 2 ** int(math.floor(math.log2(n)))
    s = pow2(c)
    if c < n:
        s = s + pow2(2 * c)[0::2][: n - c]
    return np.asarray(s, dtype=np.float32)

def _masked_softmax(s, mask):
    p = jax.nn.softmax(jnp.where(mask, s, NEG_INF), axis=-1)
    return p * mask

def _compress(kv, pos, w1, w2):
    S = kv.shape[1]
    n_cmp = (S - CMP_BLOCK) // CMP_STRIDE + 1
    idx = jnp.arange(n_cmp)[:, None] * CMP_STRIDE + jnp.arange(CMP_BLOCK)[None, :]
    blocks = kv[:, idx] + pos[None, None, :, None, :]
    hid = jax.nn.gelu(jnp.einsum('bnlgd,lde->bnge', blocks, w1))
    return jnp.einsum('bnge,ed->bngd', hid, w2)

def _nsa_mixer(h, w_in, gate_b, cmp_pos, cmp_w1, cmp_w2):
    B, S, _ = h.shape
    G, R, Dh, QB = NSA_KV_GROUPS, NSA_GROUP_SIZE, HEAD_DIM, NSA_Q_BLOCK
    proj = h @ w_in
    q, kc, vc, ks, vs, kw, vw, gl, q_mem = _split(
        proj, [MIX_WIDTH] + [KV_WIDTH] * 6 + [3 * MIX_HEADS, MEM_WIDTH])
    q = q.reshape(B, S, G, R, Dh)
    kc, vc, ks, vs, kw, vw = (t.reshape(B, S, G, Dh) for t in (kc, vc, ks, vs, kw, vw))
    gates = jax.nn.sigmoid(gl + gate_b).reshape(B, S, 3, G, R)

    kc_b = _compress(kc, cmp_pos[0], cmp_w1[0], cmp_w2[0])
    vc_b = _compress(vc, cmp_pos[1], cmp_w1[1], cmp_w2[1])
    n_cmp = kc_b.shape[1]
    n_blk = S // SEL_BLOCK
    n_sel = min(SEL_TOPN, n_blk)
    ks_blk = ks.reshape(B, n_blk, SEL_BLOCK, G, Dh).transpose(0, 3, 1, 2, 4)
    vs_blk = vs.reshape(B, n_blk, SEL_BLOCK, G, Dh).transpose(0, 3, 1, 2, 4)
    kw_pad = jnp.pad(kw, ((0, 0), (WINDOW, 0), (0, 0), (0, 0)))
    vw_pad = jnp.pad(vw, ((0, 0), (WINDOW, 0), (0, 0), (0, 0)))

    slopes = jnp.asarray(_alibi_slopes(MIX_HEADS).reshape(G, R))[None, :, :, None, None]
    cmp_start = jnp.arange(n_cmp) * CMP_STRIDE
    cmp_end = cmp_start + CMP_BLOCK - 1
    sel_start = jnp.arange(n_blk) * SEL_BLOCK
    overlap = ((cmp_start[:, None] <= sel_start[None, :] + SEL_BLOCK - 1)
               & (cmp_end[:, None] >= sel_start[None, :])).astype(jnp.float32)
    blk_ids = jnp.arange(n_blk)
    b_idx = jnp.arange(B)[:, None, None, None]
    g_idx = jnp.arange(G)[None, :, None, None]
    scale = HEAD_DIM ** -0.5

    def chunk(c0):
        t = c0 + jnp.arange(QB)
        qc = lax.dynamic_slice_in_dim(q, c0, QB, axis=1)
        dist_c = t[:, None] - cmp_end[None, :]
        s_c = jnp.einsum('bqgrd,bngd->bgrqn', qc, kc_b).astype(jnp.float32) * scale \
            - slopes * dist_c.astype(jnp.float32)
        p_c = _masked_softmax(s_c, dist_c >= 0)
        o_c = jnp.einsum('bgrqn,bngd->bqgrd', p_c.astype(vc_b.dtype), vc_b)
        imp = jnp.einsum('bgrqn,nj->bgqj', p_c, overlap)
        tb = (t // SEL_BLOCK)[:, None]
        valid = blk_ids[None, :] <= tb
        forced = (blk_ids[None, :] == 0) | (blk_ids[None, :] == tb) | (blk_ids[None, :] == tb - 1)
        score = jnp.where(valid, jnp.where(forced, FORCE_SCORE, imp), -jnp.inf)
        top_s, top_i = lax.top_k(score, n_sel)
        kg = ks_blk[b_idx, g_idx, top_i].reshape(B, G, QB, n_sel * SEL_BLOCK, Dh)
        vg = vs_blk[b_idx, g_idx, top_i].reshape(B, G, QB, n_sel * SEL_BLOCK, Dh)
        pos = (top_i[..., None] * SEL_BLOCK + jnp.arange(SEL_BLOCK)).reshape(B, G, QB, -1)
        ok = jnp.broadcast_to(jnp.isfinite(top_s)[..., None],
                              (B, G, QB, n_sel, SEL_BLOCK)).reshape(B, G, QB, -1)
        dist_s = t[None, None, :, None] - pos
        mask_s = ok & (dist_s >= 0)
        s_s = jnp.einsum('bqgrd,bgqkd->bgrqk', qc, kg).astype(jnp.float32) * scale \
            - slopes * dist_s[:, :, None].astype(jnp.float32)
        p_s = _masked_softmax(s_s, mask_s[:, :, None])
        o_s = jnp.einsum('bgrqk,bgqkd->bqgrd', p_s.astype(vg.dtype), vg)
        kwc = lax.dynamic_slice_in_dim(kw_pad, c0, WINDOW + QB, axis=1)
        vwc = lax.dynamic_slice_in_dim(vw_pad, c0, WINDOW + QB, axis=1)
        kp = c0 - WINDOW + jnp.arange(WINDOW + QB)
        dist_w = t[:, None] - kp[None, :]
        mask_w = (kp[None, :] >= 0) & (dist_w >= 0) & (dist_w < WINDOW)
        s_w = jnp.einsum('bqgrd,bkgd->bgrqk', qc, kwc).astype(jnp.float32) * scale \
            - slopes * dist_w.astype(jnp.float32)
        p_w = _masked_softmax(s_w, mask_w)
        o_w = jnp.einsum('bgrqk,bkgd->bqgrd', p_w.astype(vwc.dtype), vwc)
        gc = lax.dynamic_slice_in_dim(gates, c0, QB, axis=1)[..., None]
        return gc[:, :, 0] * o_c + gc[:, :, 1] * o_s + gc[:, :, 2] * o_w

    starts = jnp.arange(S // QB) * QB
    o = lax.map(chunk, starts)
    o = jnp.moveaxis(o, 0, 1).reshape(B, S, MIX_WIDTH)
    return o, q_mem

def _wkv7_scan(r, w, k, v, a, b):
    B, S, H, N = r.shape

    def step(state, inp):
        r_t, w_t, k_t, v_t, a_t, b_t = inp
        sa = jnp.einsum('bhvk,bhk->bhv', state, a_t)
        state = state * w_t[:, :, None, :] + sa[..., None] * b_t[:, :, None, :] \
            + v_t[..., None] * k_t[:, :, None, :]
        return state, jnp.einsum('bhvk,bhk->bhv', state, r_t)

    xs = tuple(jnp.moveaxis(t, 1, 0) for t in (r, w, k, v, a, b))
    s0 = jnp.zeros((B, H, N, N), jnp.float32)
    _, y = lax.scan(step, s0, xs)
    return jnp.moveaxis(y, 0, 1)

def _rwkv7_mixer(h, w_in, mu, w0, w2, a0, a2, g2, k_k, k_a, r_k, lnx_w, lnx_b):
    B, S, _ = h.shape
    H, N = MIX_HEADS, HEAD_DIM
    proj = h @ w_in
    z, q_mem = proj[..., :RW_SHIFT], proj[..., RW_SHIFT:]
    z_prev = jnp.pad(z, ((0, 0), (1, 0), (0, 0)))[:, :-1]
    z = z + (z_prev - z) * mu
    r, k, v, zw, za, zg = _split(z, [MIX_WIDTH] * 3 + [DECAY_LORA, ICLR_LORA, GATE_LORA])
    w_log = -jax.nn.softplus(-(w0 + jnp.tanh(zw) @ w2)) - 0.5
    decay = jnp.exp(-jnp.exp(w_log.astype(jnp.float32)))
    a = jax.nn.sigmoid(a0 + za @ a2)
    g = jax.nn.sigmoid(zg) @ g2
    kk = (k * k_k).astype(jnp.float32).reshape(B, S, H, N)
    kk = kk / jnp.maximum(jnp.sqrt(jnp.sum(kk * kk, axis=-1, keepdims=True)), 1e-12)
    k = k * (1 + (a - 1) * k_a)

    def heads(t):
        return t.astype(jnp.float32).reshape(B, S, H, N)

    rh, wh, kh, vh, ah = heads(r), heads(decay), heads(k), heads(v), heads(a)
    y = _wkv7_scan(rh, wh, kh, vh, -kk, kk * ah)
    mean = jnp.mean(y, axis=-1, keepdims=True)
    var = jnp.mean(jnp.square(y - mean), axis=-1, keepdims=True)
    y = ((y - mean) * lax.rsqrt(var + GN_EPS)).reshape(B, S, MIX_WIDTH)
    y = y * lnx_w.astype(jnp.float32) + lnx_b.astype(jnp.float32)
    bonus = jnp.sum(rh * kh * r_k.astype(jnp.float32), axis=-1, keepdims=True) * vh
    out = (y + bonus.reshape(B, S, MIX_WIDTH)) * g.astype(jnp.float32)
    return out.astype(h.dtype), q_mem

def _mem_attention(q_mem, mem_n, w_kv):
    B, S, _ = q_mem.shape
    M = mem_n.shape[1]
    k, v = jnp.split(mem_n @ w_kv, 2, axis=-1)
    q = q_mem.reshape(B, S, MEM_HEADS, HEAD_DIM)
    k = k.reshape(B, M, MEM_HEADS, HEAD_DIM)
    v = v.reshape(B, M, MEM_HEADS, HEAD_DIM)
    s = jnp.einsum('bshd,bmhd->bhsm', q, k).astype(jnp.float32) * (HEAD_DIM ** -0.5)
    p = jax.nn.softmax(s, axis=-1).astype(v.dtype)
    return jnp.einsum('bhsm,bmhd->bshd', p, v).reshape(B, S, MEM_WIDTH)

def _swiglu(h, w_in, w_out):
    gate, up = jnp.split(h @ w_in, 2, axis=-1)
    return (jax.nn.silu(gate) * up) @ w_out

def second_inputs(seed: int = 0) -> dict:
    key = jax.random.key(seed)
    ks = jax.random.split(key, 32)
    f32 = jnp.float32

    def nrm(k, shape, scale):
        return jax.random.normal(k, shape, f32) * scale

    D = D_MODEL
    return {
        'x': nrm(ks[0], (BATCH, SEQ, D), 1.0),
        'mem': nrm(ks[1], (BATCH, N_MEM, D), 1.0),
        'norm1': 1.0 + nrm(ks[2], (DEPTH_2, D), 0.05),
        'norm_mem': 1.0 + nrm(ks[3], (DEPTH_2, D), 0.05),
        'w_mem_kv': nrm(ks[4], (DEPTH_2, D, 2 * MEM_WIDTH), D ** -0.5),
        'w_o': nrm(ks[5], (DEPTH_2, MIX_WIDTH + MEM_WIDTH, D), (MIX_WIDTH + MEM_WIDTH) ** -0.5),
        'norm2': 1.0 + nrm(ks[6], (DEPTH_2, D), 0.05),
        'w_ffn_in': nrm(ks[7], (DEPTH_2, D, 2 * FFN_HIDDEN), D ** -0.5),
        'w_ffn_out': nrm(ks[8], (DEPTH_2, FFN_HIDDEN, D), FFN_HIDDEN ** -0.5),
        'nsa_w_in': nrm(ks[9], (N_NSA, D, NSA_IN), D ** -0.5),
        'nsa_gate_b': nrm(ks[10], (N_NSA, 3 * MIX_HEADS), 0.1),
        'nsa_cmp_pos': nrm(ks[11], (N_NSA, 2, CMP_BLOCK, HEAD_DIM), 0.1),
        'nsa_cmp_w1': nrm(ks[12], (N_NSA, 2, CMP_BLOCK, HEAD_DIM, CMP_HIDDEN), (CMP_BLOCK * HEAD_DIM) ** -0.5),
        'nsa_cmp_w2': nrm(ks[13], (N_NSA, 2, CMP_HIDDEN, HEAD_DIM), CMP_HIDDEN ** -0.5),
        'rw_w_in': nrm(ks[14], (N_RWKV, D, RW_IN), D ** -0.5),
        'rw_mu': jax.random.uniform(ks[15], (N_RWKV, RW_SHIFT), f32),
        'rw_w0': jax.random.uniform(ks[16], (N_RWKV, MIX_WIDTH), f32, -5.0, 1.0),
        'rw_w2': nrm(ks[17], (N_RWKV, DECAY_LORA, MIX_WIDTH), 0.1 * DECAY_LORA ** -0.5),
        'rw_a0': nrm(ks[18], (N_RWKV, MIX_WIDTH), 0.5),
        'rw_a2': nrm(ks[19], (N_RWKV, ICLR_LORA, MIX_WIDTH), 0.3 * ICLR_LORA ** -0.5),
        'rw_g2': nrm(ks[20], (N_RWKV, GATE_LORA, MIX_WIDTH), GATE_LORA ** -0.5),
        'rw_k_k': 0.85 + nrm(ks[21], (N_RWKV, MIX_WIDTH), 0.05),
        'rw_k_a': 1.0 + nrm(ks[22], (N_RWKV, MIX_WIDTH), 0.05),
        'rw_r_k': nrm(ks[23], (N_RWKV, MIX_HEADS, HEAD_DIM), 0.1),
        'rw_lnx_w': 1.0 + nrm(ks[24], (N_RWKV, MIX_WIDTH), 0.05),
        'rw_lnx_b': nrm(ks[25], (N_RWKV, MIX_WIDTH), 0.02),
        'final_norm': 1.0 + nrm(ks[26], (D,), 0.05),
    }

def second_block(x, mem, norm1, norm_mem, w_mem_kv, w_o, norm2, w_ffn_in, w_ffn_out,
              nsa_w_in, nsa_gate_b, nsa_cmp_pos, nsa_cmp_w1, nsa_cmp_w2,
              rw_w_in, rw_mu, rw_w0, rw_w2, rw_a0, rw_a2, rw_g2, rw_k_k, rw_k_a, rw_r_k,
              rw_lnx_w, rw_lnx_b, final_norm):
    for i in range(DEPTH_2):
        j = i // 2
        hn = _rmsnorm(x, norm1[i])
        mn = _rmsnorm(mem, norm_mem[i])
        if i % 2 == 0:
            mix, q_mem = _nsa_mixer(hn, nsa_w_in[j], nsa_gate_b[j], nsa_cmp_pos[j],
                                    nsa_cmp_w1[j], nsa_cmp_w2[j])
        else:
            mix, q_mem = _rwkv7_mixer(hn, rw_w_in[j], rw_mu[j], rw_w0[j], rw_w2[j], rw_a0[j],
                                      rw_a2[j], rw_g2[j], rw_k_k[j], rw_k_a[j], rw_r_k[j],
                                      rw_lnx_w[j], rw_lnx_b[j])
        cross = _mem_attention(q_mem, mn, w_mem_kv[i])
        x = x + jnp.concatenate([mix, cross], axis=-1) @ w_o[i]
        x = x + _swiglu(_rmsnorm(x, norm2[i]), w_ffn_in[i], w_ffn_out[i])
    return _rmsnorm(x, final_norm)


def setup_inputs(seed=0):
    out = dict(first_inputs(seed))
    for name, value in second_inputs(seed + 1).items():
        if name != "x":
            out[name + "_2"] = value
    return out


def reference(
    x, c, w_ada, b_ada, norm_mix_g, w_in, b_in, conv_dw_w, conv_dw_b, conv_ln_g, conv_ln_b,
    w_conv_pw, b_conv_pw, qk_conv_w, qk_conv_b, mlstm_norm_g, w_out, norm_ffn_g, w_ffn_up,
    w_ffn_down, final_norm_g, mem_2, norm1_2, norm_mem_2, w_mem_kv_2, w_o_2, norm2_2,
    w_ffn_in_2, w_ffn_out_2, nsa_w_in_2, nsa_gate_b_2, nsa_cmp_pos_2, nsa_cmp_w1_2,
    nsa_cmp_w2_2, rw_w_in_2, rw_mu_2, rw_w0_2, rw_w2_2, rw_a0_2, rw_a2_2, rw_g2_2, rw_k_k_2,
    rw_k_a_2, rw_r_k_2, rw_lnx_w_2, rw_lnx_b_2, final_norm_2,
):
    x = first_block(
        x, c, w_ada, b_ada, norm_mix_g, w_in, b_in, conv_dw_w, conv_dw_b, conv_ln_g, conv_ln_b,
        w_conv_pw, b_conv_pw, qk_conv_w, qk_conv_b, mlstm_norm_g, w_out, norm_ffn_g, w_ffn_up,
        w_ffn_down, final_norm_g,
    )
    return second_block(
        x, mem_2, norm1_2, norm_mem_2, w_mem_kv_2, w_o_2, norm2_2, w_ffn_in_2, w_ffn_out_2,
        nsa_w_in_2, nsa_gate_b_2, nsa_cmp_pos_2, nsa_cmp_w1_2, nsa_cmp_w2_2, rw_w_in_2, rw_mu_2,
        rw_w0_2, rw_w2_2, rw_a0_2, rw_a2_2, rw_g2_2, rw_k_k_2, rw_k_a_2, rw_r_k_2, rw_lnx_w_2,
        rw_lnx_b_2, final_norm_2,
    )


_drawn_inputs = setup_inputs


def setup_inputs(seed=0):
    import zlib

    import numpy as np

    out = dict(_drawn_inputs(seed))
    spreads = {}
    factors = {'conv_dw_b': 8.0,
     'conv_ln_g': 3.247,
     'conv_ln_b': 8.0,
     'b_conv_pw': 8.0,
     'qk_conv_b': 8.0,
     'mlstm_norm_g': 4.103,
     'norm_mem_2': 8.0,
     'rw_w2_2': 25.33,
     'rw_k_k_2': 23.325,
     'rw_lnx_w_2': 11.818,
     'rw_lnx_b_2': 28.792,
     'nsa_gate_b_2': 4.764,
     'nsa_cmp_pos_2': 2.706,
     'rw_k_a_2': 3.319,
     'rw_r_k_2': 2.669}
    for name, (base, spread) in spreads.items():
        noise = np.random.default_rng([zlib.crc32(name.encode()), seed]).standard_normal(out[name].shape)
        drawn = base * np.exp(spread * noise) if base else spread * noise
        out[name] = __import__('jax').numpy.asarray(drawn.astype(out[name].dtype))
    for name, factor in factors.items():
        out[name] = (out[name] * factor).astype(out[name].dtype)
    return out
```

```python
from contextlib import ExitStack

import numpy as np

import concourse.bass as bass
from concourse import mybir

P = 128
D = 1024
S = 512
DT = D // P
SLOT_COLS = 256
FF = 2816
FT = FF // P
TAPS = 31
QK_TAPS = 4
ML_HEADS = 4
N_MEM = 256
MT = 2
HEADS = 12
GROUPS = 4
DH = 64
N_CMP = (S - 32) // 16 + 1
CHUNK = 64
EPS = 1e-6
GN_EPS = 64e-5
BIG = 1.0e30

F32 = mybir.dt.float32
F32R = mybir.dt.float32r
ACT = mybir.ActivationFunctionType
ALU = mybir.AluOpType
AX = mybir.AxisListType

PHASES_LIST = [
    ("ada1", 8, 8),
    ("glu", 8, 8),
    ("qk", 8, 8),
    ("v", 4, 4),
    ("if", 1, 1),
    ("ada2", 16, 16),
    ("pw", 4, 4),
    ("o", 4, 4),
    ("merge", 8, 8),
    ("w_out", 4, 4),
    ("up_a", 22, 22), ("down_a", 12, 4),
    ("memkv0", 2, 2), ("nsa", 11, 11), ("wo0", 4, 4), ("up_b", 22, 22), ("down_b", 12, 4),
    ("memkv1", 2, 2), ("rwkv", 12, 12), ("wo1", 4, 4), ("up_c", 22, 22), ("down_c", 12, 4),
]


def phase_table():
    table, n, u = {}, 0, 0
    for name, slots, units in PHASES_LIST:
        table[name] = (n, u)
        n += slots
        u += units
    return table, n, u


PH, N_SLOTS, N_UNITS = phase_table()

COLS_LIST = [
    ("c", 8), ("b_ada", 48), ("norm_mix_g", 8), ("b_glu", 16), ("b_qk", 16), ("b_o", 8), ("b_merge", 16),
    ("b_i", 1), ("b_f", 1), ("conv_w", 8 * TAPS), ("conv_b", 8), ("ln_g", 8), ("ln_b", 8), ("b_pw", 8),
    ("qk_w", 16 * QK_TAPS), ("qk_b", 16), ("mlstm_g", 8), ("ffn_g", 8), ("final_g", 8),
    ("norm1", 16), ("norm_mem", 16), ("norm2", 16), ("final2", 8),
    ("mu", 21), ("w0", 6), ("a0", 6), ("k_k", 6), ("k_a", 6), ("r_k", 6), ("lnx_w", 6), ("lnx_b", 6),
    ("row_b_v", D), ("row_gate_b", 36),
    ("ident", P), ("after", P), ("dist", S), ("dist_c", 4 * N_CMP), ("seen_c", 4 * N_CMP),
]


def cols_table():
    table, at = {}, 0
    for name, n in COLS_LIST:
        table[name] = (at, n)
        at += n
    return table, at


CT, N_COLS = cols_table()


def _tiles(v):
    v = np.asarray(v)
    pad = -len(v) % P
    if pad:
        v = np.concatenate([v, np.zeros(pad, v.dtype)])
    return v.reshape(-1, P).T


def _slot(w):
    out = np.zeros((D, SLOT_COLS), np.float32)
    out[: w.shape[0], : w.shape[1]] = w
    return out.reshape(DT, P, SLOT_COLS).transpose(1, 0, 2).reshape(P, DT * SLOT_COLS)


def _groups(w):
    return [_slot(w[:, g:g + SLOT_COLS]) for g in range(0, w.shape[1], SLOT_COLS)]


def _pairs(w, half):
    return [s for g in range(0, half, SLOT_COLS)
            for s in (_slot(w[:, g:g + SLOT_COLS]), _slot(w[:, half + g:half + g + SLOT_COLS]))]


def _down(w):
    return [_slot(w[k:k + D, g:g + SLOT_COLS]) for g in range(0, D, SLOT_COLS) for k in range(0, FF, D)]


def stream_of_weights(a):
    w_in = a["w_in"][0]
    gates = np.zeros((D, SLOT_COLS), np.float32)
    gates[:, 0:4] = w_in[:, 6144:6148]
    gates[:, P:P + 4] = w_in[:, 6148:6152]
    nsa, rw = a["nsa_w_in_2"][0], a["rw_w_in_2"][0]
    ada = _groups(a["w_ada"][0])
    slots = ada[:8]
    slots += _pairs(w_in[:, 0:2048], D)
    slots += _groups(w_in[:, 2048:4096])
    slots += _groups(w_in[:, 4096:5120])
    slots += [_slot(gates)]
    slots += ada[8:]
    slots += _groups(a["w_conv_pw"][0])
    slots += _groups(w_in[:, 5120:6144])
    slots += _groups(w_in[:, 6152:8200])
    slots += _groups(a["w_out"][0])
    slots += _pairs(a["w_ffn_up"][0], FF) + _down(a["w_ffn_down"][0])
    slots += _groups(a["w_mem_kv_2"][0])
    slots += _groups(nsa[:, 0:2304]) + [_slot(nsa[:, 2304:2340]), _slot(nsa[:, 2340:2596])]
    slots += _groups(a["w_o_2"][0]) + _pairs(a["w_ffn_in_2"][0], FF) + _down(a["w_ffn_out_2"][0])
    slots += _groups(a["w_mem_kv_2"][1])
    slots += _groups(rw[:, 0:2592]) + [_slot(rw[:, 2592:2848])]
    slots += _groups(a["w_o_2"][1]) + _pairs(a["w_ffn_in_2"][1], FF) + _down(a["w_ffn_out_2"][1])
    assert len(slots) == N_SLOTS
    return np.stack(slots)


def parameter_columns(a):
    c = {}
    b_in = a["b_in"][0]
    c["c"] = _tiles(a["c"][0])
    c["b_ada"] = _tiles(a["b_ada"][0])
    c["norm_mix_g"] = _tiles(a["norm_mix_g"][0])
    c["b_glu"] = _tiles(b_in[0:2048])
    c["b_qk"] = _tiles(b_in[2048:4096])
    c["b_o"] = _tiles(b_in[5120:6144])
    c["b_i"] = _tiles(b_in[6144:6148])
    c["b_f"] = _tiles(b_in[6148:6152])
    c["b_merge"] = _tiles(b_in[6152:8200])
    c["conv_w"] = a["conv_dw_w"][0].reshape(TAPS, 8, P).transpose(2, 1, 0).reshape(P, -1)
    c["conv_b"] = _tiles(a["conv_dw_b"][0])
    c["ln_g"] = _tiles(a["conv_ln_g"][0])
    c["ln_b"] = _tiles(a["conv_ln_b"][0])
    c["b_pw"] = _tiles(a["b_conv_pw"][0])
    c["qk_w"] = a["qk_conv_w"][0].reshape(QK_TAPS, 16, P).transpose(2, 1, 0).reshape(P, -1)
    c["qk_b"] = _tiles(a["qk_conv_b"][0])
    c["mlstm_g"] = _tiles(a["mlstm_norm_g"][0])
    c["ffn_g"] = _tiles(a["norm_ffn_g"][0])
    c["final_g"] = _tiles(a["final_norm_g"])
    for name, key in (("norm1", "norm1_2"), ("norm_mem", "norm_mem_2"), ("norm2", "norm2_2")):
        c[name] = np.concatenate([_tiles(a[key][0]), _tiles(a[key][1])], 1)
    c["final2"] = _tiles(a["final_norm_2"])
    c["mu"] = _tiles(a["rw_mu_2"][0])
    for name in ("w0", "a0", "k_k", "k_a", "lnx_w", "lnx_b"):
        c[name] = _tiles(a[f"rw_{name}_2"][0])
    c["r_k"] = _tiles(a["rw_r_k_2"][0].reshape(-1))
    c["row_b_v"] = np.broadcast_to(b_in[4096:5120], (P, D))
    c["row_gate_b"] = np.broadcast_to(a["nsa_gate_b_2"][0], (P, 36))
    p, j = np.arange(P)[:, None], np.arange(P)[None, :]
    c["ident"] = (p == j).astype(np.float32)
    c["after"] = np.where(p > j, -BIG, 0.0).astype(np.float32)
    u = np.arange(S)[None, :] - (S - P)
    c["dist"] = np.where(u <= p, p - u, BIG).astype(np.float32)
    t = np.arange(4)[None, :, None] * P + np.arange(P)[:, None, None]
    dc = t - (16 * np.arange(N_CMP) + 31)[None, None, :]
    c["dist_c"] = np.where(dc >= 0, dc, BIG).astype(np.float32).reshape(P, -1)
    c["seen_c"] = (dc >= 0).astype(np.float32).reshape(P, -1)
    for name, n in COLS_LIST:
        assert c[name].shape == (P, n), (name, c[name].shape)
    return np.concatenate([np.asarray(c[name], np.float32) for name, _ in COLS_LIST], 1)


def by_tiles(x):
    return np.ascontiguousarray(x.T.reshape(-1, P, x.shape[0]).transpose(1, 0, 2))


def compression_weights(a):
    pos, w1, w2 = a["nsa_cmp_pos_2"][0], a["nsa_cmp_w1_2"][0], a["nsa_cmp_w2_2"][0]
    pos = np.tile(pos.transpose(2, 0, 1), (2, 1, 1))
    w1 = np.tile(w1.transpose(0, 2, 1, 3), (1, 2, 1, 1))
    return pos, w1, np.concatenate([w2[0], w2[0], w2[1]], 1)


def recurrence_constants():
    a, b = np.arange(64)[:, None], np.arange(64)[None, :]
    same = a // 16 == b // 16
    masks = [a < b, a <= b, same & (a > b), same & (a < b), ~same & (a > b), a == b]
    p, q = np.arange(P)[:, None], np.arange(P)[None, :]
    half = (p // 64 == q // 64).astype(np.float32)
    masks = [np.tile(m.astype(np.float32), (2, 1)) for m in masks]
    return np.concatenate(masks + [half / 64, half], 1).astype(np.float32)


def selectors():
    return (np.arange(4)[:, None, None] == np.arange(4)[None, :, None]).astype(np.float32).repeat(P, 2)


class Chain:

    def __init__(self, eng, sem):
        self.eng, self.sem, self.n = eng, sem, 0

    def link(self, ins):
        ins.then_inc(self.sem, 1)
        self.n = self.n + 1
        self.eng.wait_ge(self.sem, self.n)


def flat(ap):
    return ap.rearrange("p a b -> p (a b)")


def shared_signals():
    table = {}

    def again(semaphore, counts):
        base = 0
        for name, count in counts:
            table[name] = (semaphore, base)
            base += count

    split = ("n1", "cln", "nfa", "mem0", "l0", "nfb", "mem1", "l1", "nfc")
    in_place = ("fin1", "fin2")
    order = ("n1", "cln", "nfa", "fin1", "mem0", "l0", "nfb", "mem1", "l1", "nfc", "fin2")
    for kind, count in (("sq", DT), ("sum", DT), ("std", 1), ("rstd", 1)):
        again("norm_" + kind, [(f"{n}_{kind}", count) for n in order])
    for kind in ("t", "hi", "lo"):
        again("norm_" + kind, [(f"{n}_{kind}", DT) for n in order if n in split])
    again("norm_x", [(f"{n}_x", DT) for n in in_place])
    for kind in ("silu", "hid_hi", "hid_lo"):
        again(kind, [(f"{kind}_{n}", FT) for n in "abc"])
    again("gate_sigmoid", [("sig_o", DT), ("sig_merge", 2 * DT)])
    full, mem = 4 * (3 * HEADS + 4), 16
    for kind, count in (("scores", full), ("neg", full), ("exp", full), ("pT", full), ("turned", full),
                        ("out", full), ("group", 16), ("seen", 4 * HEADS)):
        again("at_" + kind, [(f"at_{kind}0", count), (f"at_{kind}1", 0)])
    again("cat_turned", [("cat_turned0", DT), ("cat_turned1", 2)])
    again("cat_hi", [("cat_hi0", DT), ("cat_hi1", 2)])
    again("cat_lo", [("cat_lo0", DT), ("cat_lo1", 2)])
    return table


SHARED = shared_signals()


class Kernel:

    def __init__(self, nc, ctx):
        self.nc, self.ctx, self.sems = nc, ctx, {}

    def sem(self, name):
        name = SHARED.get(name, (name, 0))[0]
        if name not in self.sems:
            self.sems[name] = self.ctx.enter_context(self.nc.semaphore(name))
        return self.sems[name]

    def on(self, name, value):
        return self.sem(name), value + SHARED.get(name, (name, 0))[1]

    def col(self, name, j=0, n=1):
        at, width = CT[name]
        return self.cols[:, at + j:at + j + n]


def rounds(eng, count, body):
    if count == 1:
        body(0)
    else:
        with eng.Fori(0, count) as i:
            body(i)


def chained_rounds(chain, count, per, body):
    base = chain.n

    def one(i):
        chain.n = i * per + base
        body(i)

    rounds(chain.eng, count, one)
    chain.n = base + per * count


def bank_pair(u):
    return 2 * (u % 4)


def sync_program(k, sp):
    sp.dma_start(k.cols[:], k.cols_dram).then_inc(k.sem("cols_landed"), 16)
    sp.dma_start(flat(k.raw[0]), k.slots_dram[0]).then_inc(k.raw_landed[0], 16)
    sp.dma_start(flat(k.raw[1]), k.slots_dram[1]).then_inc(k.raw_landed[1], 16)
    sp.dma_start(k.xT[:], k.x_dram).then_inc(k.sem("x_landed"), 16)
    sp.dma_start(k.row_bv[:], k.row_bv_dram).then_inc(k.sem("row_bv_landed"), 16)
    sp.dma_start(k.sel[:], k.sel_dram).then_inc(k.sem("sel_landed"), 16)

    def pair(i):
        for j in range(2):
            sp.wait_ge(*k.on("w_low", i * 2 + (j + 1)))
            src = k.slots_dram[bass.ds(i * 2 + (2 + j), 1)].rearrange("a p n -> (a p) n")
            sp.dma_start(flat(k.raw[j]), src).then_inc(k.raw_landed[j], 16)

    rounds(sp, k.n_slots // 2 - 1, pair)
    if k.n_slots % 2:
        sp.wait_ge(*k.on("w_low", k.n_slots - 2))
        sp.dma_start(flat(k.raw[0]), k.slots_dram[k.n_slots - 1]).then_inc(k.raw_landed[0], 16)
    sp.wait_ge(*k.on("fin2_x", DT))
    sp.dma_start(k.out_dram, k.xT[:]).then_inc(k.sem("out_stored"), 16)
    sp.wait_ge(k.sem("out_stored"), 16)


def gpsimd_program(k, pool):
    def pair(i):
        for j in range(2):
            pool.wait_ge(*k.on("w_high", i * 2 + (j + 1)))
            pool.tensor_tensor(flat(k.w_lo[j]), flat(k.raw[j]), flat(k.w_hi[j]).bitcast(F32),
                               ALU.subtract).then_inc(k.sem("w_low"), 1)

    rounds(pool, k.n_slots // 2, pair)
    if k.n_slots % 2:
        pool.wait_ge(*k.on("w_high", k.n_slots))
        pool.tensor_tensor(flat(k.w_lo[0]), flat(k.raw[0]), flat(k.w_hi[0]).bitcast(F32),
                           ALU.subtract).then_inc(k.sem("w_low"), 1)


def pe_slot(k, pe, n0, j, i, per, rhs, width=S, k0=0, kts=DT, start=True, stop=True, banks=None,
            natural=False):
    par = (n0 + j) % 2
    pe.wait_ge(*k.on("w_low", i * per + (n0 + j + 1)))
    wh, wl = k.w_hi[par], k.w_lo[par]
    xh, xl = rhs
    if natural:
        for e in range(2):
            for q in range(2):
                for kt in range(kts):
                    for a, (x, w) in enumerate(((xh, wh), (xh, wl), (xl, wh))):
                        t = 2 * e + q
                        mm = pe.matmul(k.ps[:, banks + e, q * width:(q + 1) * width],
                                       x[:, kt, t * P:(t + 1) * P], w[:, kt, 0:width],
                                       start=(kt == 0 and a == 0), stop=(kt == kts - 1 and a == 2))
            mm.then_inc(k.sem("mm_done"), 1)
        return
    for e in range(2):
        for kt in range(kts):
            for a, (w, x) in enumerate(((wh, xh), (wh, xl), (wl, xh))):
                mm = pe.matmul(k.ps[:, banks + e, 0:width], w[:, kt, e * P:(e + 1) * P],
                               x[:, k0 + kt, 0:width],
                               start=(start and kt == 0 and a == 0),
                               stop=(stop and kt == kts - 1 and a == 2))
        mm.then_inc(k.sem("mm_done"), 1)


def pe_linear(k, pe, phase, rhs, slots=None, first=0, width=S, natural=False):
    n0, u0 = PH[phase]
    n0, u0 = n0 + first, u0 + first
    slots = slots or dict((p, s) for p, s, _ in PHASES_LIST)[phase]

    def some(count, n, u):
        def body(i):
            for j in range(count[1]):
                pe.wait_ge(*k.on("psum_free", i * 4 + (u + j + 1)))
                pe_slot(k, pe, n, j, i, 4, rhs, width=width, banks=bank_pair(u + j), natural=natural)
        rounds(pe, count[0], body)

    if slots // 4:
        some((slots // 4, 4), n0, u0)
    if slots % 4:
        some((1, slots % 4), n0 + slots // 4 * 4, u0 + slots // 4 * 4)


def pe_ada(k, pe, phase, slots):
    n0, u0 = PH[phase]

    def body(i):
        for j in range(4):
            par = (n0 + j) % 2
            pe.wait_ge(*k.on("psum_free", i * 4 + (u0 + j + 1)))
            pe.wait_ge(*k.on("w_low", i * 4 + (n0 + j + 1)))
            b = bank_pair(u0 + j)
            for e in range(2):
                for kt in range(DT):
                    for a, w in enumerate((k.w_hi[par], k.w_lo[par])):
                        mm = pe.matmul(k.ps[:, b + e, 0:2], w[:, kt, e * P:(e + 1) * P], k.cHL[:, kt, :],
                                       start=(kt == 0 and a == 0), stop=(kt == DT - 1 and a == 1))
                mm.then_inc(k.sem("mm_done"), 1)

    rounds(pe, slots // 4, body)


def pe_all_taken(k, pe, phase):
    pe.wait_ge(*k.on("psum_free", 4 + PH[phase][1]))


def pe_down(k, pe, phase, rhs):
    n0, u0 = PH[phase]
    pe_all_taken(k, pe, phase)

    def body(i):
        for j in range(2):
            pe.wait_ge(*k.on("psum_free", i * 2 + (u0 + j + 3)))
            for c in range(3):
                kts = min(DT, FT - c * DT)
                pe_slot(k, pe, n0, 3 * j + c, i, 6, rhs, k0=c * DT, kts=kts,
                        start=(c == 0), stop=(c == 2), banks=2 * j)

    rounds(pe, 2, body)


def act_high(k, act, par, landed):
    act.wait_ge(k.raw_landed[par], landed)
    act.activation(flat(k.w_hi[par]), flat(k.raw[par]), ACT.Copy).then_inc(k.sem("w_high"), 1)


def act_slot(k, act, n, i, per):
    act.wait_ge(*k.on("mm_done", i * (2 * per) + 2 * (n + 1)))
    if n + 2 < k.n_slots:
        act_high(k, act, n % 2, i * (8 * per) + 16 * ((n + 2) // 2 + 1))


def act_linear(k, act, phase, evac=None, slots=None, first=0):
    n0, u0 = PH[phase]
    n0, u0 = n0 + first, u0 + first
    slots = slots or dict((p, s) for p, s, _ in PHASES_LIST)[phase]

    def body(i, n, u, base, count):
        for j in range(count):
            act_slot(k, act, n + j, i, 4)
            if evac:
                evac(i, base, j, bank_pair(u + j))

    if slots // 4:
        rounds(act, slots // 4, lambda i: body(i, n0, u0, 0, 4))
    if slots % 4:
        r = slots // 4 * 4
        body(0, n0 + r, u0 + r, r, slots % 4)


def act_down(k, act, phase):
    n0, u0 = PH[phase]
    last = n0 + 12 >= k.n_slots

    def body(i):
        for j in range(6):
            act_slot(k, act, n0 + j, i, 6)

    if last:
        for j in range(12):
            act_slot(k, act, n0 + j, 0, 6)
    else:
        rounds(act, 2, body)


def pe_mean(k, pe, name, src, tiles, width, bank, inv, ready):
    for t in range(tiles):
        ready(t)
        pe.matmul(k.ps[:, bank, 0:width], inv[:], src(t), start=(t == 0), stop=(t == tiles - 1)) \
            .then_inc(k.sem(name), 1)


def act_squares(k, act, name, src, tiles, width, wbuf=0):
    for t in range(tiles):
        if t >= 2:
            act.wait_ge(*k.on(name + "_sum", t - 1))
        act.activation(k.work[:, wbuf + t % 2, 0:width], src(t), ACT.Square).then_inc(k.sem(name + "_sq"), 1)


def pe_squares(k, pe, name, tiles, width, bank, inv, wbuf=0):
    pe_mean(k, pe, name + "_sum", lambda t: k.work[:, wbuf + t % 2, 0:width], tiles, width, bank, inv,
            lambda t: pe.wait_ge(*k.on(name + "_sq", t + 1)))


def act_std(k, act, name, tiles, width, bank, eps=None):
    act.wait_ge(*k.on(name + "_sum", tiles))
    act.activation(k.std[:, 0:width], k.ps[:, bank, 0:width], ACT.Sqrt, bias=(eps or k.eps)[:, 0:1]) \
        .then_inc(k.sem(name + "_std"), 1)


def dve_rstd(k, dve, name, width):
    dve.wait_ge(*k.on(name + "_std", 1))
    dve.reciprocal(k.rstd[:, 0:width], k.std[:, 0:width]).then_inc(k.sem(name + "_rstd"), 1)
    dve.wait_ge(*k.on(name + "_rstd", 1))


def dve_scale_split(k, dve, name, src, scale, shift, low, high, tiles, width, func_after=False):
    def one(t):
        if t < tiles:
            if t >= 2:
                dve.wait_ge(*k.on(name + "_lo", t - 1))
            dve.scalar_tensor_tensor(k.work[:, 2 + t % 2, 0:width], src(t), scale(t), k.rstd[:, 0:width],
                                     ALU.mult, ALU.mult).then_inc(k.sem(name + "_t"), 1)
    one(0)
    for t in range(tiles):
        one(t + 1)
        dve.wait_ge(*k.on(name + "_hi", t + 1))
        w = k.work[:, 2 + t % 2, 0:width]
        if shift is None:
            dve.wait_ge(*k.on(name + "_t", t + 1))
            ins = dve.tensor_tensor(low(t), w, high(t).bitcast(F32), ALU.subtract)
        else:
            dve.wait_ge(*k.on(name + "_t", t + 1))
            ins = dve.scalar_tensor_tensor(low(t), w, shift(t), high(t).bitcast(F32), ALU.add, ALU.subtract)
        ins.then_inc(k.sem(name + "_lo"), 1)


def act_scale_split(k, act, name, shift, high, tiles, width, func=None):
    for t in range(tiles):
        act.wait_ge(*k.on(name + "_t", t + 1))
        w = k.work[:, 2 + t % 2, 0:width]
        if func is not None:
            act.activation(w, w, func, bias=shift(t)).then_inc(k.sem(name + "_f"), 1)
            act.wait_ge(*k.on(name + "_f", t + 1))
            act.activation(high(t), w, ACT.Copy).then_inc(k.sem(name + "_hi"), 1)
        elif shift is None:
            act.activation(high(t), w, ACT.Copy).then_inc(k.sem(name + "_hi"), 1)
        else:
            act.activation(high(t), w, ACT.Identity, bias=shift(t)).then_inc(k.sem(name + "_hi"), 1)


def slot_tile(i, base, j, e):
    return i * 8 + (2 * (base + j) + e)


def pick(t, j):
    if isinstance(j, int):
        return t[:, j]
    return t[:, bass.ds(j, 1)].rearrange("p a n -> p (a n)")


def pcol(k, name, j):
    at, _ = CT[name]
    if isinstance(j, int):
        return k.cols[:, at + j:at + j + 1]
    return k.cols[:, bass.ds(j + at, 1)]


def ml_scores_range(i):
    return i * P, S - i * P


SC_OFF = [0, 512, 896, 1152]


def pe_mlstm(k, pe):
    pe_all_taken(k, pe, "pw")
    pe.wait_ge(*k.on("ml_g", 1))
    for i in range(4):
        mm = pe.transpose(k.ps[:, 0, 4 * i:4 * i + 4], k.rows[0:4, 0, i * P:(i + 1) * P],
                          k.col("ident", 0, 4)[0:4, :])
    mm.then_inc(k.sem("ml_gT"), 1)
    pe.wait_ge(*k.on("ml_rows", 1))
    pe.wait_ge(*k.on("sel_landed", 16))
    for h in range(ML_HEADS):
        if h:
            pe.wait_ge(*k.on("ml_std", h))
            pe.wait_ge(*k.on("ml_hc", h))
        sel = k.sel[:, h]
        pe.matmul(k.ps[:, 1], sel, k.rows[0:4, 1], start=True, stop=True)
        pe.matmul(k.ps[:, 2], sel, k.rows[0:4, 2], start=True, stop=True).then_inc(k.sem("ml_bc"), 1)
        for i in range(4):
            t0, n = ml_scores_range(i)
            if 4 * h + i >= 2:
                pe.wait_ge(*k.on("ml_sc", 4 * h + i - 1))
            for c in range(2):
                mm = pe.matmul(k.ps[:, 3 + i % 2, 0:n], k.kT[:, 2 * h + c, t0:t0 + P],
                               k.qT[:, 2 * h + c, t0:S], start=(c == 0), stop=(c == 1))
            mm.then_inc(k.sem("ml_S"), 1)
        for i in range(4):
            t0, n = ml_scores_range(i)
            pe.wait_ge(*k.on("ml_sc", 4 * h + i + 1))
            sc = k.scT[:, SC_OFF[i]:SC_OFF[i] + n]
            for e in range(2):
                pe.matmul(k.ps[:, 5 + e, t0:S], k.v[:, i, h * 256 + e * P:h * 256 + (e + 1) * P], sc,
                          start=(i == 0), stop=(i == 3))
            mm = pe.matmul(k.ps[:, 7, t0:S], k.one[:], sc, start=(i == 0), stop=(i == 3))
        mm.then_inc(k.sem("ml_num"), 1)
        pe.wait_ge(*k.on("ml_h", 2 * (h + 1)))
        for e in range(2):
            mm = pe.matmul(k.ps[:, 1], k.inv_h[:], k.qT[:, 2 * h + e], start=(e == 0), stop=(e == 1))
        mm.then_inc(k.sem("ml_mean"), 1)
        for e in range(2):
            pe.wait_ge(*k.on("ml_sq", 2 * h + e + 1))
            mm = pe.matmul(k.ps[:, 2], k.inv_h[:], k.work[:, 2 + e], start=(e == 0), stop=(e == 1))
        mm.then_inc(k.sem("ml_var"), 1)


def tensor_block1(k, pe):
    pe.wait_ge(*k.on("c_split", 1))
    pe_ada(k, pe, "ada1", 8)
    pe_all_taken(k, pe, "glu")
    pe.wait_ge(*k.on("consts", 1))
    pe_squares(k, pe, "n1", DT, S, 0, k.inv_d)
    pe.wait_ge(*k.on("n1_lo", DT))
    h = (k.h_hi, k.h_lo)
    pe_linear(k, pe, "glu", h)
    pe_linear(k, pe, "qk", h)
    pe_linear(k, pe, "v", h, width=256, natural=True)
    pe_linear(k, pe, "if", h)
    pe_ada(k, pe, "ada2", 16)
    pe_mlstm(k, pe)
    pe.wait_ge(*k.on("conv", 8))
    pe.wait_ge(*k.on("ml_out", 2 * ML_HEADS))
    pe_mean(k, pe, "cln_mean", lambda t: k.aT[:, t, 0:S], DT, S, 0, k.inv_d, lambda t: None)
    pe_squares(k, pe, "cln", DT, S, 1, k.inv_d)
    pe.wait_ge(*k.on("cln_lo", DT))
    pe_linear(k, pe, "pw", (k.cs_hi, k.cs_lo))
    pe_linear(k, pe, "o", h)
    pe_linear(k, pe, "merge", h)
    pe.wait_ge(*k.on("y_lo", DT))
    pe_linear(k, pe, "w_out", (k.cs_hi, k.cs_lo))
    pe_ffn(k, pe, "a")


def pe_ffn(k, pe, name):
    n = "nf" + name
    pe_all_taken(k, pe, "up_" + name)
    pe_squares(k, pe, n, DT, S, 0, k.inv_d)
    pe.wait_ge(*k.on(n + "_lo", DT))
    pe_linear(k, pe, "up_" + name, (k.h_hi, k.h_lo))
    pe.wait_ge(*k.on("hid_lo_" + name, FT))
    pe_down(k, pe, "down_" + name, (k.hid_hi, k.hid_lo))


def act_mlstm_gates(k, act):
    act.wait_ge(*k.on("ml_neg", 1))
    act.activation(k.rows[0:4, 3], k.rows[0:4, 3], ACT.Exp).then_inc(k.sem("ml_exp"), 1)
    act.wait_ge(*k.on("ml_exp", 1))
    act.activation(k.rows[0:4, 3], k.rows[0:4, 3], ACT.Ln, bias=1.0).then_inc(k.sem("ml_ln"), 1)
    act.wait_ge(*k.on("ml_fm", 1))
    act.activation(k.rows[0:4, 2], k.rows[0:4, 2], ACT.Exp).then_inc(k.sem("ml_rows"), 1)


def act_mlstm_heads(k, act):
    for h in range(ML_HEADS):
        act.wait_ge(*k.on("ml_nm", h + 1))
        for i in range(4):
            _, n = ml_scores_range(i)
            if i >= 2:
                act.wait_ge(*k.on("ml_sc", 4 * h + i - 1))
            g = k.gcol[:, 4 * i + h:4 * i + h + 1]
            act.activation(k.work[:, 2 + i % 2, 0:P], k.work[:, 1, i * P:(i + 1) * P], ACT.Exp, bias=g) \
                .then_inc(k.sem("ml_D"), 1)
            if i < 3:
                act.activation(k.work[:, 2 + i % 2, P:n], k.work[:, 0, (i + 1) * P:S], ACT.Exp, bias=g) \
                    .then_inc(k.sem("ml_D"), 1)
        for e in range(2):
            act.wait_ge(*k.on("ml_hc", 2 * h + e + 1))
            act.activation(k.work[:, 2 + e], k.qT[:, 2 * h + e], ACT.Square).then_inc(k.sem("ml_sq"), 1)
        act.wait_ge(*k.on("ml_var", h + 1))
        act.activation(k.std[:], k.ps[:, 2], ACT.Sqrt, bias=k.eps[:, 0:1]).then_inc(k.sem("ml_std"), 1)


def scalar_block1(k, act):
    act.wait_ge(*k.on("cols_landed", 16))
    act_high(k, act, 0, 16)
    act_high(k, act, 1, 16)
    act.activation(k.csilu[:], k.col("c", 0, 8), ACT.Silu).then_inc(k.sem("c_silu"), 1)
    act.wait_ge(*k.on("c_silu", 1))
    act.activation(k.cHL[:, :, 0], k.csilu[:], ACT.Copy).then_inc(k.sem("c_high"), 1)
    act_linear(k, act, "ada1")
    act.wait_ge(*k.on("x_landed", 16))
    act.wait_ge(*k.on("consts", 1))
    act_squares(k, act, "n1", lambda t: k.xT[:, t], DT, S)
    act_std(k, act, "n1", DT, S, 0)
    act_scale_split(k, act, "n1", lambda t: k.mod[:, t:t + 1], lambda t: k.h_hi[:, t], DT, S)

    def glu(i, base, j, bank):
        if j % 2:
            act.wait_ge(*k.on("psum_free", i * 4 + (4 + PH["glu"][1] + j - 1)))
            for e in range(2):
                g = i * 4 + (8 + (j // 2) * 2 + e)
                act.activation(k.work[:, e], k.ps[:, bank + e], ACT.Sigmoid, bias=pcol(k, "b_glu", g)) \
                    .then_inc(k.sem("glu_sig"), 1)

    act_linear(k, act, "glu", glu)

    def qk(i, base, j, bank):
        for e in range(2):
            t = slot_tile(i, base, j, e)
            act.activation(k.qpre[:, e, 3:3 + S], k.ps[:, bank + e], ACT.Identity, bias=pcol(k, "b_qk", t)) \
                .then_inc(k.sem("qk_pre"), 1)
        for e in range(2):
            t = slot_tile(i, base, j, e)
            act.wait_ge(*k.on("qk_conv", i * 8 + (2 * j + e + 1)))
            act.activation(pick(k.qkT, t), k.work[:, e], ACT.Silu).then_inc(k.sem("qk_done"), 1)

    act_linear(k, act, "qk", qk)
    act_linear(k, act, "v")
    act_linear(k, act, "if")
    act_mlstm_gates(k, act)
    act_linear(k, act, "ada2")
    act_mlstm_heads(k, act)
    for t in range(DT):
        act.wait_ge(*k.on("cln_c", t + 1))
        if t >= 2:
            act.wait_ge(*k.on("cln_sum", t - 1))
        act.activation(k.work[:, t % 2], k.aT[:, t, 0:S], ACT.Square).then_inc(k.sem("cln_sq"), 1)
    act_std(k, act, "cln", DT, S, 1)
    act_scale_split(k, act, "cln", lambda t: pcol(k, "ln_b", t), lambda t: k.cs_hi[:, t], DT, S, func=ACT.Silu)
    act_linear(k, act, "pw")

    def gate(name, phase):
        def evac(i, base, j, bank):
            for e in range(2):
                act.wait_ge(*k.on("psum_free", i * 4 + (4 + PH[phase][1] + base + j)))
                act.activation(k.work[:, e], k.ps[:, bank + e], ACT.Sigmoid,
                               bias=pcol(k, name, slot_tile(i, base, j, e))).then_inc(k.sem("sig_" + phase), 1)
        return evac

    act_linear(k, act, "o", gate("b_o", "o"))
    act_linear(k, act, "merge", gate("b_merge", "merge"))
    act_split(k, act, "y", lambda t: k.qT[:, t], lambda t: k.cs_hi[:, t], DT, ("psum_free", 4 + PH["w_out"][1]))
    act_linear(k, act, "w_out")
    act_ffn(k, act, "a", lambda t: k.mod[:, 24 + t:25 + t])


def act_split(k, act, name, src, high, tiles, ready):
    act.wait_ge(*k.on(ready[0], ready[1]))
    for t in range(tiles):
        act.activation(high(t), src(t), ACT.Copy).then_inc(k.sem(name + "_hi"), 1)


def dve_split(k, dve, name, src, high, low, tiles):
    for t in range(tiles):
        dve.wait_ge(*k.on(name + "_hi", t + 1))
        dve.tensor_tensor(low(t), src(t), high(t).bitcast(F32), ALU.subtract).then_inc(k.sem(name + "_lo"), 1)


def act_ffn(k, act, name, shift):
    n = "nf" + name
    u0 = PH["up_" + name][1]
    act.wait_ge(*k.on("psum_free", 4 + u0))
    act_squares(k, act, n, lambda t: k.xT[:, t], DT, S)
    act_std(k, act, n, DT, S, 0)
    act_scale_split(k, act, n, shift, lambda t: k.h_hi[:, t], DT, S)

    def evac(i, base, j, bank):
        if j % 2 == 0:
            for e in range(2):
                if e == 0:
                    act.wait_ge(*k.on("psum_free", i * 4 + (4 + u0 + base + j)))
                act.activation(k.work[:, e], k.ps[:, bank + e], ACT.Silu).then_inc(k.sem("silu_" + name), 1)
        else:
            act.wait_ge(*k.on("psum_free", i * 4 + (4 + u0 + base + j + 1)))
            for e in range(2):
                t = i * 4 + (base + j - 1 + e)
                act.activation(pick(k.hid_hi, t), k.work[:, 2 + e], ACT.Copy).then_inc(k.sem("hid_hi_" + name), 1)

    act_linear(k, act, "up_" + name, evac)
    act_down(k, act, "down_" + name)


def dve_linear(k, dve, phase, evac, slots=None, first=0, chain=None, per=0):
    n0, u0 = PH[phase]
    n0, u0 = n0 + first, u0 + first
    slots = slots or dict((p, s) for p, s, _ in PHASES_LIST)[phase]

    def body(i, base, count):
        for j in range(count):
            dve.wait_ge(*k.on("mm_done", i * 8 + 2 * (n0 + base + j + 1)))
            evac(i, base, j, bank_pair(u0 + base + j))

    if slots // 4:
        if chain:
            chained_rounds(chain, slots // 4, per, lambda i: body(i, 0, 4))
        else:
            rounds(dve, slots // 4, lambda i: body(i, 0, 4))
    if slots % 4:
        body(0, slots // 4 * 4, slots % 4)


def dve_ada(k, dve, phase, col0):
    def evac(i, base, j, bank):
        out = k.mod[:, bass.ds(i * 8 + (col0 + 2 * j), 2)] if not isinstance(i, int) \
            else k.mod[:, col0 + 8 * i + 2 * j:col0 + 8 * i + 2 * j + 2]
        dve.tensor_reduce(out, k.ps[:, bank:bank + 2, 0:2], AX.X, ALU.add).then_inc(k.sem("psum_free"), 1)
    dve_linear(k, dve, phase, evac)


def dve_mlstm_gates(k, dve, ch):
    R = lambda j: k.rows[0:4, j]
    bank = bank_pair(PH["if"][1])
    n = PH["if"][0]
    dve.wait_ge(*k.on("mm_done", 2 * (n + 1)))
    ch.link(dve.tensor_scalar(R(0), k.ps[0:4, bank], k.col("b_i")[0:4, :], None, ALU.add))
    ch.link(dve.tensor_scalar(R(1), k.ps[0:4, bank + 1], k.col("b_f")[0:4, :], None, ALU.add))
    dve.memset(R(4), 0.0).then_inc(k.sem("psum_free"), 1)
    dve.wait_ge(*k.on("psum_free", 4 + PH["if"][1] + 1))
    dve.scalar_tensor_tensor(R(3), R(1), -1.0, R(1), ALU.mult, ALU.min).then_inc(k.sem("ml_neg"), 1)
    dve.wait_ge(*k.on("ml_ln", 1))
    ch.link(dve.scalar_tensor_tensor(R(3), R(1), 0.0, R(3), ALU.min, ALU.subtract))
    ch.link(dve.tensor_tensor_scan(R(1), R(4), R(3), 0.0, ALU.add, ALU.add))
    dve.tensor_tensor(R(0), R(0), R(1), ALU.subtract).then_inc(k.sem("ml_g"), 1)
    dve.wait_ge(*k.on("ml_g", 1))
    ch.link(dve.tensor_tensor_scan(R(3), R(0), R(4), 0.0, ALU.max, ALU.add))
    ch.link(dve.scalar_tensor_tensor(R(2), R(1), -1.0, R(3), ALU.mult, ALU.subtract))
    dve.tensor_scalar(R(1), R(3), -1.0, None, ALU.mult).then_inc(k.sem("ml_fm"), 1)
    dve.wait_ge(*k.on("ml_fm", 1))


def dve_mlstm_heads(k, dve, ch):
    dve.wait_ge(*k.on("ml_gT", 1))
    ch.link(dve.tensor_copy(k.gcol[:], k.ps[:, 0, 0:16]))
    for h in range(ML_HEADS):
        dve.wait_ge(*k.on("ml_bc", h + 1))
        ch.link(dve.tensor_copy(k.work[:, 0], k.ps[:, 1]))
        for i in range(4):
            ins = dve.tensor_tensor(k.work[:, 1, i * P:(i + 1) * P], k.work[:, 0, i * P:(i + 1) * P],
                                    k.col("after", 0, P), ALU.add)
            if i < 3:
                ch.link(ins)
        ins.then_inc(k.sem("ml_nm"), 1)
        nd = 0
        for i in range(4):
            t0, n = ml_scores_range(i)
            nd += 2 if i < 3 else 1
            dve.wait_ge(*k.on("ml_S", 4 * h + i + 1))
            dve.wait_ge(*k.on("ml_D", 7 * h + nd))
            dve.scalar_tensor_tensor(k.scT[:, SC_OFF[i]:SC_OFF[i] + n], k.ps[:, 3 + i % 2, 0:n], 1.0 / 16,
                                     k.work[:, 2 + i % 2, 0:n], ALU.mult, ALU.mult).then_inc(k.sem("ml_sc"), 1)
        ch.link(dve.tensor_copy(k.work[:, 0], k.ps[:, 2]))
        dve.wait_ge(*k.on("ml_num", h + 1))
        ch.link(dve.tensor_tensor(k.work[:, 0], k.ps[:, 7], k.work[:, 0], ALU.max))
        ch.link(dve.scalar_tensor_tensor(k.work[:, 1], k.ps[:, 7], -1.0, k.work[:, 0], ALU.mult, ALU.max))
        ch.link(dve.reciprocal(k.work[:, 1], k.work[:, 1]))
        for e in range(2):
            dve.tensor_tensor(k.qT[:, 2 * h + e], k.ps[:, 5 + e], k.work[:, 1], ALU.mult) \
                .then_inc(k.sem("ml_h"), 1)
        dve.wait_ge(*k.on("ml_mean", h + 1))
        for e in range(2):
            dve.wait_ge(*k.on("ml_h", 2 * h + e + 1))
            dve.tensor_tensor(k.qT[:, 2 * h + e], k.qT[:, 2 * h + e], k.ps[:, 1], ALU.subtract) \
                .then_inc(k.sem("ml_hc"), 1)
        dve.wait_ge(*k.on("ml_std", h + 1))
        ch.link(dve.reciprocal(k.rstd[:], k.std[:]))
        for e in range(2):
            t = 2 * h + e
            dve.scalar_tensor_tensor(k.qT[:, t], k.qT[:, t], pcol(k, "mlstm_g", t), k.rstd[:],
                                     ALU.mult, ALU.mult).then_inc(k.sem("ml_out"), 1)


def vector_block1(k, dve, ch):
    for ap, value in ((k.inv_d, 1.0 / D), (k.inv_h, 1.0 / 256), (k.one, 1.0), (k.eps, EPS)):
        ch.link(dve.memset(ap[:], value))
    ch.link(dve.memset(k.aT[:, :, 0:TAPS - 1], 0.0))
    dve.memset(k.qpre[:, :, 0:QK_TAPS - 1], 0.0).then_inc(k.sem("consts"), 1)
    dve.memset(k.mod[:], 0.0).then_inc(k.sem("psum_free"), 4)
    dve.wait_ge(*k.on("psum_free", 4))
    dve.wait_ge(*k.on("cols_landed", 16))
    dve.wait_ge(*k.on("c_high", 1))
    dve.tensor_tensor(k.cHL[:, :, 1], k.csilu[:], k.cHL[:, :, 0].bitcast(F32), ALU.subtract) \
        .then_inc(k.sem("c_split"), 1)
    dve_ada(k, dve, "ada1", 0)
    dve.wait_ge(*k.on("psum_free", 4 + PH["glu"][1]))
    ch.link(dve.tensor_tensor(k.mod[:, 0:16], k.mod[:, 0:16], k.col("b_ada", 0, 16), ALU.add))
    ch.link(dve.scalar_tensor_tensor(k.A[:], k.mod[:, 8:16], 1.0, k.col("norm_mix_g", 0, 8), ALU.add, ALU.mult))
    dve_rstd(k, dve, "n1", S)
    dve_scale_split(k, dve, "n1", lambda t: k.xT[:, t], lambda t: k.A[:, t:t + 1],
                    lambda t: k.mod[:, t:t + 1], lambda t: k.h_lo[:, t], lambda t: k.h_hi[:, t], DT, S)

    def glu(i, base, j, bank):
        if j % 2:
            for e in range(2):
                t = i * 4 + ((j // 2) * 2 + e)
                dve.wait_ge(*k.on("glu_sig", i * 4 + ((j // 2) * 2 + e + 1)))
                u = PH["glu"][1] + j - 1
                if isinstance(t, int):
                    out = k.aT[:, t, TAPS - 1:TAPS - 1 + S]
                else:
                    out = k.aT[:, bass.ds(t, 1), TAPS - 1:TAPS - 1 + S].rearrange("p a n -> p (a n)")
                ins = dve.scalar_tensor_tensor(out, k.ps[:, bank_pair(u) + e], pcol(k, "b_glu", t),
                                               k.work[:, e], ALU.add, ALU.mult)
                if e:
                    ins.then_inc(k.sem("psum_free"), 2)

    dve_linear(k, dve, "glu", glu)
    dve.wait_ge(*k.on("psum_free", 4 + PH["qk"][1]))

    def taps(out, src, w, bias, count, last=None, ready=None):
        ch.link(dve.tensor_scalar(out, src(0), w(0), bias, ALU.mult, ALU.add))
        for t in range(1, count - 1):
            ch.link(dve.scalar_tensor_tensor(out, src(t), w(t), out, ALU.mult, ALU.add))
        return dve.scalar_tensor_tensor(last, src(count - 1), w(count - 1), out, ALU.mult, ALU.add)

    def qk(i, base, j, bank):
        for e in range(2):
            t = slot_tile(i, base, j, e)
            dve.wait_ge(*k.on("qk_pre", i * 8 + (2 * j + e + 1)))
            w = lambda m, t=t: pcol(k, "qk_w", t * QK_TAPS + m)
            ins = taps(k.work[:, e], lambda m: k.qpre[:, e, m:m + S], w, pcol(k, "qk_b", t), QK_TAPS,
                       last=k.work[:, e])
            ins.then_inc(k.sem("qk_conv"), 1)
        t = i * 4 + (base + j)
        def src(m, t=t):
            if isinstance(t, int):
                return k.aT[:, t, m:m + S]
            return k.aT[:, bass.ds(t, 1), m:m + S].rearrange("p a n -> p (a n)")
        ins = taps(k.work[:, 2], src, lambda m: pcol(k, "conv_w", t * TAPS + m), pcol(k, "conv_b", t), TAPS,
                   last=src(0))
        ins.then_inc(k.sem("conv"), 1)
        dve.memset(k.zero[:], 0.0).then_inc(k.sem("psum_free"), 1)

    dve_linear(k, dve, "qk", qk, chain=ch, per=4 * (2 * 3 + TAPS - 1))

    dve.wait_ge(*k.on("row_bv_landed", 16))

    def v(i, base, j, bank):
        for e in range(2):
            c = (base + j) * 256
            ins = dve.tensor_tensor(k.v[:, 2 * e:2 * e + 2, c:c + 256],
                                    k.ps[:, bank + e].rearrange("p (t c) -> p t c", t=2),
                                    k.row_bv2[:, :, c:c + 256], ALU.add)
        ins.then_inc(k.sem("psum_free"), 1)

    dve_linear(k, dve, "v", v)
    dve_mlstm_gates(k, dve, ch)
    dve_ada(k, dve, "ada2", 16)
    dve.wait_ge(*k.on("psum_free", 4 + PH["pw"][1]))
    ch.link(dve.tensor_tensor(k.mod[:, 16:48], k.mod[:, 16:48], k.col("b_ada", 16, 32), ALU.add))
    dve_mlstm_heads(k, dve, ch)
    dve.wait_ge(*k.on("cln_mean", DT))
    for t in range(DT):
        dve.wait_ge(*k.on("conv", DT))
        dve.tensor_tensor(k.aT[:, t, 0:S], k.aT[:, t, 0:S], k.ps[:, 0], ALU.subtract).then_inc(k.sem("cln_c"), 1)
    dve_rstd(k, dve, "cln", S)
    dve_scale_split(k, dve, "cln", lambda t: k.aT[:, t, 0:S], lambda t: pcol(k, "ln_g", t), None,
                    lambda t: k.cs_lo[:, t], lambda t: k.cs_hi[:, t], DT, S)

    def pw(i, base, j, bank):
        for e in range(2):
            t = 2 * (base + j) + e
            ins = dve.tensor_scalar(k.aT[:, t, 0:S], k.ps[:, bank + e], pcol(k, "b_pw", t), None, ALU.add)
            if e == 0:
                ch.link(ins)
        ins.then_inc(k.sem("psum_free"), 1)

    dve_linear(k, dve, "pw", pw)
    dve.wait_ge(*k.on("psum_free", 4 + PH["o"][1]))
    dve.wait_ge(*k.on("ml_out", 2 * ML_HEADS))

    def o(i, base, j, bank):
        for e in range(2):
            t = 2 * (base + j) + e
            dve.wait_ge(*k.on("sig_o", t + 1))
            ins = dve.tensor_tensor(k.qT[:, t], k.qT[:, t], k.work[:, e], ALU.mult)
            if e == 0:
                ch.link(ins)
        ins.then_inc(k.sem("psum_free"), 1)

    dve_linear(k, dve, "o", o)
    dve.wait_ge(*k.on("psum_free", 4 + PH["merge"][1]))

    def merge(i, base, j, bank):
        for e in range(2):
            t = 2 * j + e
            dve.wait_ge(*k.on("sig_merge", 2 * (base + j) + e + 1))
            if base == 0:
                ins = dve.tensor_tensor(k.aT[:, t, 0:S], k.aT[:, t, 0:S], k.work[:, e], ALU.mult)
            else:
                ch.link(dve.tensor_tensor(k.qT[:, t], k.qT[:, t], k.work[:, e], ALU.mult))
                ins = dve.tensor_tensor(k.qT[:, t], k.qT[:, t], k.aT[:, t, 0:S], ALU.add)
            if e == 0:
                ch.link(ins)
        ins.then_inc(k.sem("psum_free"), 1)
        dve.wait_ge(*k.on("psum_free", 4 + PH["merge"][1] + base + j + 1))

    n0, u0 = PH["merge"]
    for s in range(8):
        dve.wait_ge(*k.on("mm_done", 2 * (n0 + s + 1)))
        merge(0, s // 4 * 4, s % 4, bank_pair(u0 + s))
    dve_split(k, dve, "y", lambda t: k.qT[:, t], lambda t: k.cs_hi[:, t], lambda t: k.cs_lo[:, t], DT)
    dve_residual(k, dve, ch, "w_out", lambda t: k.mod[:, 16 + t:17 + t])
    ch.link(dve.scalar_tensor_tensor(k.A[:], k.mod[:, 32:40], 1.0, k.col("ffn_g", 0, 8), ALU.add, ALU.mult))
    dve_ffn(k, dve, ch, "a", lambda t: k.A[:, t:t + 1], lambda t: k.mod[:, 24 + t:25 + t],
            lambda t: k.mod[:, 40 + t:41 + t])


def dve_residual(k, dve, ch, phase, gain):
    def evac(i, base, j, bank):
        for e in range(2):
            t = 2 * (base + j) + e
            if gain is None:
                ins = dve.tensor_tensor(k.xT[:, t], k.ps[:, bank + e], k.xT[:, t], ALU.add)
            else:
                ins = dve.scalar_tensor_tensor(k.xT[:, t], k.ps[:, bank + e], gain(t), k.xT[:, t],
                                               ALU.mult, ALU.add)
            if e == 0:
                ch.link(ins)
        ins.then_inc(k.sem("psum_free"), 1)
    dve_linear(k, dve, phase, evac)
    dve.wait_ge(*k.on("psum_free", 4 + PH[phase][1] + 4))


def dve_ffn(k, dve, ch, name, scale, shift, gain):
    n = "nf" + name
    n0, u0 = PH["up_" + name]
    dve_rstd(k, dve, n, S)
    dve_scale_split(k, dve, n, lambda t: k.xT[:, t], scale, shift, lambda t: k.h_lo[:, t],
                    lambda t: k.h_hi[:, t], DT, S)

    def evac(i, base, j, bank):
        if j % 2 == 0:
            return
        for e in range(2):
            dve.wait_ge(*k.on("silu_" + name, i * 4 + (base + j - 1 + e + 1)))
            ins = dve.tensor_tensor(k.work[:, 2 + e], k.work[:, e], k.ps[:, bank + e], ALU.mult)
            if e == 0:
                ch.link(ins)
        ins.then_inc(k.sem("psum_free"), 2)
        dve.wait_ge(*k.on("psum_free", i * 4 + (4 + u0 + base + j + 1)))
        for e in range(2):
            t = i * 4 + (base + j - 1 + e)
            dve.wait_ge(*k.on("hid_hi_" + name, i * 4 + (base + j - 1 + e + 1)))
            dve.tensor_tensor(pick(k.hid_lo, t), k.work[:, 2 + e], pick(k.hid_hi, t).bitcast(F32),
                              ALU.subtract).then_inc(k.sem("hid_lo_" + name), 1)
        dve.wait_ge(*k.on("hid_lo_" + name, i * 4 + (base + j + 1)))

    dve_linear(k, dve, "up_" + name, evac, chain=ch, per=2)
    n0, u0 = PH["down_" + name]
    for u in range(4):
        dve.wait_ge(*k.on("mm_done", 2 * (n0 + 3 * (u + 1))))
        for e in range(2):
            t = 2 * u + e
            src = k.ps[:, 2 * (u % 2) + e]
            if gain is None:
                ins = dve.tensor_tensor(k.xT[:, t], src, k.xT[:, t], ALU.add)
            else:
                ins = dve.scalar_tensor_tensor(k.xT[:, t], src, gain(t), k.xT[:, t], ALU.mult, ALU.add)
            if e == 0:
                ch.link(ins)
        ins.then_inc(k.sem("psum_free"), 1)
    dve.wait_ge(*k.on("psum_free", 4 + u0 + 4))


def dve_norm_in_place(k, dve, name, scale, dst=None):
    dve_rstd(k, dve, name, S)
    dst = dst or (lambda t: k.xT[:, t])
    for t in range(DT):
        ins = dve.scalar_tensor_tensor(dst(t), k.xT[:, t], scale(t), k.rstd[:], ALU.mult, ALU.mult)
        ins.then_inc(k.sem(name + "_x"), 1)
    dve.wait_ge(*k.on(name + "_x", DT))


def act_memory(k, act, i, before=None):
    s = str(i)
    act.wait_ge(*k.on("psum_free", 4 + PH["memkv" + s][1]))
    act.dma_start(k.memT[:], k.mem_dram).then_inc(k.sem("mem_landed"), 16)
    act.wait_ge(*k.on("mem_landed", 16 * (i + 1)))
    act_squares(k, act, "mem" + s, lambda t: k.memT[:, t], DT, N_MEM)
    if before:
        act.wait_ge(*k.on(before, DT))
    act_std(k, act, "mem" + s, DT, N_MEM, 0)
    act_scale_split(k, act, "mem" + s, None, lambda t: k.m_hi[:, t], DT, N_MEM)
    act_linear(k, act, "memkv" + s)


def pe_memory(k, pe, i):
    s = str(i)
    pe_all_taken(k, pe, "memkv" + s)
    pe_squares(k, pe, "mem" + s, DT, N_MEM, 0, k.inv_d)
    pe.wait_ge(*k.on("mem" + s + "_lo", DT))
    n0, u0 = PH["memkv" + s]
    m = (k.m_hi, k.m_lo)
    pe.wait_ge(*k.on("psum_free", u0 + 1))
    pe_slot(k, pe, n0, 0, 0, 4, m, width=N_MEM, banks=bank_pair(u0))
    pe.wait_ge(*k.on("psum_free", u0 + 2))
    par = (n0 + 1) % 2
    pe.wait_ge(*k.on("w_low", n0 + 2))
    for e in range(2):
        for kt in range(DT):
            for a, (x, w) in enumerate(((k.m_hi, k.w_hi[par]), (k.m_hi, k.w_lo[par]), (k.m_lo, k.w_hi[par]))):
                mm = pe.matmul(k.ps[:, bank_pair(u0 + 1) + e, 0:256], x[:, kt, e * P:(e + 1) * P],
                               w[:, kt, :], start=(kt == 0 and a == 0), stop=(kt == DT - 1 and a == 2))
        mm.then_inc(k.sem("mm_done"), 1)


def dve_memory(k, dve, i):
    s = str(i)
    dve_rstd(k, dve, "mem" + s, N_MEM)
    dve_scale_split(k, dve, "mem" + s, lambda t: k.memT[:, t], lambda t: pcol(k, "norm_mem", 8 * i + t), None,
                    lambda t: k.m_lo[:, t], lambda t: k.m_hi[:, t], DT, N_MEM)
    n0, u0 = PH["memkv" + s]
    for j, dst in enumerate((k.mkT, k.mv)):
        dve.wait_ge(*k.on("mm_done", 2 * (n0 + j + 1)))
        b = bank_pair(u0 + j)
        dve.tensor_copy(dst[:], k.ps[:, b:b + 2, 0:N_MEM]).then_inc(k.sem("psum_free"), 1)


def alibi_slopes():
    eight = [2.0 ** -(i + 1) for i in range(8)]
    more = [2.0 ** (-0.5 * (i + 1)) for i in range(16)][0::2][:HEADS - 8]
    return [float(np.float32(v)) for v in eight + more]


def attention_tiles(which):
    tiles, groups = [], []
    for i in range(4):
        for kind in which:
            n = 4 if kind == "mem" else HEADS
            groups.append((kind, i, len(tiles) + n))
            tiles += [(kind, i, h, len(groups) - 1) for h in range(n)]
    return tiles, groups


def attention_keys(k, kind, i, h):
    half = slice((h % 2) * DH, (h % 2) * DH + DH)
    if kind == "mem":
        q = k.mq[half, h // 2, i * P:(i + 1) * P]
        return q, k.mkT[half, h // 2, :], N_MEM, [(P, k.mv[:, j, h * DH:(h + 1) * DH]) for j in range(2)]
    g = h // 3
    q = k.nq[half, h // 2, i * P:(i + 1) * P]
    if kind == "cmp":
        return q, k.kcb[half, g * N_CMP:(g + 1) * N_CMP], N_CMP, [(N_CMP, k.vcb[:, g, :])]
    keys, values = (k.kds, k.vs) if kind == "sel" else (k.kdw, k.vw)
    return q, keys[half, g, 0:(i + 1) * P], (i + 1) * P, \
        [(P, values[:, j, g * DH:(g + 1) * DH]) for j in range(i + 1)]


def attention_out(kind, group, h):
    return 4 + 2 * (group % 2) + h // 6, h % 6 * DH


def pe_attention(k, pe, which, s):
    tiles, groups = attention_tiles(which)
    n = len(tiles)
    for step in range(n + 2):
        if step < n:
            kind, i, h, g = tiles[step]
            q, keys, width, _ = attention_keys(k, kind, i, h)
            if step >= 2:
                pe.wait_ge(*k.on("at_neg" + s, step - 1))
            pe.matmul(k.ps[:, step % 2, 0:width], q, keys, start=True, stop=True) \
                .then_inc(k.sem("at_scores" + s), 1)
        if 0 <= step - 1 < n:
            t = step - 1
            kind, i, h, g = tiles[t]
            _, _, width, _ = attention_keys(k, kind, i, h)
            pe.wait_ge(*k.on("at_exp" + s, t + 1))
            if kind == "cmp":
                pe.wait_ge(*k.on("at_seen" + s, sum(x[0] == "cmp" for x in tiles[:t + 1])))
            if t >= 2:
                pe.wait_ge(*k.on("at_pT" + s, t - 1))
            for j in range(-(-width // P)):
                w = min(P, width - j * P)
                mm = pe.transpose(k.ps[0:w, 2 + t % 2, j * P:(j + 1) * P], k.ap[:, t % 2, j * P:j * P + w],
                                  k.col("ident", 0, P))
            mm.then_inc(k.sem("at_turned" + s), 1)
        if step - 2 >= 0:
            t = step - 2
            kind, i, h, g = tiles[t]
            _, _, width, values = attention_keys(k, kind, i, h)
            bank, c = attention_out(kind, g, h)
            if h == 0 and g >= 2:
                pe.wait_ge(*k.on("at_group" + s, g - 1))
            pe.wait_ge(*k.on("at_pT" + s, t + 1))
            for j, (rows, v) in enumerate(values):
                mm = pe.matmul(k.ps[:, bank, c:c + DH], k.apT[0:rows, t % 2, j * P:(j + 1) * P], v,
                               start=(j == 0), stop=(j == len(values) - 1))
            mm.then_inc(k.sem("at_out" + s), 1)


def act_attention(k, act, which, s):
    tiles, groups = attention_tiles(which)
    for t, (kind, i, h, g) in enumerate(tiles):
        _, _, width, _ = attention_keys(k, kind, i, h)
        act.wait_ge(*k.on("at_neg" + s, t + 1))
        if t >= 2:
            act.wait_ge(*k.on("at_turned" + s, t - 1))
        if h == 0 and g >= 2:
            act.wait_ge(*k.on("at_group" + s, g - 1))
        act.activation(k.ap[:, t % 2, 0:width], k.aneg[:, t % 2, 0:width], ACT.Exp, scale=-1.0,
                       bias=k.amax[:, t % 2:t % 2 + 1], accum_out=k.asum[:, g % 2, h:h + 1]) \
            .then_inc(k.sem("at_exp" + s), 1)


def dve_attention(k, dve, ch, which, s):
    tiles, groups = attention_tiles(which)
    n = len(tiles)
    for step in range(n + 1):
        if step < n:
            kind, i, h, g = tiles[step]
            _, _, width, _ = attention_keys(k, kind, i, h)
            if kind == "mem":
                table = k.azero[:, 0:width]
            elif kind == "cmp":
                table = k.table_c[:, h, i * N_CMP:(i + 1) * N_CMP]
            else:
                table = k.table[:, h, S - P - i * P:S]
            dve.wait_ge(*k.on("at_scores" + s, step + 1))
            if step >= 2:
                dve.wait_ge(*k.on("at_exp" + s, step - 1))
            dve.tensor_tensor_reduce(out=k.aneg[:, step % 2, 0:width], in0=k.ps[:, step % 2, 0:width],
                                     in1=table, scale=-1.0, scalar=3.0e38, op0=ALU.add, op1=ALU.min,
                                     accum_out=k.amax[:, step % 2:step % 2 + 1]) \
                .then_inc(k.sem("at_neg" + s), 1)
        if step >= 1:
            t = step - 1
            kind, i, h, g = tiles[t]
            _, _, width, _ = attention_keys(k, kind, i, h)
            if kind == "cmp":
                dve.wait_ge(*k.on("at_exp" + s, t + 1))
                p = k.ap[:, t % 2, 0:width]
                dve.tensor_tensor(p, p, k.col("seen_c", i * N_CMP, N_CMP), ALU.mult) \
                    .then_inc(k.sem("at_seen" + s), 1)
            rows = min(width, P)
            cols = max(width, P)
            dve.wait_ge(*k.on("at_turned" + s, t + 1))
            if t >= 2:
                dve.wait_ge(*k.on("at_out" + s, t - 1))
            dve.tensor_copy(k.apT[0:rows, t % 2, 0:cols], k.ps[0:rows, 2 + t % 2, 0:cols]) \
                .then_inc(k.sem("at_pT" + s), 1)
            for g, (kind, i, end) in enumerate(groups):
                if t == end or t + 1 == end == n:
                    dve_combine(k, dve, ch, s, kind, i, g, end)


def dve_combine(k, dve, ch, s, kind, i, g, end):
    heads = 4 if kind == "mem" else HEADS
    w = k.aw[:, 0:heads]
    dve.wait_ge(*k.on("at_out" + s, end))
    dve.wait_ge(*k.on("at_exp" + s, end))
    ch.link(dve.reciprocal(w, k.asum[:, g % 2, 0:heads]))
    if kind != "mem":
        b = ("cmp", "sel", "win").index(kind)
        ch.link(dve.tensor_tensor(w, w, k.gates[:, i, b * HEADS:(b + 1) * HEADS], ALU.mult))
    for half in range(1 if kind == "mem" else 2):
        n = 4 if kind == "mem" else 6
        src = k.ps[:, 4 + 2 * (g % 2) + half, 0:n * DH].rearrange("p (h d) -> p h d", d=DH)
        wb = w[:, half * 6:half * 6 + n].unsqueeze(2).broadcast_to([P, n, DH])
        at = (768 if kind == "mem" else half * 384) - k.cat_from
        dst = k.cat[:, i, at:at + n * DH]
        if kind in ("mem", "cmp"):
            ch.link(dve.tensor_tensor(dst.rearrange("p (h d) -> p h d", d=DH), src, wb, ALU.mult))
        else:
            tmp = k.work[:, 0, 0:n * DH]
            ch.link(dve.tensor_tensor(tmp.rearrange("p (h d) -> p h d", d=DH), src, wb, ALU.mult))
            ch.link(dve.tensor_tensor(dst, dst, tmp, ALU.add))
    dve.memset(k.zero[:], 0.0).then_inc(k.sem("at_group" + s), 1)


def scalar_layer0(k, act):
    act_norm_stats(k, act, "fin1")
    act_memory(k, act, 0, "fin1_x")
    act_norm_stats(k, act, "l0", after=("fin1_x", DT))
    act_scale_split(k, act, "l0", None, lambda t: k.h_hi[:, t], DT, S)
    act.dma_start(k.pos[:], k.pos_dram).then_inc(k.sem("pos_landed"), 16)
    act.dma_start(k.w2[:], k.w2_dram).then_inc(k.sem("w2_landed"), 16)
    act.dma_start(k.w1[:], k.w1_dram[0]).then_inc(k.sem("w1_landed"), 16)
    act_linear(k, act, "nsa", slots=6)
    act.wait_ge(*k.on("ks_ready", 1))
    dup_keys(k, act, k.kT1, k.kds)
    act_linear(k, act, "nsa", first=6, slots=5)
    act.wait_ge(*k.on("kw_ready", 1))
    dup_keys(k, act, k.kT2, k.kdw)
    for v in range(2):
        act.wait_ge(*k.on("cmp_hidden", v + 1))
        if v == 0:
            act.dma_start(k.w1[:], k.w1_dram[1]).then_inc(k.sem("w1_landed"), 16)
        act.activation(k.hidc[:, v].rearrange("p (half n) -> p half n", half=2), k.ps[:, 2 * v:2 * v + 2, 0:62],
                       ACT.Gelu_apprx_tanh) \
            .then_inc(k.sem("cmp_gelu"), 1)
    act.wait_ge(*k.on("gates_sum", 4))
    act.activation(k.gates[:], k.gates[:], ACT.Sigmoid).then_inc(k.sem("gates"), 1)
    act.wait_ge(*k.on("cmp_out", 2))
    for h, slope in enumerate(alibi_slopes()):
        act.activation(k.table[:, h], k.col("dist", 0, S), ACT.Copy, scale=-slope).then_inc(k.sem("tables"), 1)
        act.activation(k.table_c[:, h], k.col("dist_c", 0, 4 * N_CMP), ACT.Copy, scale=-slope) \
            .then_inc(k.sem("tables"), 1)
    act_attention(k, act, ("cmp", "sel", "win", "mem"), "0")
    act_cat_split(k, act, "0", range(DT))
    act_linear(k, act, "wo0")
    act_ffn(k, act, "b", None)


def act_norm_stats(k, act, name, after=None):
    if after:
        act.wait_ge(*k.on(after[0], after[1]))
    act_squares(k, act, name, lambda t: k.xT[:, t], DT, S)
    act_std(k, act, name, DT, S, 0)


def dup_keys(k, act, src, dst):
    for odd in range(2):
        rows = slice(odd * DH, odd * DH + DH)
        for half in range(2):
            act.dma_start(dst[half * DH:half * DH + DH, odd::2], src[rows]).then_inc(k.sem("keys_twice"), 16)


def act_cat_split(k, act, s, tiles):
    for n, c in enumerate(tiles):
        act.wait_ge(*k.on("cat_turned" + s, n + 1))
        act.activation(k.xs_hi[:, c], k.ps[:, n % 2], ACT.Copy).then_inc(k.sem("cat_hi" + s), 1)


def pe_cat_turn(k, pe, s, tiles):
    for n, c in enumerate(tiles):
        if n >= 2:
            pe.wait_ge(*k.on("cat_lo" + s, n - 1))
        for i in range(4):
            mm = pe.transpose(k.ps[:, n % 2, i * P:(i + 1) * P], k.cat[:, i, c * P - k.cat_from:(c + 1) * P - k.cat_from],
                              k.col("ident", 0, P))
        mm.then_inc(k.sem("cat_turned" + s), 1)


def dve_cat_split(k, dve, s, tiles):
    for n, c in enumerate(tiles):
        dve.wait_ge(*k.on("cat_hi" + s, n + 1))
        dve.tensor_tensor(k.xs_lo[:, c], k.ps[:, n % 2], k.xs_hi[:, c].bitcast(F32), ALU.subtract) \
            .then_inc(k.sem("cat_lo" + s), 1)


def tensor_layer0(k, pe):
    pe_all_taken(k, pe, "memkv0")
    pe_squares(k, pe, "fin1", DT, S, 0, k.inv_d)
    pe.wait_ge(*k.on("fin1_std", 1))
    pe_memory(k, pe, 0)
    pe_all_taken(k, pe, "nsa")
    pe_squares(k, pe, "l0", DT, S, 0, k.inv_d)
    pe.wait_ge(*k.on("l0_lo", DT))
    h = (k.h_hi, k.h_lo)
    pe_linear(k, pe, "nsa", h, slots=6)
    pe_linear(k, pe, "nsa", h, first=6, slots=1, width=256, natural=True)
    pe_linear(k, pe, "nsa", h, first=7, slots=1)
    pe_linear(k, pe, "nsa", h, first=8, slots=1, width=256, natural=True)
    pe_linear(k, pe, "nsa", h, first=9, slots=1, width=36, natural=True)
    pe_linear(k, pe, "nsa", h, first=10, slots=1)
    pe_all_taken(k, pe, "wo0")
    for v in range(2):
        pe.wait_ge(*k.on("w1_landed", 16 * (v + 1)))
        pe.wait_ge(*k.on("blocks", v + 1))
        for half in range(2):
            rows = slice(half * DH, half * DH + DH)
            for l in range(32):
                mm = pe.matmul(k.ps[:, 2 * v + half, 0:62], k.w1[rows, l, :], k.blocks[rows, :, :, l],
                               start=(l == 0), stop=(l == 31))
        mm.then_inc(k.sem("cmp_hidden"), 1)
    pe.wait_ge(*k.on("w2_landed", 16))
    pe.wait_ge(*k.on("cmp_gelu", 1))
    pe.matmul(k.ps[:, 4, 0:4 * N_CMP], k.w2[:, 0:P], k.hidc[:, 0], start=True, stop=True) \
        .then_inc(k.sem("cmp_k"), 1)
    pe.wait_ge(*k.on("cmp_gelu", 2))
    for g in range(GROUPS):
        c = (g % 2) * 62 + (g // 2) * N_CMP
        mm = pe.matmul(k.ps[0:N_CMP, 5, g * DH:(g + 1) * DH], k.hidc[:, 1, c:c + N_CMP], k.w2[:, P:P + DH],
                       start=True, stop=True)
    mm.then_inc(k.sem("cmp_v"), 1)
    pe.wait_ge(*k.on("cmp_out", 2))
    pe.wait_ge(*k.on("keys_twice", 16 * 8))
    pe_attention(k, pe, ("cmp", "sel", "win", "mem"), "0")
    pe.wait_ge(*k.on("at_group0", 16))
    pe_cat_turn(k, pe, "0", range(DT))
    pe.wait_ge(*k.on("cat_lo0", DT))
    pe_linear(k, pe, "wo0", (k.xs_hi, k.xs_lo))
    pe_ffn(k, pe, "b")


def vector_layer0(k, dve, ch):
    dve_norm_in_place(k, dve, "fin1", lambda t: pcol(k, "final_g", t))
    dve_memory(k, dve, 0)
    dve_rstd(k, dve, "l0", S)
    dve_scale_split(k, dve, "l0", lambda t: k.xT[:, t], lambda t: pcol(k, "norm1", t), None,
                    lambda t: k.h_lo[:, t], lambda t: k.h_hi[:, t], DT, S)
    n0, u0 = PH["nsa"]

    def take(j, sem=None):
        dve.wait_ge(*k.on("mm_done", 2 * (n0 + j + 1)))
        return bank_pair(u0 + j)

    for j in range(3):
        b = take(j)
        dve.tensor_scalar(k.nq[:, 2 * j:2 * j + 2], k.ps[:, b:b + 2], 0.125, None, ALU.mult) \
            .then_inc(k.sem("psum_free"), 1)
    for j, dst in ((3, k.kcT), (4, k.vcT), (5, k.kT1)):
        b = take(j)
        dve.tensor_copy(dst[:], k.ps[:, b:b + 2]).then_inc(k.sem("psum_free"), 1)
    dve.wait_ge(*k.on("psum_free", 4 + u0 + 6))
    dve.memset(k.zero[:], 0.0).then_inc(k.sem("ks_ready"), 1)
    dve.wait_ge(*k.on("pos_landed", 16))
    dve_blocks(k, dve, 0, k.kcT)

    def natural(j, dst):
        b = take(j)
        for e in range(2):
            ins = dve.tensor_copy(dst[:, 2 * e:2 * e + 2], k.ps[:, b + e].rearrange("p (t c) -> p t c", t=2))
        ins.then_inc(k.sem("psum_free"), 1)

    natural(6, k.vs)
    b = take(7)
    dve.wait_ge(*k.on("keys_twice", 16 * 4))
    dve.tensor_copy(k.kT2[:], k.ps[:, b:b + 2]).then_inc(k.sem("psum_free"), 1)
    dve.wait_ge(*k.on("psum_free", 4 + u0 + 8))
    dve.memset(k.zero[:], 0.0).then_inc(k.sem("kw_ready"), 1)
    natural(8, k.vw)
    b = take(9)
    for t in range(4):
        dve.tensor_tensor(k.gates[:, t], k.ps[:, b + t // 2, (t % 2) * 36:(t % 2) * 36 + 36],
                          k.col("row_gate_b", 0, 36), ALU.add).then_inc(k.sem("gates_sum"), 1)
    dve.wait_ge(*k.on("gates_sum", 4))
    dve.memset(k.zero[:], 0.0).then_inc(k.sem("psum_free"), 1)
    b = take(10)
    dve.tensor_scalar(k.mq[:], k.ps[:, b:b + 2], 0.125, None, ALU.mult).then_inc(k.sem("psum_free"), 1)
    dve.wait_ge(*k.on("cmp_hidden", 1))
    dve_blocks(k, dve, 1, k.vcT)
    dve.wait_ge(*k.on("cmp_k", 1))
    for half in range(2):
        ins = dve.tensor_copy(
            k.kcb[:].rearrange("p (pair half n) -> p half pair n", half=2, n=N_CMP)[:, half],
            k.ps[:, 4, half * 62:(half + 1) * 62].rearrange("p (pair n) -> p pair n", n=N_CMP))
    ins.then_inc(k.sem("cmp_out"), 1)
    dve.wait_ge(*k.on("cmp_v", 1))
    dve.tensor_copy(flat(k.vcb[:]), k.ps[0:N_CMP, 5, 0:4 * DH]).then_inc(k.sem("cmp_out"), 1)
    dve.wait_ge(*k.on("cmp_out", 2))
    ch.link(dve.memset(k.azero[:], 0.0))
    dve.wait_ge(*k.on("tables", 2 * HEADS))
    dve.wait_ge(*k.on("gates", 1))
    dve_attention(k, dve, ch, ("cmp", "sel", "win", "mem"), "0")
    dve_cat_split(k, dve, "0", range(DT))
    dve_residual(k, dve, ch, "wo0", None)
    dve_ffn(k, dve, ch, "b", lambda t: pcol(k, "norm2", t), None, None)


def dve_blocks(k, dve, v, src):
    for pair in range(2):
        for a in range(2):
            t = src[:, pair].rearrange("p (m b) -> p m b", b=16)[:, a:a + N_CMP]
            pos = k.pos[:, v, a * 16:(a + 1) * 16].unsqueeze(1).broadcast_to([P, N_CMP, 16])
            ins = dve.tensor_tensor(k.blocks[:, pair, :, a * 16:(a + 1) * 16], t, pos, ALU.add)
    ins.then_inc(k.sem("blocks"), 1)


PAIRS = HEADS // 2
SETS = 3
CH = S // CHUNK
DECAY = float(np.float32(np.exp(-0.5)))
HALVES = (slice(0, DH), slice(DH, P))


def rw_orders():
    pe, act, dve = [], [], []
    for t in range(21):
        act.append(("z", t))
        dve.append(("shift", t))
    act += ["tanh", "sig_g"]
    dve.append("omka")
    for s in range(SETS):
        for p in range(2):
            pe += [(n, s, p) for n in ("U", "A", "TV", "SS", "BON", "TB", "TK", "AT", "AA", "BT", "CP", "CV")]
            act += [(n, s, p) for n in ("sgw", "a", "kk2", "W", "Wi", "Wp", "std", "natB", "natK")]
            dve += [(n, s, p) for n in ("kk0", "L", "kp", "rk", "natV", "bv", "rt", "at", "hats", "DT", "D", "O",
                                        "BT", "CP", "CV")]
        for stage in (("D2", "D2T"), ("D4", "D4T", "X1"), ("D8", "X2"), ("X3",), ("ZT", "Z", "X"), ("Z2",),
                      ("U2",), ("TT",)):
            for p in range(2):
                pe += [(n, s, p) for n in stage]
                act += [(n, s, p) for n in stage if n in ("D2T", "D4T", "Z", "X", "Z2")]
                if stage[0] == "D2":
                    dve.append(("XT", s, p))
                if stage[0] == "Z2":
                    dve.append(("IZ", s, p))
                dve += [(n, s, p) for n in stage if n not in ("D2T", "D4T", "Z", "X", "Z2")]
        dve.append(("M0", s))
        for c in range(CH):
            pe += [("G", s, c), ("P", s, c), ("M", s, c), ("Y", s, c)]
            dve += [("G", s, c), ("P", s, c), ("M", s, c)]
        for p in range(2):
            dve.append(("y", s, p))
            pe.append(("mean", s, p))
            dve.append(("yc", s, p))
            act.append(("ysq", s, p))
            pe.append(("var", s, p))
            act.append(("ystd", s, p))
            pe.append(("g", s, p))
            dve.append(("out", s, p))
    return {"pe": pe, "act": act, "dve": dve}


class Steps:

    ORDERS = rw_orders()
    NUMBER = {e: {name: n + 1 for n, name in enumerate(order)} for e, order in ORDERS.items()}

    def __init__(self, k, engine, eng):
        self.k, self.engine, self.eng, self.n = k, engine, eng, 0
        self.sem = k.sem("rw_" + engine)

    def done(self, ins, name):
        assert self.ORDERS[self.engine][self.n] == name, (self.engine, self.n, name)
        self.n += 1
        ins.then_inc(self.sem, 1)

    def after(self, engine, name):
        self.eng.wait_ge(self.k.sem("rw_" + engine), self.NUMBER[engine][name])


def chunks(ap):
    return ap.rearrange("p (c n) -> p c n", n=CHUNK)


def pe_small(k, pe, bank, lhs, rhs, transpose=False):
    for half in HALVES:
        for c in range(CH):
            cs = slice(c * CHUNK, (c + 1) * CHUNK)
            out = k.ps[half, bank, cs]
            mm = pe.matmul(out, lhs[half, cs], k.i64[half, :] if transpose else rhs[half, cs],
                           start=True, stop=True)
    return mm


def tensor_layer1(k, pe):
    st = Steps(k, "pe", pe)
    pe_memory(k, pe, 1)
    pe_all_taken(k, pe, "rwkv")
    pe_squares(k, pe, "l1", DT, S, 0, k.inv_d)
    pe.wait_ge(*k.on("l1_lo", DT))
    pe_linear(k, pe, "rwkv", (k.h_hi, k.h_lo))
    pe_all_taken(k, pe, "wo1")
    pe.wait_ge(*k.on("rw_params", 16 * 4))
    st.after("act", "sig_g")
    for s in range(SETS):
        for p in range(2):
            j = 2 * s + p
            js = slice(j * P, (j + 1) * P)
            if s or p:
                st.after("dve", ("CV", s, 0) if p else ("out", s - 1, 1))
                st.after("act", ("natK", s, 0) if p else ("ystd", s - 1, 1))
            st.done(pe.matmul(k.ps[:, 0], k.wa2[HALVES[0], js], k.zwa[HALVES[0]], start=True, stop=True), ("U", s, p))
            st.done(pe.matmul(k.ps[:, 1], k.wa2[HALVES[1], js], k.zwa[HALVES[1]], start=True, stop=True), ("A", s, p))
            st.done(pe_small(k, pe, 6, k.v3[:, j], None, transpose=True), ("TV", s, p))
            st.after("act", ("kk2", s, p))
            st.done(pe.matmul(k.ps[:, 2], k.blk1[:], k.t3, start=True, stop=True), ("SS", s, p))
            st.after("dve", ("rk", s, p))
            st.done(pe.matmul(k.ps[:, 3], k.blk1[:], k.tb, start=True, stop=True), ("BON", s, p))
            st.after("dve", ("hats", s, p))
            st.done(pe_small(k, pe, 4, k.t2, None, transpose=True), ("TB", s, p))
            st.done(pe_small(k, pe, 5, k.t4, None, transpose=True), ("TK", s, p))
            st.done(pe_small(k, pe, 7, k.t2, k.at[:, p]), ("AT", s, p))
            st.after("act", ("std", s, p))
            st.done(pe_small(k, pe, 0, k.at[:, p], k.t2), ("AA", s, p))
            st.done(pe_small(k, pe, 1, k.t4, k.at[:, p]), ("BT", s, p))
            st.done(pe_small(k, pe, 2, k.t2, k.r3[:, j]), ("CP", s, p))
            st.after("dve", ("bv", s, p))
            st.done(pe_small(k, pe, 3, k.t4, k.r3[:, j]), ("CV", s, p))
        for p in range(2):
            b = 4 * p
            st.after("dve", ("CV", s, 1))
            st.after("act", ("natK", s, 1))
            st.done(pe_small(k, pe, b, k.DT_[p], k.D_[p]), ("D2", s, p))
            st.done(pe_small(k, pe, b + 1, k.D_[p], k.DT_[p]), ("D2T", s, p))
        for p in range(2):
            b = 4 * p
            st.after("dve", ("D2", s, p))
            st.after("act", ("D2T", s, p))
            st.done(pe_small(k, pe, b, k.D2T_[p], k.D2_[p]), ("D4", s, p))
            st.done(pe_small(k, pe, b + 1, k.D2_[p], k.D2T_[p]), ("D4T", s, p))
            st.done(pe_small(k, pe, b + 2, k.D2_[p], k.XT_[p]), ("X1", s, p))
        for p in range(2):
            b = 4 * p
            st.after("dve", ("X1", s, p))
            st.after("act", ("D4T", s, p))
            st.done(pe_small(k, pe, b, k.DT_[p], k.D_[p]), ("D8", s, p))
            st.done(pe_small(k, pe, b + 1, k.D_[p], k.XT_[p]), ("X2", s, p))
        for p in range(2):
            st.after("dve", ("X2", s, p))
            st.done(pe_small(k, pe, 4 * p + 2, k.D2_[p], k.XT_[p]), ("X3", s, p))
        for p in range(2):
            b = 4 * p
            st.after("dve", ("X3", s, p))
            st.done(pe_small(k, pe, b, k.O_[p], k.XT_[p]), ("ZT", s, p))
            st.done(pe_small(k, pe, b + 1, k.XT_[p], k.O_[p]), ("Z", s, p))
            st.done(pe_small(k, pe, b + 3, k.XT_[p], None, transpose=True), ("X", s, p))
        for p in range(2):
            st.after("dve", ("ZT", s, p))
            st.after("act", ("Z", s, p))
            st.done(pe_small(k, pe, 4 * p + 2, k.DT_[p], k.D_[p]), ("Z2", s, p))
        for p in range(2):
            st.after("act", ("Z2", s, p))
            st.after("dve", ("IZ", s, p))
            st.done(pe_small(k, pe, 4 * p, k.D2T_[p], k.E_[p]), ("U2", s, p))
        for p in range(2):
            st.after("dve", ("U2", s, p))
            st.done(pe_small(k, pe, 4 * p + 1, k.D2_[p], k.E_[p]), ("TT", s, p))
        st.after("dve", ("TT", s, 1))
        st.after("dve", ("M0", s))
        for c in range(CH):
            cs = slice(c * CHUNK, (c + 1) * CHUNK)
            m = c % 2
            if c:
                st.after("dve", ("M", s, c - 1))
            for p in range(2):
                for half in HALVES:
                    out = k.ps[half, 0, p * DH:(p + 1) * DH]
                    pe.matmul(out, k.at[half, p, cs], k.M[half, m, p], start=True, stop=False)
                    mm = pe.matmul(out, k.BT[half, p, cs], k.nV[half, p, cs], start=False, stop=True)
            st.done(mm, ("G", s, c))
            st.after("dve", ("G", s, c))
            for p in range(2):
                for half in HALVES:
                    mm = pe.matmul(k.ps[half, 1, p * DH:(p + 1) * DH], k.TT[half, p, cs], k.G[half, p],
                                   start=True, stop=True)
            st.done(mm, ("P", s, c))
            st.after("dve", ("P", s, c))
            for p in range(2):
                for half in HALVES:
                    out = k.ps[half, 2, p * DH:(p + 1) * DH]
                    pe.matmul(out, k.nB[half, p, cs], k.Pm[half, m, p], start=True, stop=False)
                    mm = pe.matmul(out, k.nK[half, p, cs], k.nV[half, p, cs], start=False, stop=True)
            st.done(mm, ("M", s, c))
            for p in range(2):
                j = 2 * s + p
                for half in HALVES:
                    out = k.ps[half, 4 + p, cs]
                    pe.matmul(out, k.M[half, m, p], k.r3[half, j, cs], start=True, stop=False)
                    pe.matmul(out, k.Pm[half, m, p], k.CP[half, p, cs], start=False, stop=False)
                    mm = pe.matmul(out, k.nV[half, p, cs], k.CV[half, p, cs], start=False, stop=True)
            st.done(mm, ("Y", s, c))
        for p in range(2):
            j = 2 * s + p
            js = slice(j * P, (j + 1) * P)
            st.after("dve", ("y", s, p))
            st.done(pe.matmul(k.ps[:, 0 + p], k.blkm[:], k.k3[:, j], start=True, stop=True), ("mean", s, p))
            st.after("act", ("ysq", s, p))
            st.done(pe.matmul(k.ps[:, 2 + p], k.blkm[:], k.t0, start=True, stop=True), ("var", s, p))
            pe.matmul(k.ps[:, 6 + p], k.g2a[:, js], k.zg0, start=True, stop=False)
            st.done(pe.matmul(k.ps[:, 6 + p], k.g2b[0:32, js], k.zg1[0:32], start=False, stop=True), ("g", s, p))
    st.after("dve", ("out", SETS - 1, 1))
    pe_attention(k, pe, ("mem",), "1")
    pe.wait_ge(*k.on("at_group1", 4))
    pe_cat_turn(k, pe, "1", range(6, DT))
    pe.wait_ge(*k.on("cat_lo1", 2))
    pe.wait_ge(*k.on("mix_lo", 6))
    pe_linear(k, pe, "wo1", (k.xs_hi, k.xs_lo))
    pe_ffn(k, pe, "c")
    pe_all_taken_end(k, pe)
    pe_squares(k, pe, "fin2", DT, S, 0, k.inv_d)


def pe_all_taken_end(k, pe):
    pe.wait_ge(k.sem("psum_free"), 4 + N_UNITS)


def scalar_layer1(k, act):
    st = Steps(k, "act", act)
    act_memory(k, act, 1)
    act_norm_stats(k, act, "l1")
    act_scale_split(k, act, "l1", None, lambda t: k.h_hi[:, t], DT, S)
    for dst, src in ((k.wa2, k.wa2_dram), (k.g2a, k.g2_dram[0:P]), (k.g2b[0:32], k.g2_dram[P:P + 32]),
                     (k.rconst, k.rconst_dram)):
        act.dma_start(dst, src).then_inc(k.sem("rw_params"), 16)
    n0, u0 = PH["rwkv"]
    for j in range(12):
        act_slot(k, act, n0 + j, 0, 4)
        if j < 11:
            for e in range(2):
                t = 2 * j + e
                if t < 21:
                    if t >= 2:
                        st.after("dve", ("shift", t - 2))
                    st.done(act.activation(k.zbuf[:, t % 2, 1:1 + S], k.ps[:, bank_pair(u0 + j) + e],
                                           ACT.Copy), ("z", t))
    st.after("dve", ("shift", 20))
    st.done(act.activation(k.zwa[HALVES[0]], k.zwa[HALVES[0]], ACT.Tanh), "tanh")
    act.activation(k.zg0, k.zg0, ACT.Sigmoid)
    st.done(act.activation(k.zg1[0:32], k.zg1[0:32], ACT.Sigmoid), "sig_g")
    for s in range(SETS):
        for p in range(2):
            j = 2 * s + p
            st.after("pe", ("U", s, p))
            if s or p:
                st.after("pe", ("CV", s, 0) if p else ("g", s - 1, 1))
                st.after("dve", ("CV", s, 0) if p else ("out", s - 1, 1))
            st.done(act.activation(k.t0, k.ps[:, 0], ACT.Sigmoid, bias=pcol(k, "w0", j)), ("sgw", s, p))
            st.after("pe", ("A", s, p))
            st.done(act.activation(k.ta, k.ps[:, 1], ACT.Sigmoid, bias=pcol(k, "a0", j)), ("a", s, p))
            st.after("dve", ("kk0", s, p))
            st.done(act.activation(k.t3, k.t2, ACT.Square), ("kk2", s, p))
            st.after("dve", ("L", s, p))
            st.done(act.activation(k.t5, k.t1, ACT.Exp), ("W", s, p))
            st.done(act.activation(k.t6, k.t1, ACT.Exp, scale=-1.0), ("Wi", s, p))
            st.done(act.activation(k.t0, k.t0, ACT.Exp), ("Wp", s, p))
            st.after("pe", ("SS", s, p))
            st.done(act.activation(k.t3, k.ps[:, 2], ACT.Sqrt), ("std", s, p))
            for n, bank, dst, src in (("natB", 4, k.nB, "TB"), ("natK", 5, k.nK, "TK")):
                st.after("pe", (src, s, p))
                st.done(act.activation(dst[:, p], k.ps[:, bank], ACT.Copy), (n, s, p))
        for stage in ((("D2T", 1, k.D2T_),), (("D4T", 1, k.DT_),), (("Z", 1, k.D_), ("X", 3, k.D2_)),
                      (("Z2", 2, k.D2T_),)):
            for p in range(2):
                for n, b, dst in stage:
                    st.after("pe", (n, s, p))
                    st.done(act.activation(dst[p], k.ps[:, 4 * p + b], ACT.Copy), (n, s, p))
        for p in range(2):
            st.after("dve", ("yc", s, p))
            if p:
                st.after("pe", ("var", s, 0))
            st.done(act.activation(k.t0, k.k3[:, 2 * s + p], ACT.Square), ("ysq", s, p))
            st.after("pe", ("var", s, p))
            if p:
                st.after("dve", ("out", s, 0))
            st.done(act.activation(k.t1, k.ps[:, 2 + p], ACT.Sqrt, bias=k.gn_eps[:, 0:1]), ("ystd", s, p))
    act_attention(k, act, ("mem",), "1")
    for t in range(6):
        act.activation(k.xs_hi[:, t], k.k3[:, t], ACT.Copy).then_inc(k.sem("mix_hi"), 1)
    act_cat_split(k, act, "1", range(6, DT))
    act_linear(k, act, "wo1")
    act_ffn(k, act, "c", None)
    act_norm_stats(k, act, "fin2", after=("psum_free", 4 + N_UNITS))


def vector_layer1(k, dve, ch):
    st = Steps(k, "dve", dve)
    dve_memory(k, dve, 1)
    dve_rstd(k, dve, "l1", S)
    dve_scale_split(k, dve, "l1", lambda t: k.xT[:, t], lambda t: pcol(k, "norm1", 8 + t), None,
                    lambda t: k.h_lo[:, t], lambda t: k.h_hi[:, t], DT, S)
    ch.link(dve.memset(k.zbuf[:, :, 0:1], 0.0))
    ch.link(dve.memset(k.gn_eps[:], GN_EPS))
    n0, u0 = PH["rwkv"]
    dsts = [k.r3[:, t] for t in range(6)] + [k.k3[:, t] for t in range(6)] + [k.v3[:, t] for t in range(6)] \
        + [k.zwa, k.zg0, k.zg1]
    for t in range(21):
        st.after("act", ("z", t))
        z = k.zbuf[:, t % 2]
        ch.link(dve.tensor_tensor(k.work[:, t % 2], z[:, 0:S], z[:, 1:1 + S], ALU.subtract))
        st.done(dve.scalar_tensor_tensor(dsts[t], k.work[:, t % 2], pcol(k, "mu", t), z[:, 1:1 + S],
                                         ALU.mult, ALU.add), ("shift", t))
        if t % 2 or t == 20:
            dve.memset(k.zero[:], 0.0).then_inc(k.sem("psum_free"), 1)
    dve.wait_ge(*k.on("mm_done", 2 * (n0 + 12)))
    b = bank_pair(u0 + 11)
    dve.tensor_scalar(k.mq[:], k.ps[:, b:b + 2], 0.125, None, ALU.mult).then_inc(k.sem("psum_free"), 1)
    st.done(dve.tensor_scalar(k.omka[:], k.col("k_a", 0, 6), -1.0, 1.0, ALU.mult, ALU.add), "omka")
    ch.link(dve.memset(k.again[:], 1.0))
    ch.link(dve.memset(chunks(k.again)[:, :, 0:1], 0.0))
    dve.wait_ge(*k.on("rw_params", 16 * 4))
    for s in range(SETS):
        for p in range(2):
            vector_pair(k, dve, ch, st, s, p)
        vector_inverse(k, dve, ch, st, s)
        st.done(dve.memset(k.M[:, 0], 0.0), ("M0", s))
        for c in range(CH):
            m = c % 2
            st.after("pe", ("G", s, c))
            st.done(dve.tensor_copy(flat(k.G[:]), k.ps[:, 0, 0:P]), ("G", s, c))
            st.after("pe", ("P", s, c))
            st.done(dve.tensor_copy(flat(k.Pm[:, m]), k.ps[:, 1, 0:P]), ("P", s, c))
            st.after("pe", ("M", s, c))
            if c == 0:
                st.after("dve", ("M0", s))
            else:
                st.after("dve", ("M", s, c - 1))
                st.after("pe", ("Y", s, c - 1))
            ch.link(dve.tensor_tensor(flat(k.M[:, 1 - m]), k.ps[:, 2, 0:P], flat(k.M[:, m]), ALU.add))
            st.done(dve.tensor_tensor(k.M[:, 1 - m], k.M[:, 1 - m],
                                      k.wc[:, :, c:c + 1].broadcast_to([P, 2, DH]), ALU.mult), ("M", s, c))
        for p in range(2):
            j = 2 * s + p
            y = k.k3[:, j]
            st.after("pe", ("Y", s, CH - 1))
            st.done(dve.tensor_copy(y, k.ps[:, 4 + p]), ("y", s, p))
            st.after("dve", ("y", s, p))
            st.after("pe", ("mean", s, p))
            st.done(dve.tensor_tensor(y, y, k.ps[:, 0 + p], ALU.subtract), ("yc", s, p))
            st.after("act", ("ystd", s, p))
            st.after("dve", ("yc", s, p))
            ch.link(dve.reciprocal(k.t1, k.t1))
            ch.link(dve.tensor_tensor(y, y, k.t1, ALU.mult))
            ch.link(dve.tensor_scalar(y, y, pcol(k, "lnx_w", j), pcol(k, "lnx_b", j), ALU.mult, ALU.add))
            ch.link(dve.tensor_tensor(y, y, k.v3[:, j], ALU.add))
            st.after("pe", ("g", s, p))
            st.done(dve.tensor_tensor(y, k.ps[:, 6 + p], y, ALU.mult), ("out", s, p))
    ch.link(dve.memset(k.azero[:], 0.0))
    dve_attention(k, dve, ch, ("mem",), "1")
    for t in range(6):
        dve.wait_ge(*k.on("mix_hi", t + 1))
        dve.tensor_tensor(k.xs_lo[:, t], k.k3[:, t], k.xs_hi[:, t].bitcast(F32), ALU.subtract) \
            .then_inc(k.sem("mix_lo"), 1)
    dve_cat_split(k, dve, "1", range(6, DT))
    dve_residual(k, dve, ch, "wo1", None)
    dve_ffn(k, dve, ch, "c", lambda t: pcol(k, "norm2", 8 + t), None, None)
    dve_norm_in_place(k, dve, "fin2", lambda t: pcol(k, "final2", t))


def vector_pair(k, dve, ch, st, s, p):
    j = 2 * s + p
    r, kk, v = k.r3[:, j], k.k3[:, j], k.v3[:, j]
    if s or p:
        st.after("pe", ("CV", s, 0) if p else ("g", s - 1, 1))
        st.after("act", ("natK", s, 0) if p else ("ystd", s - 1, 1))
        st.after("dve", ("CV", s, 0) if p else ("out", s - 1, 1))
    st.done(dve.tensor_scalar(k.t2, kk, pcol(k, "k_k", j), None, ALU.mult), ("kk0", s, p))
    st.after("act", ("sgw", s, p))
    ch.link(dve.tensor_scalar(k.t0, k.t0, -DECAY, None, ALU.mult))
    ch.link(dve.tensor_tensor_scan(k.t1, k.again, k.t0, 0.0, ALU.mult, ALU.add))
    st.done(dve.tensor_tensor(k.t0, k.t1, k.t0, ALU.subtract), ("L", s, p))
    st.after("act", ("a", s, p))
    ch.link(dve.tensor_scalar(k.t4, k.ta, pcol(k, "k_a", j), k.omka[:, j:j + 1], ALU.mult, ALU.add))
    st.after("dve", ("kk0", s, p))
    st.done(dve.tensor_tensor(kk, kk, k.t4, ALU.mult), ("kp", s, p))
    st.after("dve", ("kp", s, p))
    st.done(dve.scalar_tensor_tensor(k.tb, r, pcol(k, "r_k", j), kk, ALU.mult, ALU.mult), ("rk", s, p))
    st.after("pe", ("TV", s, p))
    st.done(dve.tensor_copy(k.nV[:, p], k.ps[:, 6]), ("natV", s, p))
    st.after("pe", ("BON", s, p))
    st.done(dve.tensor_tensor(v, v, k.ps[:, 3], ALU.mult), ("bv", s, p))
    st.after("act", ("W", s, p))
    st.after("dve", ("rk", s, p))
    st.done(dve.tensor_tensor(r, r, k.t5, ALU.mult), ("rt", s, p))
    ch.link(dve.tensor_copy(k.wc[:, p], chunks(k.t5)[:, :, CHUNK - 1]))
    st.after("act", ("std", s, p))
    ch.link(dve.tensor_scalar(k.t3, k.t3, 1e-12, None, ALU.max))
    ch.link(dve.reciprocal(k.t3, k.t3))
    ch.link(dve.tensor_tensor(k.t2, k.t2, k.t3, ALU.mult))
    st.done(dve.scalar_tensor_tensor(k.at[:, p], k.t2, -1.0, k.t0, ALU.mult, ALU.mult), ("at", s, p))
    st.after("dve", ("at", s, p))
    ch.link(dve.tensor_tensor(k.t2, k.t2, k.ta, ALU.mult))
    ch.link(dve.tensor_tensor(k.t2, k.t2, k.t6, ALU.mult))
    st.done(dve.tensor_tensor(k.t4, kk, k.t6, ALU.mult), ("hats", s, p))

    def masked(name, bank, dst, mask, src=None):
        st.after("pe", (src or name, s, p))
        st.done(dve.tensor_tensor(chunks(dst), chunks(k.ps[:, bank]),
                                  mask.unsqueeze(1).broadcast_to([P, CH, CHUNK]), ALU.mult), (name, s, p))

    masked("DT", 7, k.DT_[p], k.m_diag_up, "AT")
    masked("D", 0, k.D_[p], k.m_diag_low, "AA")
    masked("O", 0, k.O_[p], k.m_off_low, "AA")
    masked("BT", 1, k.BT[:, p], k.m_up)
    masked("CP", 2, k.CP[:, p], k.m_up_eq)
    masked("CV", 3, k.CV[:, p], k.m_up_eq)


def vector_inverse(k, dve, ch, st, s):
    i64 = k.i64.unsqueeze(1).broadcast_to([P, CH, CHUNK])

    def copy(name, p, bank, dst):
        st.after("pe", (name, s, p))
        st.done(dve.tensor_copy(dst, k.ps[:, 4 * p + bank]), (name, s, p))

    def add(name, p, bank, dst):
        st.after("pe", (name, s, p))
        st.done(dve.tensor_tensor(dst, k.ps[:, 4 * p + bank], dst, ALU.add), (name, s, p))

    for p in range(2):
        st.after("dve", ("DT", s, p))
        st.done(dve.tensor_tensor(chunks(k.XT_[p]), chunks(k.DT_[p]), i64, ALU.add), ("XT", s, p))
        copy("D2", p, 0, k.D2_[p])
    for p in range(2):
        copy("D4", p, 0, k.D_[p])
        st.after("dve", ("XT", s, p))
        add("X1", p, 2, k.XT_[p])
    for p in range(2):
        copy("D8", p, 0, k.D2_[p])
        st.after("dve", ("X1", s, p))
        add("X2", p, 1, k.XT_[p])
    for p in range(2):
        st.after("dve", ("X2", s, p))
        add("X3", p, 2, k.XT_[p])
    for p in range(2):
        copy("ZT", p, 0, k.DT_[p])
    for p in range(2):
        st.after("dve", ("ZT", s, p))
        st.done(dve.tensor_tensor(chunks(k.E_[p]), chunks(k.DT_[p]), i64, ALU.add), ("IZ", s, p))
    for p in range(2):
        st.after("dve", ("IZ", s, p))
        add("U2", p, 0, k.E_[p])
    for p in range(2):
        copy("TT", p, 1, k.TT[:, p])


def layer1_map(k, region, h_at, rest_at):
    r = region(h_at)
    k.at, k.nB, k.nK, k.nV = (r(n, [P, 2, S]) for n in ("at", "nB", "nK", "nV"))
    k.BT, k.CP, k.CV, k.TT = (r(n, [P, 2, S]) for n in ("BT", "CP", "CV", "TT"))
    r = region(h_at)
    hi, lo = r("mix_hi", [P, DT, S], F32R), r("mix_lo", [P, DT, S], F32R)
    mix = (hi, lo)
    r = region(rest_at)
    k.r3, k.k3, k.v3 = (r(n, [P, 6, S]) for n in ("r3", "k3", "v3"))
    mem = (r("mkT1", [P, 2, N_MEM]), r("mv1", [P, 2, N_MEM]), r("mq1", [P, 2, S]))
    z = r("zs", [P, 3, S])
    k.zwa, k.zg0, k.zg1 = (z[:, i] for i in range(3))
    k.wa2, k.g2a, k.g2b = (r(n, [P, 768])[:] for n in ("wa2", "g2a", "g2b"))
    k.rconst = r("rconst", [P, 6 * CHUNK + 2 * P])[:]
    masks = [k.rconst[:, i * CHUNK:(i + 1) * CHUNK] for i in range(6)]
    k.m_up, k.m_up_eq, k.m_diag_low, k.m_diag_up, k.m_off_low, k.i64 = masks
    k.blkm, k.blk1 = k.rconst[:, 384:512], k.rconst[:, 512:640]
    k.omka, k.gn_eps = r("omka", [P, 6]), r("gn_eps", [P, 1])
    k.M, k.Pm, k.G = r("M", [P, 2, 2, DH]), r("Pm", [P, 2, 2, DH]), r("G", [P, 2, DH])
    k.wc = r("wc", [P, 2, CH])
    temps_at = r.at[0]
    mats = [r(f"mat{i}", [P, S])[:] for i in range(6)]
    k.D_, k.DT_, k.O_ = mats[0:2], mats[2:4], mats[4:6]
    t = [r(f"tmp{i}", [P, S])[:] for i in range(4)]
    k.t4, k.t5, k.t6, k.ta = t
    k.again = r("again", [P, S])[:]
    k.t0, k.t1, k.t2, k.t3 = (k.work[:, i] for i in range(4))
    k.tb = k.std[:]
    k.D2_, k.D2T_ = [t[0], t[1]], [t[2], t[3]]
    k.XT_, k.E_ = [k.t0, k.t1], [k.t2, k.t3]
    r = region(temps_at)
    memT, m_hi, m_lo = r("memT1", [P, DT, N_MEM]), r("m_hi1", [P, DT, N_MEM], F32R), None
    k.zbuf = region(temps_at)("zbuf", [P, 2, 1 + S])
    m_lo = region(rest_at)("m_lo1", [P, DT, N_MEM], F32R)
    r = region(temps_at)
    att = (r("cat1", [P, 4, 256]), r("aneg1", [P, 2, S]), r("ap1", [P, 2, S]), r("apT1", [P, 2, S]),
           r("azero1", [P, N_MEM]), r("asum1", [P, 2, HEADS]), r("aw1", [P, HEADS]), r("amax1", [P, 2]))
    k.layer1_names = (mem, memT, m_hi, m_lo, att, mix, 768)


def layer_names(k, names):
    (k.mkT, k.mv, k.mq), k.memT, k.m_hi, k.m_lo, att, (k.xs_hi, k.xs_lo), k.cat_from = names
    k.cat, k.aneg, k.ap, k.apT, k.azero, k.asum, k.aw, k.amax = att


def build(nc, slots, cols, x, row_bv, sel, mem, pos, w1, w2, wa2, g2, rconst, out):
    with ExitStack() as ctx:
        k = Kernel(nc, ctx)

        def sb(name, shape, dt=F32, stack=ctx):
            return stack.enter_context(nc.sbuf_tensor(name, shape, dt))

        k.n_slots = slots.shape[0]
        k.slots_dram, k.cols_dram, k.x_dram, k.row_bv_dram, k.sel_dram = slots, cols, x, row_bv, sel
        k.out_dram = out
        k.mem_dram, k.pos_dram, k.w1_dram, k.w2_dram = mem, pos, w1, w2
        k.wa2_dram, k.g2_dram, k.rconst_dram = wa2, g2, rconst
        k.ps = ctx.enter_context(nc.psum_tensor("ps", [P, 8, S], F32))
        k.cols = sb("cols", [P, N_COLS])
        k.xT = sb("xT", [P, DT, S])
        k.raw = [sb(f"raw{j}", [P, DT, SLOT_COLS]) for j in range(2)]
        k.w_hi = [sb(f"w_hi{j}", [P, DT, SLOT_COLS], F32R) for j in range(2)]
        k.w_lo = [sb(f"w_lo{j}", [P, DT, SLOT_COLS], F32R) for j in range(2)]
        k.work = sb("work", [P, 4, S])
        k.std = k.rstd = sb("std", [P, S])
        k.inv_d, k.inv_h, k.one = sb("inv_d", [P, P]), sb("inv_h", [P, P]), sb("one", [P, P])
        k.eps, k.zero = sb("eps", [P, 1]), sb("zero", [P, 1])
        k.mod, k.A = sb("mod", [P, 48]), sb("A", [P, 8])
        k.csilu, k.cHL = sb("csilu", [P, 8]), sb("cHL", [P, 8, 2], F32R)
        k.raw_landed = [k.sem("raw_landed_even"), k.sem("raw_landed_odd")]

        h_at = nc.sbuf_base
        rest_at = h_at + 2 * DT * S * 4

        def region(base):
            at = [base]

            def place(name, shape, dt=F32):
                size = 4 * int(np.prod(shape[1:]))
                t = nc.alloc_sbuf_tensor_at(name, shape, dt, offset=at[0])
                at[0] += -(-size // 32) * 32
                return t

            place.at = at
            return place

        h = region(h_at)
        k.h_hi, k.h_lo = h("h_hi", [P, DT, S], F32R), h("h_lo", [P, DT, S], F32R)
        r = region(rest_at)
        k.aT = r("aT", [P, DT, TAPS - 1 + S])
        k.qkT = r("qkT", [P, 2 * DT, S])
        k.qT, k.kT = k.qkT[:, 0:DT], k.qkT[:, DT:2 * DT]
        cs_at = r.at[0] - DT * S * 4
        k.v = r("v", [P, 4, D])
        k.rows = r("rows", [P, 5, S])
        k.gcol = r("gcol", [P, 16])
        k.sel = r("sel", [4, ML_HEADS, P])
        early_at = r.at[0]
        k.row_bv = r("row_bv", [P, 1, D])
        k.row_bv2 = k.row_bv[:].broadcast_to([P, 2, D])
        k.qpre = r("qpre", [P, 2, QK_TAPS - 1 + S])
        k.scT = region(early_at)("scT", [P, 1280])
        r = region(cs_at)
        k.cs_hi, k.cs_lo = r("cs_hi", [P, DT, S], F32R), r("cs_lo", [P, DT, S], F32R)
        r = region(rest_at)
        k.hid_hi, k.hid_lo = r("hid_hi", [P, FT, S], F32R), r("hid_lo", [P, FT, S], F32R)
        r = region(rest_at)
        k.nq, k.mq = r("nq", [P, 6, S]), r("mq", [P, 2, S])
        k.kds, k.kdw = r("kds", [P, GROUPS, S]), r("kdw", [P, GROUPS, S])
        k.vs, k.vw = r("vs", [P, 4, 256]), r("vw", [P, 4, 256])
        k.kcb, k.vcb = r("kcb", [P, GROUPS * N_CMP]), r("vcb", [N_CMP, GROUPS, DH])
        k.mkT, k.mv = r("mkT", [P, 2, N_MEM]), r("mv", [P, 2, N_MEM])
        k.gates = r("gates", [P, 4, 36])
        k.hidc = r("hidc", [P, 2, 4 * N_CMP])
        stage_at = r.at[0]
        k.kcT, k.vcT = r("kcT", [P, 2, S]), r("vcT", [P, 2, S])
        k.kT1 = r("kT1", [P, 2, S])
        k.pos, k.w2 = r("pos", [P, 2, 32]), r("w2", [P, P + DH])
        k.blocks = r("blocks", [P, 2, N_CMP, 32])
        k.w1 = r("w1", [P, 32, P])
        k.kT2 = k.kT1
        r = region(stage_at)
        k.memT = r("memT", [P, DT, N_MEM])
        k.m_hi, k.m_lo = r("m_hi", [P, DT, N_MEM], F32R), r("m_lo", [P, DT, N_MEM], F32R)
        r = region(stage_at)
        k.table, k.table_c = r("table", [P, HEADS, S]), r("table_c", [P, HEADS, 4 * N_CMP])
        r = region(stage_at)
        k.xs_hi, k.xs_lo = r("xs_hi", [P, DT, S], F32R), r("xs_lo", [P, DT, S], F32R)
        r = region(h_at)
        k.cat = r("cat", [P, 4, D])
        k.aneg, k.ap, k.apT = r("aneg", [P, 2, S]), r("ap", [P, 2, S]), r("apT", [P, 2, S])
        k.azero = r("azero", [P, N_MEM])
        k.asum, k.aw, k.amax = r("asum", [P, 2, HEADS]), r("aw", [P, HEADS]), r("amax", [P, 2])
        assert r.at[0] <= rest_at
        layer1_map(k, region, h_at, rest_at)
        k.layer0_names = ((k.mkT, k.mv, k.mq), k.memT, k.m_hi, k.m_lo,
                          (k.cat, k.aneg, k.ap, k.apT, k.azero, k.asum, k.aw, k.amax), (k.xs_hi, k.xs_lo), 0)

        block = ctx.enter_context(nc.Block())

        @block.sync
        def _(sp):
            sync_program(k, sp)

        @block.gpsimd
        def _(pool):
            gpsimd_program(k, pool)

        @block.scalar
        def _(act):
            layer_names(k, k.layer0_names)
            scalar_block1(k, act)
            scalar_layer0(k, act)
            layer_names(k, k.layer1_names)
            scalar_layer1(k, act)

        @block.vector
        def _(dve):
            ch = Chain(dve, k.sem("vector_step"))
            layer_names(k, k.layer0_names)
            vector_block1(k, dve, ch)
            vector_layer0(k, dve, ch)
            layer_names(k, k.layer1_names)
            vector_layer1(k, dve, ch)

        @block.tensor
        def _(pe):
            layer_names(k, k.layer0_names)
            tensor_block1(k, pe)
            tensor_layer0(k, pe)
            layer_names(k, k.layer1_names)
            tensor_layer1(k, pe)


def layout(inputs):
    a = {name: np.asarray(value) for name, value in inputs.items()}
    pos, w1, w2 = compression_weights(a)
    arrays = {
        "slots": stream_of_weights(a),
        "cols": parameter_columns(a),
        "x": by_tiles(a["x"][0]),
        "row_bv": np.broadcast_to(a["b_in"][0][4096:5120], (P, 1, D)),
        "sel": selectors(),
        "mem": by_tiles(a["mem_2"][0]),
        "pos": pos, "w1": w1, "w2": w2,
        "wa2": np.concatenate([a["rw_w2_2"][0], a["rw_a2_2"][0]]),
        "g2": a["rw_g2_2"][0],
        "rconst": recurrence_constants(),
    }
    return {name + "_dram": np.ascontiguousarray(value) for name, value in arrays.items()}


def kernel(**inputs):
    import concourse.bacc as bacc
    from concourse.bass_utils import run_bass_kernel_spmd

    arrays = layout(inputs)
    nc = bacc.Bacc("TRN2", target_bir_lowering=False, num_devices=1)
    args = [nc.dram_tensor(name, v.shape, F32, kind="ExternalInput").ap() for name, v in arrays.items()]
    args.append(nc.dram_tensor("out_dram", (P, DT, S), F32, kind="ExternalOutput").ap())
    build(nc, *args)
    result = run_bass_kernel_spmd(nc, [arrays], core_ids=[0])
    got = np.asarray(result.results[0]["out_dram"])
    return np.ascontiguousarray(got.transpose(1, 0, 2).reshape(D, S).T)[None]
```

```python
from contextlib import ExitStack

import numpy as np

import concourse.bass as bass
from concourse import mybir

P = 128
D = 1024
S = 512
DT = D // P
SLOT_COLS = 256
FF = 2816
FT = FF // P
TAPS = 31
CONV_POOL = 7
CONV_SHARED = 16
QK_TAPS = 4
ML_HEADS = 4
N_MEM = 256
HEADS = 12
GROUPS = 4
DH = 64
N_CMP = (S - 32) // 16 + 1
CHUNK = 64
NORM_BANK = 7
SBUF_END = 224 * 1024
EPS = 1e-6
GN_EPS = 64e-5
BIG = 1.0e30

F32 = mybir.dt.float32
F32R = mybir.dt.float32r
ACT = mybir.ActivationFunctionType
ALU = mybir.AluOpType

PHASES_LIST = [
    ("ada1", 8, 8),
    ("glu", 8, 8),
    ("qk", 8, 8),
    ("if", 1, 1),
    ("v", 4, 4),
    ("ada2", 16, 16),
    ("pw", 4, 4),
    ("o", 4, 4),
    ("merge", 8, 8),
    ("w_out", 4, 4),
    ("up_a", 22, 22), ("down_a", 12, 4),
    ("memkv0", 2, 2), ("nsa", 11, 11), ("wo0", 4, 4), ("up_b", 22, 22), ("down_b", 12, 4),
    ("memkv1", 2, 2), ("rwkv", 12, 12), ("wo1", 4, 4), ("up_c", 22, 22), ("down_c", 12, 4),
]


def phase_table():
    table, n, u = {}, 0, 0
    for name, slots, units in PHASES_LIST:
        table[name] = (n, u)
        n += slots
        u += units
    return table, n, u


PH, N_SLOTS, N_UNITS = phase_table()

COLS_LIST = [
    ("c", 8), ("b_ada", 48), ("norm_mix_g", 8), ("b_glu", 16), ("b_qk", 16), ("b_o", 8), ("b_merge", 16),
    ("b_i", 1), ("b_f", 1), ("conv_w", 8 * TAPS), ("conv_b", 8), ("ln_g", 8), ("ln_b", 8), ("b_pw", 8),
    ("qk_w", 16 * QK_TAPS), ("qk_b", 16), ("mlstm_g", 8), ("ffn_g", 8), ("final_g", 8),
    ("norm1", 16), ("norm_mem", 16), ("norm2", 16), ("final2", 8),
    ("mu", 21), ("w0", 6), ("a0", 6), ("k_k", 6), ("k_a", 6), ("r_k", 6), ("lnx_w", 6), ("lnx_b", 6),
    ("row_gate_b", 36),
    ("ident", P), ("after", P), ("dist", S), ("dist_c", 4 * N_CMP), ("seen_c", 4 * N_CMP),
]


def cols_table():
    table, at = {}, 0
    for name, n in COLS_LIST:
        table[name] = (at, n)
        at += n
    return table, at


CT, N_COLS = cols_table()


def _tiles(v):
    v = np.asarray(v)
    pad = -len(v) % P
    if pad:
        v = np.concatenate([v, np.zeros(pad, v.dtype)])
    return v.reshape(-1, P).T


def _slot(w):
    out = np.zeros((D, SLOT_COLS), np.float32)
    out[: w.shape[0], : w.shape[1]] = w
    return out.reshape(DT, P, SLOT_COLS).transpose(1, 0, 2).reshape(P, DT * SLOT_COLS)


def _groups(w):
    return [_slot(w[:, g:g + SLOT_COLS]) for g in range(0, w.shape[1], SLOT_COLS)]


def _pairs(w, half):
    return [s for g in range(0, half, SLOT_COLS)
            for s in (_slot(w[:, g:g + SLOT_COLS]), _slot(w[:, half + g:half + g + SLOT_COLS]))]


def _down(w):
    return [_slot(w[k:k + D, g:g + SLOT_COLS]) for g in range(0, D, SLOT_COLS) for k in range(0, FF, D)]


def stream_of_weights(a):
    w_in = a["w_in"][0]
    gates = np.zeros((D, SLOT_COLS), np.float32)
    gates[:, 0:4] = w_in[:, 6144:6148]
    gates[:, P:P + 4] = w_in[:, 6148:6152]
    nsa, rw = a["nsa_w_in_2"][0], a["rw_w_in_2"][0]
    ada = _groups(a["w_ada"][0])
    slots = ada[:8]
    slots += _pairs(w_in[:, 0:2048], D)
    slots += _groups(w_in[:, 2048:4096])
    slots += [_slot(gates)]
    slots += _groups(w_in[:, 4096:5120])
    slots += ada[8:]
    slots += _groups(a["w_conv_pw"][0])
    slots += _groups(w_in[:, 5120:6144])
    slots += _groups(w_in[:, 6152:8200])
    slots += _groups(a["w_out"][0])
    slots += _pairs(a["w_ffn_up"][0], FF) + _down(a["w_ffn_down"][0])
    slots += _groups(a["w_mem_kv_2"][0])
    slots += _groups(nsa[:, 0:2304]) + [_slot(nsa[:, 2304:2340]), _slot(nsa[:, 2340:2596])]
    slots += _groups(a["w_o_2"][0]) + _pairs(a["w_ffn_in_2"][0], FF) + _down(a["w_ffn_out_2"][0])
    slots += _groups(a["w_mem_kv_2"][1])
    slots += _groups(rw[:, 0:2592]) + [_slot(rw[:, 2592:2848])]
    slots += _groups(a["w_o_2"][1]) + _pairs(a["w_ffn_in_2"][1], FF) + _down(a["w_ffn_out_2"][1])
    assert len(slots) == N_SLOTS
    return np.stack(slots)


def parameter_columns(a):
    c = {}
    b_in = a["b_in"][0]
    c["c"] = _tiles(a["c"][0])
    c["b_ada"] = _tiles(a["b_ada"][0])
    c["norm_mix_g"] = _tiles(a["norm_mix_g"][0])
    c["b_glu"] = _tiles(b_in[0:2048])
    c["b_qk"] = _tiles(b_in[2048:4096])
    c["b_o"] = _tiles(b_in[5120:6144])
    c["b_i"] = _tiles(b_in[6144:6148])
    c["b_f"] = _tiles(b_in[6148:6152])
    c["b_merge"] = _tiles(b_in[6152:8200])
    c["conv_w"] = a["conv_dw_w"][0].reshape(TAPS, 8, P).transpose(2, 1, 0).reshape(P, -1)
    c["conv_b"] = _tiles(a["conv_dw_b"][0])
    c["ln_g"] = _tiles(a["conv_ln_g"][0])
    c["ln_b"] = _tiles(a["conv_ln_b"][0])
    c["b_pw"] = _tiles(a["b_conv_pw"][0])
    c["qk_w"] = a["qk_conv_w"][0].reshape(QK_TAPS, 16, P).transpose(2, 1, 0).reshape(P, -1)
    c["qk_b"] = _tiles(a["qk_conv_b"][0])
    c["mlstm_g"] = _tiles(a["mlstm_norm_g"][0])
    c["ffn_g"] = _tiles(a["norm_ffn_g"][0])
    c["final_g"] = _tiles(a["final_norm_g"])
    for name, key in (("norm1", "norm1_2"), ("norm_mem", "norm_mem_2"), ("norm2", "norm2_2")):
        c[name] = np.concatenate([_tiles(a[key][0]), _tiles(a[key][1])], 1)
    c["final2"] = _tiles(a["final_norm_2"])
    c["mu"] = _tiles(a["rw_mu_2"][0])
    for name in ("w0", "a0", "k_k", "k_a", "lnx_w", "lnx_b"):
        c[name] = _tiles(a[f"rw_{name}_2"][0])
    c["r_k"] = _tiles(a["rw_r_k_2"][0].reshape(-1))
    c["row_gate_b"] = np.broadcast_to(a["nsa_gate_b_2"][0], (P, 36))
    p, j = np.arange(P)[:, None], np.arange(P)[None, :]
    c["ident"] = (p == j).astype(np.float32)
    c["after"] = np.where(p > j, -BIG, 0.0).astype(np.float32)
    u = np.arange(S)[None, :] - (S - P)
    c["dist"] = np.where(u <= p, p - u, BIG).astype(np.float32)
    t = np.arange(4)[None, :, None] * P + np.arange(P)[:, None, None]
    dc = t - (16 * np.arange(N_CMP) + 31)[None, None, :]
    c["dist_c"] = np.where(dc >= 0, dc, BIG).astype(np.float32).reshape(P, -1)
    c["seen_c"] = (dc >= 0).astype(np.float32).reshape(P, -1)
    for name, n in COLS_LIST:
        assert c[name].shape == (P, n), (name, c[name].shape)
    return np.concatenate([np.asarray(c[name], np.float32) for name, _ in COLS_LIST], 1)


def by_tiles(x):
    return np.ascontiguousarray(x.T.reshape(-1, P, x.shape[0]).transpose(1, 0, 2))


def compression_weights(a):
    pos, w1, w2 = a["nsa_cmp_pos_2"][0], a["nsa_cmp_w1_2"][0], a["nsa_cmp_w2_2"][0]
    pos = np.tile(pos.transpose(2, 0, 1), (2, 1, 1))
    w1 = np.tile(w1.transpose(0, 2, 1, 3), (1, 2, 1, 1))
    return pos, w1, np.concatenate([w2[0], w2[0], w2[1]], 1)


def recurrence_constants():
    a, b = np.arange(64)[:, None], np.arange(64)[None, :]
    same = a // 16 == b // 16
    masks = [a < b, a <= b, same & (a > b), same & (a < b), ~same & (a > b), a == b]
    p, q = np.arange(P)[:, None], np.arange(P)[None, :]
    half = (p // 64 == q // 64).astype(np.float32)
    masks = [np.tile(m.astype(np.float32), (2, 1)) for m in masks]
    return np.concatenate(masks + [half / 64, half], 1).astype(np.float32)


def selectors():
    return (np.arange(4)[:, None, None] == np.arange(4)[None, :, None]).astype(np.float32).repeat(P, 2)


class Chain:

    def __init__(self, eng, sem):
        self.eng, self.sem, self.n = eng, sem, 0

    def link(self, ins):
        ins.then_inc(self.sem, 1)
        self.n = self.n + 1
        self.eng.wait_ge(self.sem, self.n)


def flat(ap):
    return ap.rearrange("p a b -> p (a b)")


def shared_signals():
    table = {}

    def again(semaphore, counts):
        base = 0
        for name, count in counts:
            table[name] = (semaphore, base)
            base += count

    split = ("n1", "cln", "nfa", "mem0", "l0", "nfb", "mem1", "l1", "nfc")
    in_place = ("fin1", "fin2")
    order = ("n1", "cln", "nfa", "fin1", "mem0", "l0", "nfb", "mem1", "l1", "nfc", "fin2")
    for kind, count in (("sq", DT), ("sum", DT), ("std", 1), ("rstd", 1)):
        again("norm_" + kind, [(f"{n}_{kind}", count) for n in order])
    for kind in ("t", "hi", "lo"):
        again("norm_" + kind, [(f"{n}_{kind}", DT) for n in order if n in split])
    again("norm_x", [(f"{n}_x", DT) for n in in_place])
    for kind in ("silu", "hid_hi", "hid_lo"):
        again(kind, [(f"{kind}_{n}", FT) for n in "abc"])
    again("gate_sigmoid", [("sig_o", DT), ("sig_merge", 2 * DT)])
    full, mem = 4 * (3 * HEADS + 4), 16
    for kind, count in (("scores", full), ("neg", full), ("exp", full), ("pT", full), ("turned", full),
                        ("out", full), ("group", 28), ("seen", 4 * HEADS)):
        again("at_" + kind, [(f"at_{kind}0", count), (f"at_{kind}1", 0)])
    again("cat_turned", [("cat_turned0", DT), ("cat_turned1", 2)])
    again("cat_hi", [("cat_hi0", DT), ("cat_hi1", 2)])
    again("cat_lo", [("cat_lo0", DT), ("cat_lo1", 2)])
    return table


SHARED = shared_signals()


class Kernel:

    def __init__(self, nc, ctx):
        self.nc, self.ctx, self.sems = nc, ctx, {}

    def sem(self, name):
        name = SHARED.get(name, (name, 0))[0]
        if name not in self.sems:
            self.sems[name] = self.ctx.enter_context(self.nc.semaphore(name))
        return self.sems[name]

    def on(self, name, value):
        return self.sem(name), value + SHARED.get(name, (name, 0))[1]

    def col(self, name, j=0, n=1):
        at, width = CT[name]
        return self.cols[:, at + j:at + j + n]


def rounds(eng, count, body):
    if count == 1:
        body(0)
    else:
        with eng.Fori(0, count) as i:
            body(i)


def chained_rounds(chain, count, per, body):
    base = chain.n

    def one(i):
        chain.n = i * per + base
        body(i)

    rounds(chain.eng, count, one)
    chain.n = base + per * count


def bank_pair(u):
    return 2 * (u % 4)


def sync_program(k, sp):
    sp.dma_start(k.cols[:], k.cols_dram).then_inc(k.sem("cols_landed"), 16)
    sp.dma_start(flat(k.raw[0]), k.slots_dram[0]).then_inc(k.raw_landed[0], 16)
    sp.dma_start(k.xT[:], k.x_dram).then_inc(k.sem("x_landed"), 16)
    sp.dma_start(flat(k.raw[1]), k.slots_dram[1]).then_inc(k.raw_landed[1], 16)
    sp.dma_start(k.row_bv[:], k.row_bv_dram).then_inc(k.sem("row_bv_landed"), 16)
    sp.dma_start(k.sel[:], k.sel_dram).then_inc(k.sem("sel_landed"), 16)

    def pair(i):
        for j in range(2):
            sp.wait_ge(*k.on("w_low", i * 2 + (j + 1)))
            src = k.slots_dram[bass.ds(i * 2 + (2 + j), 1)].rearrange("a p n -> (a p) n")
            sp.dma_start(flat(k.raw[j]), src).then_inc(k.raw_landed[j], 16)

    rounds(sp, k.n_slots // 2 - 1, pair)
    if k.n_slots % 2:
        sp.wait_ge(*k.on("w_low", k.n_slots - 2))
        sp.dma_start(flat(k.raw[0]), k.slots_dram[k.n_slots - 1]).then_inc(k.raw_landed[0], 16)
    for t in range(0, DT, 2):
        sp.wait_ge(*k.on("fin2_x", t + 2))
        sp.dma_start(k.out_dram[:, t:t + 2], k.xT[:, t:t + 2]).then_inc(k.sem("out_stored"), 16)
    sp.wait_ge(k.sem("out_stored"), 16 * (DT // 2))


def pool_low(k, pool, first, skipped, rounds_, last):
    def one(j, i):
        pool.wait_ge(*k.on("w_high", i * 2 + (first + j + 1 - skipped)))
        par = (first + j) % 2
        pool.tensor_tensor(flat(k.w_lo[par]), flat(k.raw[par]), flat(k.w_hi[par]).bitcast(F32),
                           ALU.subtract).then_inc(k.sem("w_low"), 1)

    rounds(pool, rounds_, lambda i: (one(0, i), one(1, i)))
    if last:
        one(2 * rounds_, 0)


def pool_convolution(k, pool):
    ch = Chain(pool, k.sem("pool_step"))
    pool.wait_ge(*k.on("psum_free", 4 + PH["qk"][1]))
    acc, tap = k.pool_acc[:], k.pool_tap[:]
    tiles = [(t, TAPS) for t in range(CONV_POOL, DT)] + [(CONV_POOL - 1, CONV_SHARED)]
    for n, (t, taps) in enumerate(tiles):
        for m in range(taps):
            src, w = k.aT[:, t, m:m + S], k.col("conv_w", t * TAPS + m)
            if m == 0:
                if n:
                    pool.wait_ge(*k.on("conv_pool", n))
                ch.link(pool.tensor_scalar(acc, src, w, k.col("conv_b", t), ALU.mult, ALU.add))
                continue
            ch.link(pool.tensor_scalar(tap, src, w, None, ALU.mult))
            if m < taps - 1:
                ch.link(pool.tensor_tensor(acc, acc, tap, ALU.add))
            elif taps < TAPS:
                pool.tensor_tensor(acc, acc, tap, ALU.add).then_inc(k.sem("conv_shared"), 1)
            else:
                pool.tensor_tensor(k.aT[:, t, 0:S], acc, tap, ALU.add).then_inc(k.sem("conv_pool"), 1)


def gpsimd_program(k, pool):
    glu, ada2, pw = PH["glu"][0], PH["ada2"][0], PH["pw"][0]
    pool.wait_ge(*k.on("w_low", glu))
    pool_low(k, pool, glu, glu, (ada2 - glu) // 2, (ada2 - glu) % 2)
    pool_convolution(k, pool)
    pool.wait_ge(*k.on("w_low", pw))
    pool_low(k, pool, pw, glu + pw - ada2, (N_SLOTS - pw) // 2, (N_SLOTS - pw) % 2)


def pe_slot(k, pe, n0, j, i, per, rhs, width=S, k0=0, kts=DT, start=True, stop=True, banks=None,
            natural=False, ready=None):
    par = (n0 + j) % 2
    pe.wait_ge(*k.on("w_low", i * per + (n0 + j + 1)))
    wh, wl = k.w_hi[par], k.w_lo[par]
    xh, xl = rhs
    if natural:
        for e in range(2):
            for q in range(2):
                for kt in range(kts):
                    for a, (x, w) in enumerate(((xh, wh), (xh, wl), (xl, wh))):
                        t = 2 * e + q
                        mm = pe.matmul(k.ps[:, banks + e, q * width:(q + 1) * width],
                                       x[:, kt, t * P:(t + 1) * P], w[:, kt, 0:width],
                                       start=(kt == 0 and a == 0), stop=(kt == kts - 1 and a == 2))
            mm.then_inc(k.sem("mm_done"), 1)
        return
    for e in range(2):
        for kt in range(kts):
            if ready and e == 0:
                pe.wait_ge(*k.on(ready, kt + 1))
            for a, (w, x) in enumerate(((wh, xh), (wh, xl), (wl, xh))):
                mm = pe.matmul(k.ps[:, banks + e, 0:width], w[:, kt, e * P:(e + 1) * P],
                               x[:, k0 + kt, 0:width],
                               start=(start and kt == 0 and a == 0),
                               stop=(stop and kt == kts - 1 and a == 2))
        mm.then_inc(k.sem("mm_done"), 1)


def pe_linear(k, pe, phase, rhs, slots=None, first=0, width=S, natural=False,
              ready=None):
    n0, u0 = PH[phase]
    n0, u0 = n0 + first, u0 + first
    slots = slots or dict((p, s) for p, s, _ in PHASES_LIST)[phase]

    def some(count, n, u):
        def body(i):
            for j in range(count[1]):
                pe.wait_ge(*k.on("psum_free", i * 4 + (u + j + 1)))
                pe_slot(k, pe, n, j, i, 4, rhs, width=width, banks=bank_pair(u + j), natural=natural)
        rounds(pe, count[0], body)

    if ready:
        pe.wait_ge(*k.on("psum_free", u0 + 1))
        pe_slot(k, pe, n0, 0, 0, 4, rhs, width=width, banks=bank_pair(u0), ready=ready)
        n0, u0, slots = n0 + 1, u0 + 1, slots - 1
    if slots // 4:
        some((slots // 4, 4), n0, u0)
    if slots % 4:
        some((1, slots % 4), n0 + slots // 4 * 4, u0 + slots // 4 * 4)


def pe_ada_slot(k, pe, n, bank):
    pe.wait_ge(k.raw_landed[n % 2], 16 * (n // 2 + 1))
    for kt in range(DT):
        mm = pe.matmul(k.ps[:, bank, 0:256], k.cb[:, kt], k.raw[n % 2][:, kt],
                       start=(kt == 0), stop=(kt == DT - 1))
        if kt == DT - 2:
            mm.then_inc(k.sem("mm_done"), 2)
    mm.then_inc(k.sem("w_low"), 1)


def pe_stay_warm(k, pe, bank, count):
    for _ in range(count):
        pe.matmul(k.ps[:, bank], k.one[:], k.cols[:, 0:S], start=True, stop=True)


def pe_all_taken(k, pe, phase):
    pe.wait_ge(*k.on("psum_free", 4 + PH[phase][1]))


def pe_down(k, pe, phase, rhs, ready, norm=None):
    n0, u0 = PH[phase]
    pe_all_taken(k, pe, phase)
    pe.wait_ge(*k.on(ready, DT))

    def unit(i, u, before=None):
        pe.wait_ge(*k.on("psum_free", i * 2 + (u0 + u + 3)))
        for c in range(3):
            kts = min(DT, FT - c * DT)
            if c:
                pe.wait_ge(*k.on(ready, c * DT + kts))
            pe_slot(k, pe, n0, 3 * u + c, i, 6, rhs, k0=c * DT, kts=kts,
                    start=(c == 0), stop=(c == 2), banks=2 * (u % 2))
            if c == 1 and before is not None:
                pe_sum_unit(k, pe, norm, before, NORM_BANK)

    if norm:
        for u in range(4):
            unit(0, u, u - 1 if u else None)
        pe_sum_unit(k, pe, norm, 3, NORM_BANK)
    else:
        rounds(pe, 2, lambda i: (unit(i, 0), unit(i, 1)))


def pe_project(k, pe, phase, rhs, norm, ready=None):
    n0, u0 = PH[phase]
    for j in range(4):
        pe.wait_ge(*k.on("psum_free", u0 + j + 1))
        pe_slot(k, pe, n0, j, 0, 4, rhs, banks=bank_pair(u0 + j), ready=ready if j == 0 else None)
        if j >= 2:
            pe_sum_unit(k, pe, norm, j - 2, bank_pair(u0))
    for u in (2, 3):
        pe_sum_unit(k, pe, norm, u, bank_pair(u0))


def pe_sum_unit(k, pe, norm, u, bank):
    for t in (2 * u, 2 * u + 1):
        pe.wait_ge(*k.on(norm + "_sq", t + 1))
        pe.matmul(k.ps[:, bank], k.inv_d[:], k.work[:, t % 2], start=(t == 0), stop=(t == DT - 1)) \
            .then_inc(k.sem(norm + "_sum"), 1)


def act_high(k, act, par, landed):
    act.wait_ge(k.raw_landed[par], landed)
    act.activation(flat(k.w_hi[par]), flat(k.raw[par]), ACT.Copy).then_inc(k.sem("w_high"), 1)


def act_slot(k, act, n, i, per):
    act.wait_ge(*k.on("mm_done", i * (2 * per) + 2 * (n + 1)))
    if n + 2 < k.n_slots and not PH["ada2"][0] <= n + 2 < PH["pw"][0]:
        act_high(k, act, n % 2, i * (8 * per) + 16 * ((n + 2) // 2 + 1))


def act_linear(k, act, phase, evac=None, slots=None, first=0):
    n0, u0 = PH[phase]
    n0, u0 = n0 + first, u0 + first
    slots = slots or dict((p, s) for p, s, _ in PHASES_LIST)[phase]

    def body(i, n, u, base, count):
        for j in range(count):
            act_slot(k, act, n + j, i, 4)
            if evac:
                evac(i, base, j, bank_pair(u + j))

    if slots // 4:
        rounds(act, slots // 4, lambda i: body(i, n0, u0, 0, 4))
    if slots % 4:
        r = slots // 4 * 4
        body(0, n0 + r, u0 + r, r, slots % 4)


def act_square_unit(k, act, norm, phase, u):
    act.wait_ge(*k.on("psum_free", 4 + PH[phase][1] + u + 1))
    for t in (2 * u, 2 * u + 1):
        if t >= 2:
            act.wait_ge(*k.on(norm + "_sum", t - 1))
        act.activation(k.work[:, t % 2], k.xT[:, t], ACT.Square).then_inc(k.sem(norm + "_sq"), 1)


def act_project(k, act, phase, norm):
    n0, _ = PH[phase]
    for j in range(4):
        act_slot(k, act, n0 + j, 0, 4)
        if j:
            act_square_unit(k, act, norm, phase, j - 1)
    act_square_unit(k, act, norm, phase, 3)


def act_down(k, act, phase, norm=None):
    n0, u0 = PH[phase]

    def body(i):
        for j in range(6):
            act_slot(k, act, n0 + j, i, 6)

    if norm:
        for j in range(12):
            act_slot(k, act, n0 + j, 0, 6)
            if j and j % 3 == 0:
                act_square_unit(k, act, norm, phase, j // 3 - 1)
        act_square_unit(k, act, norm, phase, 3)
    else:
        rounds(act, 2, body)


def pe_mean(k, pe, name, src, tiles, width, bank, inv, ready):
    for t in range(tiles):
        ready(t)
        pe.matmul(k.ps[:, bank, 0:width], inv[:], src(t), start=(t == 0), stop=(t == tiles - 1)) \
            .then_inc(k.sem(name), 1)


def act_squares(k, act, name, src, tiles, width, wbuf=0):
    for t in range(tiles):
        if t >= 2:
            act.wait_ge(*k.on(name + "_sum", t - 1))
        act.activation(k.work[:, wbuf + t % 2, 0:width], src(t), ACT.Square).then_inc(k.sem(name + "_sq"), 1)


def pe_squares(k, pe, name, tiles, width, bank, inv, wbuf=0):
    pe_mean(k, pe, name + "_sum", lambda t: k.work[:, wbuf + t % 2, 0:width], tiles, width, bank, inv,
            lambda t: pe.wait_ge(*k.on(name + "_sq", t + 1)))


def act_std(k, act, name, tiles, width, bank, eps=None):
    act.wait_ge(*k.on(name + "_sum", tiles))
    act.activation(k.std[:, 0:width], k.ps[:, bank, 0:width], ACT.Sqrt, bias=(eps or k.eps)[:, 0:1]) \
        .then_inc(k.sem(name + "_std"), 1)


def dve_rstd(k, dve, name, width):
    dve.wait_ge(*k.on(name + "_std", 1))
    dve.reciprocal(k.rstd[:, 0:width], k.std[:, 0:width]).then_inc(k.sem(name + "_rstd"), 1)
    dve.wait_ge(*k.on(name + "_rstd", 1))


def dve_scale_split(k, dve, name, src, scale, shift, low, high, tiles, width, func_after=False):
    def one(t):
        if t < tiles:
            if t >= 2:
                dve.wait_ge(*k.on(name + "_lo", t - 1))
            dve.scalar_tensor_tensor(k.work[:, 2 + t % 2, 0:width], src(t), scale(t), k.rstd[:, 0:width],
                                     ALU.mult, ALU.mult).then_inc(k.sem(name + "_t"), 1)
    one(0)
    for t in range(tiles):
        one(t + 1)
        dve.wait_ge(*k.on(name + "_hi", t + 1))
        w = k.work[:, 2 + t % 2, 0:width]
        if shift is None:
            dve.wait_ge(*k.on(name + "_t", t + 1))
            ins = dve.tensor_tensor(low(t), w, high(t).bitcast(F32), ALU.subtract)
        else:
            dve.wait_ge(*k.on(name + "_t", t + 1))
            ins = dve.scalar_tensor_tensor(low(t), w, shift(t), high(t).bitcast(F32), ALU.add, ALU.subtract)
        ins.then_inc(k.sem(name + "_lo"), 1)


def act_scale_split(k, act, name, shift, high, tiles, width, func=None):
    for t in range(tiles):
        act.wait_ge(*k.on(name + "_t", t + 1))
        w = k.work[:, 2 + t % 2, 0:width]
        if func is not None:
            act.activation(w, w, func, bias=shift(t)).then_inc(k.sem(name + "_f"), 1)
            act.wait_ge(*k.on(name + "_f", t + 1))
            act.activation(high(t), w, ACT.Copy).then_inc(k.sem(name + "_hi"), 1)
        elif shift is None:
            act.activation(high(t), w, ACT.Copy).then_inc(k.sem(name + "_hi"), 1)
        else:
            act.activation(high(t), w, ACT.Identity, bias=shift(t)).then_inc(k.sem(name + "_hi"), 1)


def slot_tile(i, base, j, e):
    return i * 8 + (2 * (base + j) + e)


def pick(t, j):
    if isinstance(j, int):
        return t[:, j]
    return t[:, bass.ds(j, 1)].rearrange("p a n -> p (a n)")


def pcol(k, name, j):
    at, _ = CT[name]
    if isinstance(j, int):
        return k.cols[:, at + j:at + j + 1]
    return k.cols[:, bass.ds(j + at, 1)]


def ml_scores_range(i):
    return i * P, S - i * P


SC_OFF = [0, 512, 896, 1152]


EARLY_ADA = 2
ADA_AFTER = {"scores": (0, 0, 0, 0), "sums": (2, 2, 2, 2), "var": (2, 2, 1, 1)}
ADA_BANKS = (0, 3)


def pe_mlstm(k, pe):
    pe_all_taken(k, pe, "ada2")
    slots = iter(range(16))

    def modulation(count):
        for _ in range(count):
            j = next(slots)
            if j >= 2:
                pe.wait_ge(*k.on("ada_read", j - 1))
            pe_ada_slot(k, pe, PH["ada2"][0] + j, ADA_BANKS[j % 2])

    modulation(EARLY_ADA)
    pe.wait_ge(*k.on("ml_g", 1))
    for i in range(4):
        mm = pe.transpose(k.ps[:, 4, 4 * i:4 * i + 4], k.rows[0:4, 0, i * P:(i + 1) * P],
                          k.col("ident", 0, 4)[0:4, :])
    mm.then_inc(k.sem("ml_gT"), 1)
    pe.wait_ge(*k.on("ml_rows", 1))
    pe.wait_ge(*k.on("sel_landed", 16))
    pe.wait_ge(*k.on("ml_gcol", 1))
    for h in range(ML_HEADS):
        if h:
            pe.wait_ge(*k.on("ml_std", h))
            pe.wait_ge(*k.on("ml_hc", h))
        pe.wait_ge(*k.on("ada_read", EARLY_ADA + sum(sum(v[:h]) for v in ADA_AFTER.values())))
        sel = k.sel[:, h]
        pe.matmul(k.ps[:, 1], sel, k.rows[0:4, 1], start=True, stop=True)
        pe.matmul(k.ps[:, 2], sel, k.rows[0:4, 2], start=True, stop=True).then_inc(k.sem("ml_bc"), 1)
        for i in range(4):
            t0, n = ml_scores_range(i)
            if 4 * h + i >= 2:
                pe.wait_ge(*k.on("ml_sc", 4 * h + i - 1))
            for c in range(2):
                mm = pe.matmul(k.ps[:, 3 + i % 2, 0:n], k.kT[:, 2 * h + c, t0:t0 + P],
                               k.qT[:, 2 * h + c, t0:S], start=(c == 0), stop=(c == 1))
            mm.then_inc(k.sem("ml_S"), 1)
        modulation(ADA_AFTER["scores"][h])
        for i in range(4):
            t0, n = ml_scores_range(i)
            pe.wait_ge(*k.on("ml_sc", 4 * h + i + 1))
            sc = k.scT[:, SC_OFF[i]:SC_OFF[i] + n]
            for e in range(2):
                pe.matmul(k.ps[:, 5 + e, t0:S], k.v[:, i, h * 256 + e * P:h * 256 + (e + 1) * P], sc,
                          start=(i == 0), stop=(i == 3))
            mm = pe.matmul(k.ps[:, 7, t0:S], k.one[:], sc, start=(i == 0), stop=(i == 3))
        mm.then_inc(k.sem("ml_num"), 1)
        pe_stay_warm(k, pe, 3, 2)
        modulation(ADA_AFTER["sums"][h])
        pe.wait_ge(*k.on("ml_h", 2 * (h + 1)))
        for e in range(2):
            mm = pe.matmul(k.ps[:, 1], k.inv_h[:], k.qT[:, 2 * h + e], start=(e == 0), stop=(e == 1))
        mm.then_inc(k.sem("ml_mean"), 1)
        for e in range(2):
            pe.wait_ge(*k.on("ml_sq", 2 * h + e + 1))
            mm = pe.matmul(k.ps[:, 2], k.inv_h[:], k.work[:, 2 + e], start=(e == 0), stop=(e == 1))
        mm.then_inc(k.sem("ml_var"), 1)
        modulation(ADA_AFTER["var"][h])
    pe.wait_ge(*k.on("conv", CONV_POOL))
    pe.wait_ge(*k.on("conv_pool", DT - CONV_POOL))
    pe_mean(k, pe, "cln_mean", lambda t: k.aT[:, t, 0:S], DT, S, 4, k.inv_d, lambda t: None)


def tensor_block1(k, pe):
    pe.wait_ge(*k.on("c_silu", 1))
    pe.wait_ge(*k.on("psum_free", 4))
    for j in range(8):
        if j == 7:
            pe.wait_ge(*k.on("ada1_read", 1))
        pe_ada_slot(k, pe, j, 1 + j % 7)
        if j == 1:
            pe.wait_ge(*k.on("consts", 1))
            pe_squares(k, pe, "n1", DT, S, 0, k.inv_d)
    h = (k.h_hi, k.h_lo)
    pe_linear(k, pe, "glu", h, ready="n1_lo")
    pe_linear(k, pe, "qk", h)
    pe_linear(k, pe, "if", h)
    pe_linear(k, pe, "v", h, width=256, natural=True)
    pe_mlstm(k, pe)
    pe_all_taken(k, pe, "pw")
    pe.wait_ge(*k.on("ml_out", 2 * ML_HEADS))
    pe_squares(k, pe, "cln", DT, S, 1, k.inv_d)
    pe_linear(k, pe, "pw", (k.cs_hi, k.cs_lo), ready="cln_lo")
    pe_linear(k, pe, "o", h)
    pe_linear(k, pe, "merge", h)
    pe_project(k, pe, "w_out", (k.cs_hi, k.cs_lo), "nfa", ready="y_lo")
    pe_ffn(k, pe, "a")


NORM_AFTER = {"a": "fin1", "b": None, "c": "fin2"}
PROJECT_BEFORE = {"a": "w_out", "b": "wo0", "c": "wo1"}


def pe_ffn(k, pe, name):
    n = "nf" + name
    pe_all_taken(k, pe, "up_" + name)
    pe_linear(k, pe, "up_" + name, (k.h_hi, k.h_lo), ready=n + "_lo")
    pe_down(k, pe, "down_" + name, (k.hid_hi, k.hid_lo), "hid_lo_" + name, NORM_AFTER[name])


def act_mlstm_gates_log(k, act):
    act.wait_ge(*k.on("ml_neg", 1))
    act.activation(k.rows[0:4, 3], k.rows[0:4, 3], ACT.Exp).then_inc(k.sem("ml_exp"), 1)
    act.wait_ge(*k.on("ml_exp", 1))
    act.activation(k.rows[0:4, 3], k.rows[0:4, 3], ACT.Ln, bias=1.0).then_inc(k.sem("ml_ln"), 1)


def act_mlstm_gates_exp(k, act):
    act.wait_ge(*k.on("ml_fm", 1))
    act.activation(k.rows[0:4, 2], k.rows[0:4, 2], ACT.Exp).then_inc(k.sem("ml_rows"), 1)


def act_mlstm_heads(k, act):
    for h in range(ML_HEADS):
        act.wait_ge(*k.on("ml_nm", h + 1))
        for i in range(4):
            _, n = ml_scores_range(i)
            if i >= 2:
                act.wait_ge(*k.on("ml_sc", 4 * h + i - 1))
            g = k.gcol[:, 4 * i + h:4 * i + h + 1]
            act.activation(k.work[:, 2 + i % 2, 0:P], k.work[:, 1, i * P:(i + 1) * P], ACT.Exp, bias=g) \
                .then_inc(k.sem("ml_D"), 1)
            if i < 3:
                act.activation(k.work[:, 2 + i % 2, P:n], k.work[:, 0, (i + 1) * P:S], ACT.Exp, bias=g) \
                    .then_inc(k.sem("ml_D"), 1)
        for e in range(2):
            act.wait_ge(*k.on("ml_hc", 2 * h + e + 1))
            act.activation(k.work[:, 2 + e], k.qT[:, 2 * h + e], ACT.Square).then_inc(k.sem("ml_sq"), 1)
        act.wait_ge(*k.on("ml_var", h + 1))
        act.activation(k.std[:], k.ps[:, 2], ACT.Sqrt, bias=k.eps[:, 0:1]).then_inc(k.sem("ml_std"), 1)


def scalar_block1(k, act):
    act.wait_ge(*k.on("cols_landed", 16))
    act.activation(k.cb[:], k.col("c", 0, 8).unsqueeze(2).broadcast_to([P, 8, P]), ACT.Silu) \
        .then_inc(k.sem("c_silu"), 1)
    act.wait_ge(*k.on("x_landed", 16))
    act.wait_ge(*k.on("consts", 1))
    act_squares(k, act, "n1", lambda t: k.xT[:, t], DT, S)
    act_std(k, act, "n1", DT, S, 0)
    act_scale_split(k, act, "n1", lambda t: k.mod[:, t:t + 1], lambda t: k.h_hi[:, t], DT, S)
    for par in range(2):
        act_high(k, act, par, 16 * (PH["glu"][0] // 2 + 1))

    def glu(i, base, j, bank):
        if j % 2:
            act.wait_ge(*k.on("psum_free", i * 4 + (4 + PH["glu"][1] + j - 1)))
            for e in range(2):
                g = i * 4 + (8 + (j // 2) * 2 + e)
                act.activation(k.work[:, e], k.ps[:, bank + e], ACT.Sigmoid, bias=pcol(k, "b_glu", g)) \
                    .then_inc(k.sem("glu_sig"), 1)

    act_linear(k, act, "glu", glu)

    def qk(i, base, j, bank):
        for e in range(2):
            t = slot_tile(i, base, j, e)
            act.activation(k.qpre[:, e, 3:3 + S], k.ps[:, bank + e], ACT.Identity, bias=pcol(k, "b_qk", t)) \
                .then_inc(k.sem("qk_pre"), 1)
        for e in range(2):
            t = slot_tile(i, base, j, e)
            act.wait_ge(*k.on("qk_conv", i * 8 + (2 * j + e + 1)))
            act.activation(pick(k.qkT, t), k.work[:, e], ACT.Silu).then_inc(k.sem("qk_done"), 1)

    act_linear(k, act, "qk", qk)
    act_linear(k, act, "if")
    act_mlstm_gates_log(k, act)
    act_linear(k, act, "v")
    act_mlstm_gates_exp(k, act)
    act_mlstm_heads(k, act)
    n = PH["pw"][0]
    for j in range(2):
        act_high(k, act, (n + j) % 2, 16 * ((n + j) // 2 + 1))
    for t in range(DT):
        act.wait_ge(*k.on("cln_c", t + 1))
        if t >= 2:
            act.wait_ge(*k.on("cln_sum", t - 1))
        act.activation(k.work[:, t % 2], k.aT[:, t, 0:S], ACT.Square).then_inc(k.sem("cln_sq"), 1)
    act_std(k, act, "cln", DT, S, 1)
    act_scale_split(k, act, "cln", lambda t: pcol(k, "ln_b", t), lambda t: k.cs_hi[:, t], DT, S, func=ACT.Silu)
    act_linear(k, act, "pw")

    def gate(name, phase):
        def evac(i, base, j, bank):
            for e in range(2):
                act.wait_ge(*k.on("psum_free", i * 4 + (4 + PH[phase][1] + base + j)))
                act.activation(k.work[:, e], k.ps[:, bank + e], ACT.Sigmoid,
                               bias=pcol(k, name, slot_tile(i, base, j, e))).then_inc(k.sem("sig_" + phase), 1)
        return evac

    act_linear(k, act, "o", gate("b_o", "o"))
    act_linear(k, act, "merge", gate("b_merge", "merge"))
    act_split(k, act, "y", lambda t: k.qT[:, t], lambda t: k.cs_hi[:, t], DT, ("psum_free", 4 + PH["w_out"][1]))
    act_project(k, act, "w_out", "nfa")
    act_ffn(k, act, "a", lambda t: k.mod[:, 24 + t:25 + t])


def act_split(k, act, name, src, high, tiles, ready):
    act.wait_ge(*k.on(ready[0], ready[1]))
    for t in range(tiles):
        act.activation(high(t), src(t), ACT.Copy).then_inc(k.sem(name + "_hi"), 1)


def dve_split(k, dve, name, src, high, low, tiles):
    for t in range(tiles):
        dve.wait_ge(*k.on(name + "_hi", t + 1))
        dve.tensor_tensor(low(t), src(t), high(t).bitcast(F32), ALU.subtract).then_inc(k.sem(name + "_lo"), 1)


def act_ffn(k, act, name, shift):
    n = "nf" + name
    u0 = PH["up_" + name][1]
    act_std(k, act, n, DT, S, bank_pair(PH[PROJECT_BEFORE[name]][1]))
    act_scale_split(k, act, n, shift, lambda t: k.h_hi[:, t], DT, S)

    def evac(i, base, j, bank):
        if j % 2 == 0:
            for e in range(2):
                if e == 0:
                    act.wait_ge(*k.on("psum_free", i * 4 + (4 + u0 + base + j)))
                act.activation(k.work[:, e], k.ps[:, bank + e], ACT.Silu).then_inc(k.sem("silu_" + name), 1)
        else:
            act.wait_ge(*k.on("psum_free", i * 4 + (4 + u0 + base + j + 1)))
            for e in range(2):
                t = i * 4 + (base + j - 1 + e)
                act.activation(pick(k.hid_hi, t), k.work[:, 2 + e], ACT.Copy).then_inc(k.sem("hid_hi_" + name), 1)

    act_linear(k, act, "up_" + name, evac)
    act_down(k, act, "down_" + name, NORM_AFTER[name])


def dve_linear(k, dve, phase, evac, slots=None, first=0, chain=None, per=0):
    n0, u0 = PH[phase]
    n0, u0 = n0 + first, u0 + first
    slots = slots or dict((p, s) for p, s, _ in PHASES_LIST)[phase]

    def body(i, base, count):
        for j in range(count):
            dve.wait_ge(*k.on("mm_done", i * 8 + 2 * (n0 + base + j + 1)))
            evac(i, base, j, bank_pair(u0 + base + j))

    if slots // 4:
        if chain:
            chained_rounds(chain, slots // 4, per, lambda i: body(i, 0, 4))
        else:
            rounds(dve, slots // 4, lambda i: body(i, 0, 4))
    if slots % 4:
        body(0, slots // 4 * 4, slots % 4)


def dve_ada_slot(k, dve, ch, n, tile, bank, read, before):
    dve.wait_ge(*k.on("w_low", n + 1))
    if before:
        dve.wait_ge(*k.on(read, before))
    for e in range(2):
        c = e * P
        ins = dve.tensor_tensor_reduce(out=k.diag[:], in0=k.ps[:, bank, c:c + P], in1=k.col("ident", 0, P),
                                       scale=1.0, scalar=0.0, op0=ALU.mult, op1=ALU.add,
                                       accum_out=k.mod[:, tile + e:tile + e + 1])
        if e == 0:
            ch.link(ins)
        else:
            ins.then_inc(k.sem(read), 1)


CONV_EARLY = 3


class LongConvolution:

    def __init__(self, k, dve, ch):
        self.k, self.dve, self.ch, self.at = k, dve, ch, 0
        self.taps = [(t, m) for t in range(CONV_POOL) for m in range(TAPS)
                     if t < CONV_POOL - 1 or m >= CONV_SHARED]

    def some(self, count):
        k, dve = self.k, self.dve
        for t, m in self.taps[self.at:self.at + count]:
            self.at += 1
            src, w = k.aT[:, t, m:m + S], k.col("conv_w", t * TAPS + m)
            acc = k.work[:, 2] if t < CONV_EARLY else k.conv_late[:]
            if m == 0:
                if t:
                    dve.wait_ge(*k.on("conv", t))
                self.ch.link(dve.tensor_scalar(acc, src, w, k.col("conv_b", t), ALU.mult, ALU.add))
            elif m < TAPS - 1:
                so_far = acc
                if (t, m) == (CONV_POOL - 1, CONV_SHARED):
                    dve.wait_ge(*k.on("conv_shared", 1))
                    dve.wait_ge(*k.on("conv", t))
                    so_far = k.pool_acc[:]
                self.ch.link(dve.scalar_tensor_tensor(acc, src, w, so_far, ALU.mult, ALU.add))
            else:
                dve.scalar_tensor_tensor(k.aT[:, t, 0:S], src, w, acc, ALU.mult, ALU.add) \
                    .then_inc(k.sem("conv"), 1)


class Modulation:

    def __init__(self, k, dve, ch):
        self.k, self.dve, self.ch, self.at = k, dve, ch, 0

    def some(self, count):
        for _ in range(count):
            j = self.at
            dve_ada_slot(self.k, self.dve, self.ch, PH["ada2"][0] + j, 16 + 2 * j, ADA_BANKS[j % 2],
                         "ada_read", j)
            self.at += 1


def dve_mlstm_gates(k, dve, ch):
    R = lambda j: k.rows[0:4, j]
    bank = bank_pair(PH["if"][1])
    n = PH["if"][0]
    dve.wait_ge(*k.on("mm_done", 2 * (n + 1)))
    ch.link(dve.tensor_scalar(R(0), k.ps[0:4, bank], k.col("b_i")[0:4, :], None, ALU.add))
    ch.link(dve.tensor_scalar(R(1), k.ps[0:4, bank + 1], k.col("b_f")[0:4, :], None, ALU.add))
    dve.memset(R(4), 0.0).then_inc(k.sem("psum_free"), 1)
    dve.wait_ge(*k.on("psum_free", 4 + PH["if"][1] + 1))
    dve.scalar_tensor_tensor(R(3), R(1), -1.0, R(1), ALU.mult, ALU.min).then_inc(k.sem("ml_neg"), 1)
    dve.wait_ge(*k.on("ml_ln", 1))
    ch.link(dve.scalar_tensor_tensor(R(3), R(1), 0.0, R(3), ALU.min, ALU.subtract))
    ch.link(dve.tensor_tensor_scan(R(1), R(4), R(3), 0.0, ALU.add, ALU.add))
    dve.tensor_tensor(R(0), R(0), R(1), ALU.subtract).then_inc(k.sem("ml_g"), 1)
    dve.wait_ge(*k.on("ml_g", 1))
    ch.link(dve.tensor_tensor_scan(R(3), R(0), R(4), 0.0, ALU.max, ALU.add))
    ch.link(dve.scalar_tensor_tensor(R(2), R(1), -1.0, R(3), ALU.mult, ALU.subtract))
    dve.tensor_scalar(R(1), R(3), -1.0, None, ALU.mult).then_inc(k.sem("ml_fm"), 1)
    dve.wait_ge(*k.on("ml_fm", 1))


def dve_mlstm_heads(k, dve, ch, conv, mod):
    dve.wait_ge(*k.on("ml_gT", 1))
    dve.tensor_copy(k.gcol[:], k.ps[:, 4, 0:16]).then_inc(k.sem("ml_gcol"), 1)
    for h in range(ML_HEADS):
        dve.wait_ge(*k.on("ml_bc", h + 1))
        ch.link(dve.tensor_copy(k.work[:, 0], k.ps[:, 1]))
        for i in range(4):
            ins = dve.tensor_tensor(k.work[:, 1, i * P:(i + 1) * P], k.work[:, 0, i * P:(i + 1) * P],
                                    k.col("after", 0, P), ALU.add)
            if i < 3:
                ch.link(ins)
        ins.then_inc(k.sem("ml_nm"), 1)
        nd = 0
        for i in range(4):
            t0, n = ml_scores_range(i)
            nd += 2 if i < 3 else 1
            dve.wait_ge(*k.on("ml_S", 4 * h + i + 1))
            dve.wait_ge(*k.on("ml_D", 7 * h + nd))
            dve.scalar_tensor_tensor(k.scT[:, SC_OFF[i]:SC_OFF[i] + n], k.ps[:, 3 + i % 2, 0:n], 1.0 / 16,
                                     k.work[:, 2 + i % 2, 0:n], ALU.mult, ALU.mult).then_inc(k.sem("ml_sc"), 1)
        ch.link(dve.tensor_copy(k.work[:, 0], k.ps[:, 2]))
        conv.some(9)
        dve.wait_ge(*k.on("ml_num", h + 1))
        ch.link(dve.tensor_tensor(k.work[:, 0], k.ps[:, 7], k.work[:, 0], ALU.max))
        ch.link(dve.scalar_tensor_tensor(k.work[:, 1], k.ps[:, 7], -1.0, k.work[:, 0], ALU.mult, ALU.max))
        ch.link(dve.reciprocal(k.work[:, 1], k.work[:, 1]))
        for e in range(2):
            dve.tensor_tensor(k.qT[:, 2 * h + e], k.ps[:, 5 + e], k.work[:, 1], ALU.mult) \
                .then_inc(k.sem("ml_h"), 1)
        mod.some(ADA_AFTER["sums"][h])
        conv.some(4)
        dve.wait_ge(*k.on("ml_mean", h + 1))
        for e in range(2):
            dve.wait_ge(*k.on("ml_h", 2 * h + e + 1))
            dve.tensor_tensor(k.qT[:, 2 * h + e], k.qT[:, 2 * h + e], k.ps[:, 1], ALU.subtract) \
                .then_inc(k.sem("ml_hc"), 1)
        conv.some(6)
        dve.wait_ge(*k.on("ml_std", h + 1))
        ch.link(dve.reciprocal(k.rstd[:], k.std[:]))
        for e in range(2):
            t = 2 * h + e
            dve.scalar_tensor_tensor(k.qT[:, t], k.qT[:, t], pcol(k, "mlstm_g", t), k.rstd[:],
                                     ALU.mult, ALU.mult).then_inc(k.sem("ml_out"), 1)
        mod.some(ADA_AFTER["var"][h])
        conv.some(6)


def vector_block1(k, dve, ch):
    for ap, value in ((k.inv_d, 1.0 / D), (k.inv_h, 1.0 / 256), (k.one, 1.0), (k.eps, EPS)):
        ch.link(dve.memset(ap[:], value))
    ch.link(dve.memset(k.aT[:, :, 0:TAPS - 1], 0.0))
    dve.memset(k.qpre[:, :, 0:QK_TAPS - 1], 0.0).then_inc(k.sem("consts"), 1)
    dve.memset(k.mod[:], 0.0).then_inc(k.sem("psum_free"), 4)
    dve.wait_ge(*k.on("psum_free", 4))
    dve.wait_ge(*k.on("cols_landed", 16))
    dve_rstd(k, dve, "n1", S)
    for j in range(8):
        dve_ada_slot(k, dve, ch, j, 2 * j, 1 + j % 7, "ada1_read", j)
    dve.wait_ge(*k.on("ada1_read", 8))
    dve.tensor_tensor(k.mod[:, 0:16], k.mod[:, 0:16], k.col("b_ada", 0, 16), ALU.add) \
        .then_inc(k.sem("psum_free"), 8)
    dve.wait_ge(*k.on("psum_free", 4 + PH["glu"][1]))
    ch.link(dve.scalar_tensor_tensor(k.A[:], k.mod[:, 8:16], 1.0, k.col("norm_mix_g", 0, 8), ALU.add, ALU.mult))
    dve_scale_split(k, dve, "n1", lambda t: k.xT[:, t], lambda t: k.A[:, t:t + 1],
                    lambda t: k.mod[:, t:t + 1], lambda t: k.h_lo[:, t], lambda t: k.h_hi[:, t], DT, S)

    def glu(i, base, j, bank):
        if j % 2:
            for e in range(2):
                t = i * 4 + ((j // 2) * 2 + e)
                dve.wait_ge(*k.on("glu_sig", i * 4 + ((j // 2) * 2 + e + 1)))
                u = PH["glu"][1] + j - 1
                if isinstance(t, int):
                    out = k.aT[:, t, TAPS - 1:TAPS - 1 + S]
                else:
                    out = k.aT[:, bass.ds(t, 1), TAPS - 1:TAPS - 1 + S].rearrange("p a n -> p (a n)")
                ins = dve.scalar_tensor_tensor(out, k.ps[:, bank_pair(u) + e], pcol(k, "b_glu", t),
                                               k.work[:, e], ALU.add, ALU.mult)
                if e:
                    ins.then_inc(k.sem("psum_free"), 2)

    dve_linear(k, dve, "glu", glu)
    dve.wait_ge(*k.on("psum_free", 4 + PH["qk"][1]))

    conv = LongConvolution(k, dve, ch)

    def qk(i, base, j, bank):
        for e in range(2):
            t = slot_tile(i, base, j, e)
            dve.wait_ge(*k.on("qk_pre", i * 8 + (2 * j + e + 1)))
            out = k.work[:, e]
            for m in range(QK_TAPS):
                src, w = k.qpre[:, e, m:m + S], pcol(k, "qk_w", t * QK_TAPS + m)
                if m == 0:
                    ins = dve.tensor_scalar(out, src, w, pcol(k, "qk_b", t), ALU.mult, ALU.add)
                else:
                    ins = dve.scalar_tensor_tensor(out, src, w, out, ALU.mult, ALU.add)
                if m < QK_TAPS - 1:
                    ch.link(ins)
            ins.then_inc(k.sem("qk_conv"), 1)
        dve.memset(k.zero[:], 0.0).then_inc(k.sem("psum_free"), 1)

    n0, u0 = PH["qk"]
    for j in range(8):
        dve.wait_ge(*k.on("mm_done", 2 * (n0 + j + 1)))
        qk(0, 0, j, bank_pair(u0 + j))
        conv.some(8)

    dve.wait_ge(*k.on("row_bv_landed", 16))

    def v(i, base, j, bank):
        for e in range(2):
            c = (base + j) * 256
            ins = dve.tensor_tensor(k.v[:, 2 * e:2 * e + 2, c:c + 256],
                                    k.ps[:, bank + e].rearrange("p (t c) -> p t c", t=2),
                                    k.row_bv2[:, :, c:c + 256], ALU.add)
        ins.then_inc(k.sem("psum_free"), 1)
        conv.some(10)

    dve_mlstm_gates(k, dve, ch)
    dve_linear(k, dve, "v", v)
    mod = Modulation(k, dve, ch)
    mod.some(EARLY_ADA)
    assert conv.at >= TAPS * CONV_EARLY
    dve_mlstm_heads(k, dve, ch, conv, mod)
    assert conv.at == len(conv.taps)
    assert mod.at == 16
    dve.wait_ge(*k.on("ada_read", 16))
    dve.tensor_tensor(k.mod[:, 16:48], k.mod[:, 16:48], k.col("b_ada", 16, 32), ALU.add) \
        .then_inc(k.sem("psum_free"), 16)
    dve.wait_ge(*k.on("cln_mean", DT))
    for t in range(DT):
        dve.tensor_tensor(k.aT[:, t, 0:S], k.aT[:, t, 0:S], k.ps[:, 4], ALU.subtract).then_inc(k.sem("cln_c"), 1)
    dve_rstd(k, dve, "cln", S)
    dve_scale_split(k, dve, "cln", lambda t: k.aT[:, t, 0:S], lambda t: pcol(k, "ln_g", t), None,
                    lambda t: k.cs_lo[:, t], lambda t: k.cs_hi[:, t], DT, S)

    def pw(i, base, j, bank):
        for e in range(2):
            t = 2 * (base + j) + e
            ins = dve.tensor_scalar(k.aT[:, t, 0:S], k.ps[:, bank + e], pcol(k, "b_pw", t), None, ALU.add)
            if e == 0:
                ch.link(ins)
        ins.then_inc(k.sem("psum_free"), 1)

    dve_linear(k, dve, "pw", pw)
    dve.wait_ge(*k.on("psum_free", 4 + PH["o"][1]))
    dve.wait_ge(*k.on("ml_out", 2 * ML_HEADS))

    def o(i, base, j, bank):
        for e in range(2):
            t = 2 * (base + j) + e
            dve.wait_ge(*k.on("sig_o", t + 1))
            ins = dve.tensor_tensor(k.qT[:, t], k.qT[:, t], k.work[:, e], ALU.mult)
            if e == 0:
                ch.link(ins)
        ins.then_inc(k.sem("psum_free"), 1)

    dve_linear(k, dve, "o", o)
    dve.wait_ge(*k.on("psum_free", 4 + PH["merge"][1]))

    def merge(i, base, j, bank):
        for e in range(2):
            t = 2 * j + e
            dve.wait_ge(*k.on("sig_merge", 2 * (base + j) + e + 1))
            if base == 0:
                ins = dve.tensor_tensor(k.aT[:, t, 0:S], k.aT[:, t, 0:S], k.work[:, e], ALU.mult)
            else:
                ch.link(dve.tensor_tensor(k.qT[:, t], k.qT[:, t], k.work[:, e], ALU.mult))
                ins = dve.tensor_tensor(k.qT[:, t], k.qT[:, t], k.aT[:, t, 0:S], ALU.add)
            if e == 0:
                ch.link(ins)
        ins.then_inc(k.sem("psum_free"), 1)
        dve.wait_ge(*k.on("psum_free", 4 + PH["merge"][1] + base + j + 1))

    n0, u0 = PH["merge"]
    for s in range(8):
        dve.wait_ge(*k.on("mm_done", 2 * (n0 + s + 1)))
        merge(0, s // 4 * 4, s % 4, bank_pair(u0 + s))
    dve_split(k, dve, "y", lambda t: k.qT[:, t], lambda t: k.cs_hi[:, t], lambda t: k.cs_lo[:, t], DT)
    dve_residual(k, dve, ch, "w_out", lambda t: k.mod[:, 16 + t:17 + t])
    ch.link(dve.scalar_tensor_tensor(k.A[:], k.mod[:, 32:40], 1.0, k.col("ffn_g", 0, 8), ALU.add, ALU.mult))
    dve_ffn(k, dve, ch, "a", lambda t: k.A[:, t:t + 1], lambda t: k.mod[:, 24 + t:25 + t],
            lambda t: k.mod[:, 40 + t:41 + t])


def dve_residual(k, dve, ch, phase, gain):
    def evac(i, base, j, bank):
        for e in range(2):
            t = 2 * (base + j) + e
            if gain is None:
                ins = dve.tensor_tensor(k.xT[:, t], k.ps[:, bank + e], k.xT[:, t], ALU.add)
            else:
                ins = dve.scalar_tensor_tensor(k.xT[:, t], k.ps[:, bank + e], gain(t), k.xT[:, t],
                                               ALU.mult, ALU.add)
            if e == 0:
                ch.link(ins)
        ins.then_inc(k.sem("psum_free"), 1)
    dve_linear(k, dve, phase, evac)
    dve.wait_ge(*k.on("psum_free", 4 + PH[phase][1] + 4))


def dve_ffn(k, dve, ch, name, scale, shift, gain):
    n = "nf" + name
    n0, u0 = PH["up_" + name]
    dve_rstd(k, dve, n, S)
    dve_scale_split(k, dve, n, lambda t: k.xT[:, t], scale, shift, lambda t: k.h_lo[:, t],
                    lambda t: k.h_hi[:, t], DT, S)

    def evac(i, base, j, bank):
        if j % 2 == 0:
            return
        for e in range(2):
            dve.wait_ge(*k.on("silu_" + name, i * 4 + (base + j - 1 + e + 1)))
            ins = dve.tensor_tensor(k.work[:, 2 + e], k.work[:, e], k.ps[:, bank + e], ALU.mult)
            if e == 0:
                ch.link(ins)
        ins.then_inc(k.sem("psum_free"), 2)
        dve.wait_ge(*k.on("psum_free", i * 4 + (4 + u0 + base + j + 1)))
        for e in range(2):
            t = i * 4 + (base + j - 1 + e)
            dve.wait_ge(*k.on("hid_hi_" + name, i * 4 + (base + j - 1 + e + 1)))
            dve.tensor_tensor(pick(k.hid_lo, t), k.work[:, 2 + e], pick(k.hid_hi, t).bitcast(F32),
                              ALU.subtract).then_inc(k.sem("hid_lo_" + name), 1)
        dve.wait_ge(*k.on("hid_lo_" + name, i * 4 + (base + j + 1)))

    dve_linear(k, dve, "up_" + name, evac, chain=ch, per=2)
    n0, u0 = PH["down_" + name]
    for u in range(4):
        dve.wait_ge(*k.on("mm_done", 2 * (n0 + 3 * (u + 1))))
        for e in range(2):
            t = 2 * u + e
            src = k.ps[:, 2 * (u % 2) + e]
            if gain is None:
                ins = dve.tensor_tensor(k.xT[:, t], src, k.xT[:, t], ALU.add)
            else:
                ins = dve.scalar_tensor_tensor(k.xT[:, t], src, gain(t), k.xT[:, t], ALU.mult, ALU.add)
            if e == 0:
                ch.link(ins)
        ins.then_inc(k.sem("psum_free"), 1)
    dve.wait_ge(*k.on("psum_free", 4 + u0 + 4))


def dve_norm_in_place(k, dve, name, scale, dst=None):
    dve_rstd(k, dve, name, S)
    dst = dst or (lambda t: k.xT[:, t])
    for t in range(DT):
        ins = dve.scalar_tensor_tensor(dst(t), k.xT[:, t], scale(t), k.rstd[:], ALU.mult, ALU.mult)
        ins.then_inc(k.sem(name + "_x"), 1)
    dve.wait_ge(*k.on(name + "_x", DT))


def act_memory(k, act, i, before=None):
    s = str(i)
    act.wait_ge(*k.on("psum_free", 4 + PH["memkv" + s][1]))
    act.dma_start(k.memT[:], k.mem_dram).then_inc(k.sem("mem_landed"), 16)
    act.wait_ge(*k.on("mem_landed", 16 * (i + 1)))
    act_squares(k, act, "mem" + s, lambda t: k.memT[:, t], DT, N_MEM)
    if before:
        act.wait_ge(*k.on(before, DT))
    act_std(k, act, "mem" + s, DT, N_MEM, 0)
    act_scale_split(k, act, "mem" + s, None, lambda t: k.m_hi[:, t], DT, N_MEM)
    act_linear(k, act, "memkv" + s)


def pe_memory(k, pe, i):
    s = str(i)
    pe_all_taken(k, pe, "memkv" + s)
    pe_squares(k, pe, "mem" + s, DT, N_MEM, 0, k.inv_d)
    n0, u0 = PH["memkv" + s]
    m = (k.m_hi, k.m_lo)
    pe.wait_ge(*k.on("psum_free", u0 + 1))
    pe_slot(k, pe, n0, 0, 0, 4, m, width=N_MEM, banks=bank_pair(u0), ready="mem" + s + "_lo")
    pe.wait_ge(*k.on("psum_free", u0 + 2))
    par = (n0 + 1) % 2
    pe.wait_ge(*k.on("w_low", n0 + 2))
    for e in range(2):
        for kt in range(DT):
            for a, (x, w) in enumerate(((k.m_hi, k.w_hi[par]), (k.m_hi, k.w_lo[par]), (k.m_lo, k.w_hi[par]))):
                mm = pe.matmul(k.ps[:, bank_pair(u0 + 1) + e, 0:256], x[:, kt, e * P:(e + 1) * P],
                               w[:, kt, :], start=(kt == 0 and a == 0), stop=(kt == DT - 1 and a == 2))
        mm.then_inc(k.sem("mm_done"), 1)


def dve_memory(k, dve, i):
    s = str(i)
    dve_rstd(k, dve, "mem" + s, N_MEM)
    dve_scale_split(k, dve, "mem" + s, lambda t: k.memT[:, t], lambda t: pcol(k, "norm_mem", 8 * i + t), None,
                    lambda t: k.m_lo[:, t], lambda t: k.m_hi[:, t], DT, N_MEM)
    n0, u0 = PH["memkv" + s]
    for j, dst in enumerate((k.mkT, k.mv)):
        dve.wait_ge(*k.on("mm_done", 2 * (n0 + j + 1)))
        b = bank_pair(u0 + j)
        dve.tensor_copy(dst[:], k.ps[:, b:b + 2, 0:N_MEM]).then_inc(k.sem("psum_free"), 1)


def alibi_slopes():
    eight = [2.0 ** -(i + 1) for i in range(8)]
    more = [2.0 ** (-0.5 * (i + 1)) for i in range(16)][0::2][:HEADS - 8]
    return [float(np.float32(v)) for v in eight + more]


TURN_LAG, VALUE_LAG = 2, 4


def attention_tiles(which):
    tiles, groups = [], []
    for i in range(4):
        for kind in which:
            for h0, n in ((0, 4),) if kind == "mem" else ((0, 6), (6, 6)):
                tiles += [(kind, i, h0 + h, len(groups)) for h in range(n)]
                groups.append((kind, i, h0, n, len(tiles)))
    return tiles, groups


def attention_keys(k, kind, i, h):
    half = slice((h % 2) * DH, (h % 2) * DH + DH)
    if kind == "mem":
        q = k.mq[half, h // 2, i * P:(i + 1) * P]
        return q, k.mkT[half, h // 2, :], N_MEM, [(P, k.mv[:, j, h * DH:(h + 1) * DH]) for j in range(2)]
    g = h // 3
    q = k.nq[half, h // 2, i * P:(i + 1) * P]
    if kind == "cmp":
        return q, k.kcb[half, g * N_CMP:(g + 1) * N_CMP], N_CMP, [(N_CMP, k.vcb[:, g, :])]
    keys, values = (k.kds, k.vs) if kind == "sel" else (k.kdw, k.vw)
    return q, keys[half, g, 0:(i + 1) * P], (i + 1) * P, \
        [(P, values[:, j, g * DH:(g + 1) * DH]) for j in range(i + 1)]


def pe_attention(k, pe, which, s):
    tiles, groups = attention_tiles(which)
    n = len(tiles)
    pe_stay_warm(k, pe, 7, 8)
    for step in range(n + VALUE_LAG):
        if step < n:
            kind, i, h, g = tiles[step]
            q, keys, width, _ = attention_keys(k, kind, i, h)
            if step >= 3:
                pe.wait_ge(*k.on("at_neg" + s, step - 2))
            pe.matmul(k.ps[:, step % 3, 0:width], q, keys, start=True, stop=True) \
                .then_inc(k.sem("at_scores" + s), 1)
        t = step - TURN_LAG
        if 0 <= t < n:
            kind, i, h, g = tiles[t]
            _, _, width, _ = attention_keys(k, kind, i, h)
            pe.wait_ge(*k.on("at_exp" + s, t + 1))
            if kind == "cmp":
                pe.wait_ge(*k.on("at_seen" + s, sum(x[0] == "cmp" for x in tiles[:t + 1])))
            if t >= 2:
                pe.wait_ge(*k.on("at_pT" + s, t - 1))
            for j in range(-(-width // P)):
                w = min(P, width - j * P)
                mm = pe.transpose(k.ps[0:w, 3 + t % 2, j * P:(j + 1) * P], k.ap[:, t % 4, j * P:j * P + w],
                                  k.col("ident", 0, P))
            mm.then_inc(k.sem("at_turned" + s), 1)
        t = step - VALUE_LAG
        if t >= 0:
            kind, i, h, g = tiles[t]
            _, _, width, values = attention_keys(k, kind, i, h)
            c = (h - groups[g][2]) * DH
            if c == 0 and g >= 3:
                pe.wait_ge(*k.on("at_group" + s, g - 2))
            pe.wait_ge(*k.on("at_pT" + s, t + 1))
            for j, (rows, v) in enumerate(values):
                mm = pe.matmul(k.ps[:, 5 + g % 3, c:c + DH], k.apT[0:rows, t % 3, j * P:(j + 1) * P], v,
                               start=(j == 0), stop=(j == len(values) - 1))
            mm.then_inc(k.sem("at_out" + s), 1)


def act_attention(k, act, which, s):
    tiles, groups = attention_tiles(which)
    for t, (kind, i, h, g) in enumerate(tiles):
        _, _, width, _ = attention_keys(k, kind, i, h)
        c = h - groups[g][2]
        act.wait_ge(*k.on("at_neg" + s, t + 1))
        if c == 0 and g >= 3:
            act.wait_ge(*k.on("at_group" + s, g - 2))
        p = k.ap[:, t % 4, 0:width]
        act.activation(p, p, ACT.Exp, scale=-1.0, bias=k.amax[:, t % 4:t % 4 + 1],
                       accum_out=k.asum[:, g % 3, c:c + 1]).then_inc(k.sem("at_exp" + s), 1)


def dve_attention(k, dve, ch, which, s):
    tiles, groups = attention_tiles(which)
    n = len(tiles)
    for step in range(n + VALUE_LAG + 1):
        t = step - TURN_LAG
        if 0 <= t < n and tiles[t][0] == "cmp":
            i = tiles[t][1]
            dve.wait_ge(*k.on("at_exp" + s, t + 1))
            p = k.ap[:, t % 4, 0:N_CMP]
            dve.tensor_tensor(p, p, k.col("seen_c", i * N_CMP, N_CMP), ALU.mult) \
                .then_inc(k.sem("at_seen" + s), 1)
        if step < n:
            kind, i, h, g = tiles[step]
            _, _, width, _ = attention_keys(k, kind, i, h)
            if kind == "mem":
                table = k.azero[:, 0:width]
            elif kind == "cmp":
                table = k.table_c[:, h, i * N_CMP:(i + 1) * N_CMP]
            else:
                table = k.table[:, h, S - P - i * P:S]
            dve.wait_ge(*k.on("at_scores" + s, step + 1))
            if step >= 4:
                dve.wait_ge(*k.on("at_turned" + s, step - 3))
            dve.tensor_tensor_reduce(out=k.ap[:, step % 4, 0:width], in0=k.ps[:, step % 3, 0:width],
                                     in1=table, scale=-1.0, scalar=3.0e38, op0=ALU.add, op1=ALU.min,
                                     accum_out=k.amax[:, step % 4:step % 4 + 1]) \
                .then_inc(k.sem("at_neg" + s), 1)
        if 0 <= t < n:
            _, _, width, _ = attention_keys(k, *tiles[t][0:3])
            rows = min(width, P)
            cols = max(width, P)
            dve.wait_ge(*k.on("at_turned" + s, t + 1))
            if t >= 3:
                dve.wait_ge(*k.on("at_out" + s, t - 2))
            dve.tensor_copy(k.apT[0:rows, t % 3, 0:cols], k.ps[0:rows, 3 + t % 2, 0:cols]) \
                .then_inc(k.sem("at_pT" + s), 1)
        for g, group in enumerate(groups):
            if step == group[4] + VALUE_LAG:
                dve_combine(k, dve, ch, s, g, group)


def dve_combine(k, dve, ch, s, g, group):
    kind, i, h0, n, end = group
    w = k.aw[:, 0:n]
    dve.wait_ge(*k.on("at_out" + s, end))
    dve.wait_ge(*k.on("at_exp" + s, end))
    ch.link(dve.reciprocal(w, k.asum[:, g % 3, 0:n]))
    if kind != "mem":
        b = ("cmp", "sel", "win").index(kind) * HEADS + h0
        ch.link(dve.tensor_tensor(w, w, k.gates[:, i, b:b + n], ALU.mult))
    src = k.ps[:, 5 + g % 3, 0:n * DH].rearrange("p (h d) -> p h d", d=DH)
    wb = w.unsqueeze(2).broadcast_to([P, n, DH])
    at = (768 if kind == "mem" else h0 * DH) - k.cat_from
    dst = k.cat[:, i, at:at + n * DH]
    if kind in ("mem", "cmp"):
        ins = dve.tensor_tensor(dst.rearrange("p (h d) -> p h d", d=DH), src, wb, ALU.mult)
    else:
        tmp = k.work[:, 0, 0:n * DH]
        ch.link(dve.tensor_tensor(tmp.rearrange("p (h d) -> p h d", d=DH), src, wb, ALU.mult))
        ins = dve.tensor_tensor(dst, dst, tmp, ALU.add)
    ins.then_inc(k.sem("at_group" + s), 1)
    dve.wait_ge(*k.on("at_group" + s, g + 1))


def scalar_layer0(k, act):
    act_std(k, act, "fin1", DT, S, NORM_BANK)
    act_memory(k, act, 0, "fin1_x")
    act_norm_stats(k, act, "l0", after=("fin1_x", DT))
    act_scale_split(k, act, "l0", None, lambda t: k.h_hi[:, t], DT, S)
    act.dma_start(k.pos[:], k.pos_dram).then_inc(k.sem("pos_landed"), 16)
    act.dma_start(k.w2[:], k.w2_dram).then_inc(k.sem("w2_landed"), 16)
    act.dma_start(k.w1[:], k.w1_dram[0]).then_inc(k.sem("w1_landed"), 16)
    act_linear(k, act, "nsa", slots=6)
    act.wait_ge(*k.on("ks_ready", 1))
    dup_keys(k, act, k.kT1, k.kds)
    act_linear(k, act, "nsa", first=6, slots=5)
    act.wait_ge(*k.on("kw_ready", 1))
    dup_keys(k, act, k.kT2, k.kdw)
    for v in range(2):
        act.wait_ge(*k.on("cmp_hidden", v + 1))
        if v == 0:
            act.dma_start(k.w1[:], k.w1_dram[1]).then_inc(k.sem("w1_landed"), 16)
        act.activation(k.hidc[:, v].rearrange("p (half n) -> p half n", half=2), k.ps[:, 2 * v:2 * v + 2, 0:62],
                       ACT.Gelu_apprx_tanh) \
            .then_inc(k.sem("cmp_gelu"), 1)
    act.wait_ge(*k.on("gates_sum", 4))
    act.activation(k.gates[:], k.gates[:], ACT.Sigmoid).then_inc(k.sem("gates"), 1)
    act.wait_ge(*k.on("cmp_out", 2))
    for h, slope in enumerate(alibi_slopes()):
        act.activation(k.table[:, h], k.col("dist", 0, S), ACT.Copy, scale=-slope).then_inc(k.sem("tables"), 1)
        act.activation(k.table_c[:, h], k.col("dist_c", 0, 4 * N_CMP), ACT.Copy, scale=-slope) \
            .then_inc(k.sem("tables"), 1)
    act_attention(k, act, ("cmp", "sel", "win", "mem"), "0")
    act_cat_split(k, act, "0", range(DT))
    act_project(k, act, "wo0", "nfb")
    act_ffn(k, act, "b", None)


def act_norm_stats(k, act, name, after=None):
    if after:
        act.wait_ge(*k.on(after[0], after[1]))
    act_squares(k, act, name, lambda t: k.xT[:, t], DT, S)
    act_std(k, act, name, DT, S, 0)


def dup_keys(k, act, src, dst):
    for odd in range(2):
        rows = slice(odd * DH, odd * DH + DH)
        for half in range(2):
            act.dma_start(dst[half * DH:half * DH + DH, odd::2], src[rows]).then_inc(k.sem("keys_twice"), 16)


def turn_bank(s, n):
    return (bank_pair(PH["wo" + s][1]) + 4) % 8 + n % 2


def act_cat_split(k, act, s, tiles):
    for n, c in enumerate(tiles):
        act.wait_ge(*k.on("cat_turned" + s, n + 1))
        act.activation(k.xs_hi[:, c], k.ps[:, turn_bank(s, n)], ACT.Copy).then_inc(k.sem("cat_hi" + s), 1)


def pe_cat_turn(k, pe, s, tiles):
    for n, c in enumerate(tiles):
        if n >= 2:
            pe.wait_ge(*k.on("cat_lo" + s, n - 1))
        for i in range(4):
            mm = pe.transpose(k.ps[:, turn_bank(s, n), i * P:(i + 1) * P], k.cat[:, i, c * P - k.cat_from:(c + 1) * P - k.cat_from],
                              k.col("ident", 0, P))
        mm.then_inc(k.sem("cat_turned" + s), 1)


def dve_cat_split(k, dve, s, tiles):
    for n, c in enumerate(tiles):
        dve.wait_ge(*k.on("cat_hi" + s, n + 1))
        dve.tensor_tensor(k.xs_lo[:, c], k.ps[:, turn_bank(s, n)], k.xs_hi[:, c].bitcast(F32), ALU.subtract) \
            .then_inc(k.sem("cat_lo" + s), 1)


def tensor_layer0(k, pe):
    pe_all_taken(k, pe, "memkv0")
    pe.wait_ge(*k.on("fin1_std", 1))
    pe_memory(k, pe, 0)
    pe_all_taken(k, pe, "nsa")
    pe_squares(k, pe, "l0", DT, S, 0, k.inv_d)
    h = (k.h_hi, k.h_lo)
    pe_linear(k, pe, "nsa", h, slots=6, ready="l0_lo")
    pe_linear(k, pe, "nsa", h, first=6, slots=1, width=256, natural=True)
    pe_linear(k, pe, "nsa", h, first=7, slots=1)
    pe_linear(k, pe, "nsa", h, first=8, slots=1, width=256, natural=True)
    pe_linear(k, pe, "nsa", h, first=9, slots=1, width=36, natural=True)
    pe_linear(k, pe, "nsa", h, first=10, slots=1)
    pe_all_taken(k, pe, "wo0")
    for v in range(2):
        pe.wait_ge(*k.on("w1_landed", 16 * (v + 1)))
        pe.wait_ge(*k.on("blocks", v + 1))
        for half in range(2):
            rows = slice(half * DH, half * DH + DH)
            for l in range(32):
                mm = pe.matmul(k.ps[:, 2 * v + half, 0:62], k.w1[rows, l, :], k.blocks[rows, :, :, l],
                               start=(l == 0), stop=(l == 31))
        mm.then_inc(k.sem("cmp_hidden"), 1)
    pe.wait_ge(*k.on("w2_landed", 16))
    pe.wait_ge(*k.on("cmp_gelu", 1))
    pe.matmul(k.ps[:, 4, 0:4 * N_CMP], k.w2[:, 0:P], k.hidc[:, 0], start=True, stop=True) \
        .then_inc(k.sem("cmp_k"), 1)
    pe.wait_ge(*k.on("cmp_gelu", 2))
    for g in range(GROUPS):
        c = (g % 2) * 62 + (g // 2) * N_CMP
        mm = pe.matmul(k.ps[0:N_CMP, 5, g * DH:(g + 1) * DH], k.hidc[:, 1, c:c + N_CMP], k.w2[:, P:P + DH],
                       start=True, stop=True)
    mm.then_inc(k.sem("cmp_v"), 1)
    pe.wait_ge(*k.on("cmp_out", 2))
    pe.wait_ge(*k.on("keys_twice", 16 * 8))
    pe_attention(k, pe, ("cmp", "sel", "win", "mem"), "0")
    pe.wait_ge(*k.on("at_group0", 28))
    pe_cat_turn(k, pe, "0", range(DT))
    pe_project(k, pe, "wo0", (k.xs_hi, k.xs_lo), "nfb", ready="cat_lo0")
    pe_ffn(k, pe, "b")


def vector_layer0(k, dve, ch):
    dve_norm_in_place(k, dve, "fin1", lambda t: pcol(k, "final_g", t))
    dve_memory(k, dve, 0)
    dve_rstd(k, dve, "l0", S)
    dve_scale_split(k, dve, "l0", lambda t: k.xT[:, t], lambda t: pcol(k, "norm1", t), None,
                    lambda t: k.h_lo[:, t], lambda t: k.h_hi[:, t], DT, S)
    n0, u0 = PH["nsa"]

    def take(j, sem=None):
        dve.wait_ge(*k.on("mm_done", 2 * (n0 + j + 1)))
        return bank_pair(u0 + j)

    for j in range(3):
        b = take(j)
        dve.tensor_scalar(k.nq[:, 2 * j:2 * j + 2], k.ps[:, b:b + 2], 0.125, None, ALU.mult) \
            .then_inc(k.sem("psum_free"), 1)
    for j, dst in ((3, k.kcT), (4, k.vcT), (5, k.kT1)):
        b = take(j)
        dve.tensor_copy(dst[:], k.ps[:, b:b + 2]).then_inc(k.sem("psum_free"), 1)
    dve.wait_ge(*k.on("psum_free", 4 + u0 + 6))
    dve.memset(k.zero[:], 0.0).then_inc(k.sem("ks_ready"), 1)
    dve.wait_ge(*k.on("pos_landed", 16))
    dve_blocks(k, dve, 0, k.kcT)

    def natural(j, dst):
        b = take(j)
        for e in range(2):
            ins = dve.tensor_copy(dst[:, 2 * e:2 * e + 2], k.ps[:, b + e].rearrange("p (t c) -> p t c", t=2))
        ins.then_inc(k.sem("psum_free"), 1)

    natural(6, k.vs)
    b = take(7)
    dve.wait_ge(*k.on("keys_twice", 16 * 4))
    dve.tensor_copy(k.kT2[:], k.ps[:, b:b + 2]).then_inc(k.sem("psum_free"), 1)
    dve.wait_ge(*k.on("psum_free", 4 + u0 + 8))
    dve.memset(k.zero[:], 0.0).then_inc(k.sem("kw_ready"), 1)
    natural(8, k.vw)
    b = take(9)
    for t in range(4):
        dve.tensor_tensor(k.gates[:, t], k.ps[:, b + t // 2, (t % 2) * 36:(t % 2) * 36 + 36],
                          k.col("row_gate_b", 0, 36), ALU.add).then_inc(k.sem("gates_sum"), 1)
    dve.wait_ge(*k.on("gates_sum", 4))
    dve.memset(k.zero[:], 0.0).then_inc(k.sem("psum_free"), 1)
    b = take(10)
    dve.tensor_scalar(k.mq[:], k.ps[:, b:b + 2], 0.125, None, ALU.mult).then_inc(k.sem("psum_free"), 1)
    dve.wait_ge(*k.on("cmp_hidden", 1))
    dve_blocks(k, dve, 1, k.vcT)
    dve.wait_ge(*k.on("cmp_k", 1))
    for half in range(2):
        ins = dve.tensor_copy(
            k.kcb[:].rearrange("p (pair half n) -> p half pair n", half=2, n=N_CMP)[:, half],
            k.ps[:, 4, half * 62:(half + 1) * 62].rearrange("p (pair n) -> p pair n", n=N_CMP))
    ins.then_inc(k.sem("cmp_out"), 1)
    dve.wait_ge(*k.on("cmp_v", 1))
    dve.tensor_copy(flat(k.vcb[:]), k.ps[0:N_CMP, 5, 0:4 * DH]).then_inc(k.sem("cmp_out"), 1)
    dve.wait_ge(*k.on("cmp_out", 2))
    ch.link(dve.memset(k.azero[:], 0.0))
    dve.wait_ge(*k.on("tables", 2 * HEADS))
    dve.wait_ge(*k.on("gates", 1))
    dve_attention(k, dve, ch, ("cmp", "sel", "win", "mem"), "0")
    dve_cat_split(k, dve, "0", range(DT))
    dve_residual(k, dve, ch, "wo0", None)
    dve_ffn(k, dve, ch, "b", lambda t: pcol(k, "norm2", t), None, None)


def dve_blocks(k, dve, v, src):
    for pair in range(2):
        for a in range(2):
            t = src[:, pair].rearrange("p (m b) -> p m b", b=16)[:, a:a + N_CMP]
            pos = k.pos[:, v, a * 16:(a + 1) * 16].unsqueeze(1).broadcast_to([P, N_CMP, 16])
            ins = dve.tensor_tensor(k.blocks[:, pair, :, a * 16:(a + 1) * 16], t, pos, ALU.add)
    ins.then_inc(k.sem("blocks"), 1)


SETS = HEADS // 4
CH = S // CHUNK
DECAY = float(np.float32(np.exp(-0.5)))
HALVES = (slice(0, DH), slice(DH, P))


def rw_orders():
    pe, act, dve = [], [], []
    for t in range(21):
        act.append(("z", t))
        dve.append(("shift", t))
    act += ["tanh", "sig_g"]
    dve.append("omka")
    for s in range(SETS):
        for p in range(2):
            pe += [(n, s, p) for n in ("U", "A", "TV", "SS", "BON", "TB", "TK", "AA", "AC", "BC")]
            act += [(n, s, p) for n in ("sgw", "a", "kk2", "W", "Wi", "Wp", "std", "natB", "natK")]
            dve += [(n, s, p) for n in ("kk0", "L", "kp", "rk", "at", "hats", "rt", "natV", "bv", "D", "O", "DT",
                                        "CP", "BT", "CV")]
        for stage in (("D2", "D2T"), ("D4", "D4T", "X1"), ("D8", "X2"), ("X3",), ("ZT", "X", "Z"), ("Z2",),
                      ("U2",), ("TT",)):
            for p in range(2):
                pe += [(n, s, p) for n in stage if n not in ("X1", "Z")]
                act += [(n, s, p) for n in stage if n in ("D2T", "D4T", "X", "Z", "Z2")]
                if stage[0] == "D2":
                    dve.append(("XT", s, p))
                if stage[0] == "Z2":
                    dve.append(("IZ", s, p))
                dve += [(n, s, p) for n in stage if n not in ("D2T", "D4T", "Z", "X", "Z2")]
        dve.append(("M0", s))
        for c in range(CH):
            pe += [("G", s, c), ("P", s, c), ("M", s, c), ("Y", s, c)]
            dve += [("G", s, c), ("P", s, c), ("M", s, c)]
        pe += [(n, s, p) for n in ("g", "mean", "var") for p in range(2)]
        act += [(n, s, p) for n in ("ysq", "ystd") for p in range(2)]
        dve += [(n, s, p) for n in ("y", "yc", "out") for p in range(2)]
    return {"pe": pe, "act": act, "dve": dve}


class Steps:

    ORDERS = rw_orders()
    NUMBER = {e: {name: n + 1 for n, name in enumerate(order)} for e, order in ORDERS.items()}

    def __init__(self, k, engine, eng):
        self.k, self.engine, self.eng, self.n = k, engine, eng, 0
        self.sem = k.sem("rw_" + engine)

    def done(self, ins, name):
        assert self.ORDERS[self.engine][self.n] == name, (self.engine, self.n, name)
        self.n += 1
        ins.then_inc(self.sem, 1)

    def after(self, engine, name):
        self.eng.wait_ge(self.k.sem("rw_" + engine), self.NUMBER[engine][name])


def chunks(ap):
    return ap.rearrange("p (c n) -> p c n", n=CHUNK)


def pe_small(k, pe, bank, lhs, rhs, transpose=False):
    for c in range(CH):
        for half in HALVES:
            cs = slice(c * CHUNK, (c + 1) * CHUNK)
            out = k.ps[half, bank, cs]
            mm = pe.matmul(out, lhs[half, cs], k.i64[half, :] if transpose else rhs[half, cs],
                           start=True, stop=True)
    return mm


def pe_twofold(k, pe, bank, lhs, rhs):
    for c in range(CH):
        for half in HALVES:
            out = k.ps[half, bank + c // 4, c % 4 * 2 * CHUNK:(c % 4 + 1) * 2 * CHUNK]
            mm = pe.matmul(out.rearrange("p (x n) -> p x n", x=2), lhs[half, c * CHUNK:(c + 1) * CHUNK],
                           rhs(half, c), start=True, stop=True)
    return mm


def twofold(k, bank, x):
    return k.ps[:, bank:bank + 2].rearrange("p b (c x n) -> p (b c) x n", x=2, n=CHUNK)[:, :, x]


def apart(tensor, half, first, second):
    d = second - first
    return tensor[half, first:first + 2 * d].rearrange("p (x m) -> p x m", x=2)[:, :, 0:CHUNK]


def tensor_layer1(k, pe):
    st = Steps(k, "pe", pe)
    pe_memory(k, pe, 1)
    pe_all_taken(k, pe, "rwkv")
    pe_squares(k, pe, "l1", DT, S, 0, k.inv_d)
    pe_linear(k, pe, "rwkv", (k.h_hi, k.h_lo), ready="l1_lo")
    pe_all_taken(k, pe, "wo1")
    pe.wait_ge(*k.on("rw_params", 16 * 4))
    st.after("act", "sig_g")
    for s in range(SETS):
        for p in range(2):
            j = 2 * s + p
            js = slice(j * P, (j + 1) * P)
            if s or p:
                st.after("dve", ("CV", s, 0) if p else ("out", s - 1, 1))
                st.after("act", ("natK", s, 0) if p else ("ystd", s - 1, 1))
            st.done(pe.matmul(k.ps[:, 0], k.wa2[HALVES[0], js], k.zwa[HALVES[0]], start=True, stop=True), ("U", s, p))
            st.done(pe.matmul(k.ps[:, 1], k.wa2[HALVES[1], js], k.zwa[HALVES[1]], start=True, stop=True), ("A", s, p))
            st.done(pe_small(k, pe, 6, k.v3[:, j], None, transpose=True), ("TV", s, p))
            st.after("act", ("kk2", s, p))
            st.done(pe.matmul(k.ps[:, 2], k.blk1[:], k.t3, start=True, stop=True), ("SS", s, p))
            st.after("dve", ("rk", s, p))
            st.done(pe.matmul(k.ps[:, 3], k.blk1[:], k.tb, start=True, stop=True), ("BON", s, p))
            pe_stay_warm(k, pe, 7, 9)
            st.after("dve", ("hats", s, p))
            st.done(pe_small(k, pe, 4, k.t2, None, transpose=True), ("TB", s, p))
            st.done(pe_small(k, pe, 5, k.t4, None, transpose=True), ("TK", s, p))
            st.done(pe_small(k, pe, 7, k.at[:, p], k.t2), ("AA", s, p))

            def at_rt(half, c):
                return apart(k.wide, half, k.at_in_wide + p * S + c * CHUNK, k.r3_in_wide + j * S + c * CHUNK)

            st.after("act", ("std", s, p))
            st.after("dve", ("rt", s, p))
            st.done(pe_twofold(k, pe, 0, k.t2, at_rt), ("AC", s, p))
            st.after("dve", ("bv", s, p))
            st.done(pe_twofold(k, pe, 2, k.t4, at_rt), ("BC", s, p))
        for p in range(2):
            b = 4 * p
            st.after("dve", ("CV", s, 1))
            st.after("act", ("natK", s, 1))
            st.done(pe_small(k, pe, b, k.DT_[p], k.D_[p]), ("D2", s, p))
            st.done(pe_small(k, pe, b + 1, k.D_[p], k.DT_[p]), ("D2T", s, p))
        for p in range(2):
            b = 4 * p
            st.after("dve", ("D2", s, p))
            st.after("act", ("D2T", s, p))
            st.done(pe_small(k, pe, b, k.D2T_[p], k.D2_[p]), ("D4", s, p))
            st.done(pe_twofold(k, pe, b + 1, k.D2_[p], lambda half, c: k.DX[p][half, :, c * CHUNK:(c + 1) * CHUNK]),
                    ("D4T", s, p))
        for p in range(2):
            b = 4 * p
            st.after("dve", ("X1", s, p))
            st.after("act", ("D4T", s, p))
            st.done(pe_small(k, pe, b, k.DT_[p], k.D_[p]), ("D8", s, p))
            st.done(pe_small(k, pe, b + 1, k.D_[p], k.XT_[p]), ("X2", s, p))
        for p in range(2):
            st.after("dve", ("X2", s, p))
            st.done(pe_small(k, pe, 4 * p + 2, k.D2_[p], k.XT_[p]), ("X3", s, p))
        for p in range(2):
            b = 4 * p
            st.after("dve", ("X3", s, p))
            st.done(pe_small(k, pe, b, k.O_[p], k.XT_[p]), ("ZT", s, p))
            st.done(pe_twofold(k, pe, b + 1, k.XT_[p], lambda half, c: apart(
                k.mats, half, k.i64_in_mats, k.O_in_mats[p] + c * CHUNK)), ("X", s, p))
        for p in range(2):
            st.after("dve", ("ZT", s, p))
            st.after("act", ("Z", s, p))
            st.done(pe_small(k, pe, 4 * p + 3, k.DT_[p], k.D_[p]), ("Z2", s, p))
        for p in range(2):
            st.after("act", ("Z2", s, p))
            st.after("dve", ("IZ", s, p))
            st.done(pe_small(k, pe, 4 * p, k.D2T_[p], k.E_[p]), ("U2", s, p))
        for p in range(2):
            st.after("dve", ("U2", s, p))
            st.done(pe_small(k, pe, 4 * p + 1, k.D2_[p], k.E_[p]), ("TT", s, p))
        st.after("dve", ("TT", s, 1))
        st.after("dve", ("M0", s))
        for c in range(CH):
            cs = slice(c * CHUNK, (c + 1) * CHUNK)
            m = c % 2
            if c:
                st.after("dve", ("M", s, c - 1))
            for p in range(2):
                for half in HALVES:
                    out = k.ps[half, 0, p * DH:(p + 1) * DH]
                    pe.matmul(out, k.at[half, p, cs], k.M[half, m, p], start=True, stop=False)
                    mm = pe.matmul(out, k.BT[half, p, cs], k.nV[half, p, cs], start=False, stop=True)
            st.done(mm, ("G", s, c))
            st.after("dve", ("G", s, c))
            for p in range(2):
                for half in HALVES:
                    mm = pe.matmul(k.ps[half, 1, p * DH:(p + 1) * DH], k.TT[half, p, cs], k.G[half, p],
                                   start=True, stop=True)
            st.done(mm, ("P", s, c))
            st.after("dve", ("P", s, c))
            for p in range(2):
                for half in HALVES:
                    out = k.ps[half, 2, p * DH:(p + 1) * DH]
                    pe.matmul(out, k.nB[half, p, cs], k.Pm[half, m, p], start=True, stop=False)
                    mm = pe.matmul(out, k.nK[half, p, cs], k.nV[half, p, cs], start=False, stop=True)
            st.done(mm, ("M", s, c))
            for p in range(2):
                j = 2 * s + p
                for half in HALVES:
                    out = k.ps[half, 4 + p, cs]
                    pe.matmul(out, k.M[half, m, p], k.r3[half, j, cs], start=True, stop=False)
                    pe.matmul(out, k.Pm[half, m, p], k.CP[half, p, cs], start=False, stop=False)
                    mm = pe.matmul(out, k.nV[half, p, cs], k.CV[half, p, cs], start=False, stop=True)
            st.done(mm, ("Y", s, c))
        for p in range(2):
            js = slice((2 * s + p) * P, (2 * s + p + 1) * P)
            pe.matmul(k.ps[:, 6 + p], k.g2a[:, js], k.zg0, start=True, stop=False)
            st.done(pe.matmul(k.ps[:, 6 + p], k.g2b[0:32, js], k.zg1[0:32], start=False, stop=True), ("g", s, p))
        for p in range(2):
            st.after("dve", ("y", s, p))
            st.done(pe.matmul(k.ps[:, 0 + p], k.blkm[:], k.k3[:, 2 * s + p], start=True, stop=True), ("mean", s, p))
        for p in range(2):
            st.after("act", ("ysq", s, p))
            st.done(pe.matmul(k.ps[:, 2 + p], k.blkm[:], k.ysq[p], start=True, stop=True), ("var", s, p))
        pe_stay_warm(k, pe, 5, 13)
    st.after("dve", ("out", SETS - 1, 1))
    pe_attention(k, pe, ("mem",), "1")
    pe.wait_ge(*k.on("at_group1", 4))
    pe_cat_turn(k, pe, "1", range(6, DT))
    pe.wait_ge(*k.on("cat_lo1", 2))
    pe.wait_ge(*k.on("mix_lo", 6))
    pe_project(k, pe, "wo1", (k.xs_hi, k.xs_lo), "nfc")
    pe_ffn(k, pe, "c")


def scalar_layer1(k, act):
    st = Steps(k, "act", act)
    act_memory(k, act, 1)
    act_norm_stats(k, act, "l1")
    act_scale_split(k, act, "l1", None, lambda t: k.h_hi[:, t], DT, S)
    for dst, src in ((k.wa2, k.wa2_dram), (k.g2a, k.g2_dram[0:P]), (k.g2b[0:32], k.g2_dram[P:P + 32]),
                     (k.rconst, k.rconst_dram)):
        act.dma_start(dst, src).then_inc(k.sem("rw_params"), 16)
    n0, u0 = PH["rwkv"]
    for j in range(12):
        act_slot(k, act, n0 + j, 0, 4)
        if j < 11:
            for e in range(2):
                t = 2 * j + e
                if t < 21:
                    if t >= 2:
                        st.after("dve", ("shift", t - 2))
                    st.done(act.activation(k.zbuf[:, t % 2, 1:1 + S], k.ps[:, bank_pair(u0 + j) + e],
                                           ACT.Copy), ("z", t))
    st.after("dve", ("shift", 20))
    st.done(act.activation(k.zwa[HALVES[0]], k.zwa[HALVES[0]], ACT.Tanh), "tanh")
    act.activation(k.zg0, k.zg0, ACT.Sigmoid)
    st.done(act.activation(k.zg1[0:32], k.zg1[0:32], ACT.Sigmoid), "sig_g")
    for s in range(SETS):
        for p in range(2):
            j = 2 * s + p
            st.after("pe", ("U", s, p))
            if s or p:
                st.after("pe", ("BC", s, 0) if p else ("var", s - 1, 1))
                st.after("dve", ("CV", s, 0) if p else ("out", s - 1, 1))
            st.done(act.activation(k.t0, k.ps[:, 0], ACT.Sigmoid, bias=pcol(k, "w0", j)), ("sgw", s, p))
            st.after("pe", ("A", s, p))
            st.done(act.activation(k.ta, k.ps[:, 1], ACT.Sigmoid, bias=pcol(k, "a0", j)), ("a", s, p))
            st.after("dve", ("kk0", s, p))
            st.done(act.activation(k.t3, k.t2, ACT.Square), ("kk2", s, p))
            st.after("dve", ("L", s, p))
            st.done(act.activation(k.t5, k.t1, ACT.Exp), ("W", s, p))
            st.done(act.activation(k.t6, k.t1, ACT.Exp, scale=-1.0), ("Wi", s, p))
            st.done(act.activation(k.t0, k.t0, ACT.Exp), ("Wp", s, p))
            st.after("pe", ("SS", s, p))
            st.done(act.activation(k.t3, k.ps[:, 2], ACT.Sqrt), ("std", s, p))
            for n, bank, dst, src in (("natB", 4, k.nB, "TB"), ("natK", 5, k.nK, "TK")):
                st.after("pe", (src, s, p))
                st.done(act.activation(dst[:, p], k.ps[:, bank], ACT.Copy), (n, s, p))
        for stage in (("D2T",), ("D4T",), ("X", "Z"), ("Z2",)):
            for p in range(2):
                for n in stage:
                    b = 4 * p
                    dst, src = {
                        "D2T": (k.D2T_[p], k.ps[:, b + 1]),
                        "D4T": (chunks(k.DT_[p]), twofold(k, b + 1, 0)),
                        "X": (chunks(k.D2_[p]), twofold(k, b + 1, 0)),
                        "Z": (chunks(k.D_[p]), twofold(k, b + 1, 1)),
                        "Z2": (k.D2T_[p], k.ps[:, b + 3]),
                    }[n]
                    st.after("pe", ("X" if n == "Z" else n, s, p))
                    st.done(act.activation(dst, src, ACT.Copy), (n, s, p))
        for p in range(2):
            st.after("dve", ("yc", s, p))
            st.done(act.activation(k.ysq[p], k.k3[:, 2 * s + p], ACT.Square), ("ysq", s, p))
        for p in range(2):
            st.after("pe", ("var", s, p))
            st.done(act.activation(k.ystd[p], k.ps[:, 2 + p], ACT.Sqrt, bias=k.gn_eps[:, 0:1]), ("ystd", s, p))
    act_attention(k, act, ("mem",), "1")
    for t in range(6):
        act.activation(k.xs_hi[:, t], k.k3[:, t], ACT.Copy).then_inc(k.sem("mix_hi"), 1)
    act_cat_split(k, act, "1", range(6, DT))
    act_project(k, act, "wo1", "nfc")
    act_ffn(k, act, "c", None)
    act_std(k, act, "fin2", DT, S, NORM_BANK)


def vector_layer1(k, dve, ch):
    st = Steps(k, "dve", dve)
    dve_memory(k, dve, 1)
    dve_rstd(k, dve, "l1", S)
    dve_scale_split(k, dve, "l1", lambda t: k.xT[:, t], lambda t: pcol(k, "norm1", 8 + t), None,
                    lambda t: k.h_lo[:, t], lambda t: k.h_hi[:, t], DT, S)
    ch.link(dve.memset(k.zbuf[:, :, 0:1], 0.0))
    ch.link(dve.memset(k.gn_eps[:], GN_EPS))
    n0, u0 = PH["rwkv"]
    dsts = [k.r3[:, t] for t in range(6)] + [k.k3[:, t] for t in range(6)] + [k.v3[:, t] for t in range(6)] \
        + [k.zwa, k.zg0, k.zg1]
    for t in range(21):
        st.after("act", ("z", t))
        z = k.zbuf[:, t % 2]
        ch.link(dve.tensor_tensor(k.work[:, t % 2], z[:, 0:S], z[:, 1:1 + S], ALU.subtract))
        st.done(dve.scalar_tensor_tensor(dsts[t], k.work[:, t % 2], pcol(k, "mu", t), z[:, 1:1 + S],
                                         ALU.mult, ALU.add), ("shift", t))
        if t % 2 or t == 20:
            dve.memset(k.zero[:], 0.0).then_inc(k.sem("psum_free"), 1)
    dve.wait_ge(*k.on("mm_done", 2 * (n0 + 12)))
    b = bank_pair(u0 + 11)
    dve.tensor_scalar(k.mq[:], k.ps[:, b:b + 2], 0.125, None, ALU.mult).then_inc(k.sem("psum_free"), 1)
    st.done(dve.tensor_scalar(k.omka[:], k.col("k_a", 0, 6), -1.0, 1.0, ALU.mult, ALU.add), "omka")
    ch.link(dve.memset(k.again[:], 1.0))
    ch.link(dve.memset(chunks(k.again)[:, :, 0:1], 0.0))
    dve.wait_ge(*k.on("rw_params", 16 * 4))
    for s in range(SETS):
        for p in range(2):
            vector_pair(k, dve, ch, st, s, p)
        vector_inverse(k, dve, ch, st, s)
        st.done(dve.memset(k.M[:, 0], 0.0), ("M0", s))
        for c in range(CH):
            m = c % 2
            st.after("pe", ("G", s, c))
            st.done(dve.tensor_copy(flat(k.G[:]), k.ps[:, 0, 0:P]), ("G", s, c))
            st.after("pe", ("P", s, c))
            st.done(dve.tensor_copy(flat(k.Pm[:, m]), k.ps[:, 1, 0:P]), ("P", s, c))
            st.after("pe", ("M", s, c))
            if c == 0:
                st.after("dve", ("M0", s))
            else:
                st.after("dve", ("M", s, c - 1))
                st.after("pe", ("Y", s, c - 1))
            ch.link(dve.tensor_tensor(flat(k.M[:, 1 - m]), k.ps[:, 2, 0:P], flat(k.M[:, m]), ALU.add))
            st.done(dve.tensor_tensor(k.M[:, 1 - m], k.M[:, 1 - m],
                                      k.wc[:, :, c:c + 1].broadcast_to([P, 2, DH]), ALU.mult), ("M", s, c))
        ys = [k.k3[:, 2 * s + p] for p in range(2)]
        st.after("pe", ("Y", s, CH - 1))
        for p in range(2):
            st.done(dve.tensor_copy(ys[p], k.ps[:, 4 + p]), ("y", s, p))
        for p in range(2):
            st.after("dve", ("y", s, p))
            st.after("pe", ("mean", s, p))
            st.done(dve.tensor_tensor(ys[p], ys[p], k.ps[:, 0 + p], ALU.subtract), ("yc", s, p))
        for p in range(2):
            j, y = 2 * s + p, ys[p]
            st.after("act", ("ystd", s, p))
            st.after("dve", ("yc", s, p))
            ch.link(dve.reciprocal(k.ystd[p], k.ystd[p]))
            ch.link(dve.tensor_tensor(y, y, k.ystd[p], ALU.mult))
            ch.link(dve.tensor_scalar(y, y, pcol(k, "lnx_w", j), pcol(k, "lnx_b", j), ALU.mult, ALU.add))
            ch.link(dve.tensor_tensor(y, y, k.v3[:, j], ALU.add))
            st.after("pe", ("g", s, p))
            st.done(dve.tensor_tensor(y, k.ps[:, 6 + p], y, ALU.mult), ("out", s, p))
    ch.link(dve.memset(k.azero[:], 0.0))
    dve_attention(k, dve, ch, ("mem",), "1")
    for t in range(6):
        dve.wait_ge(*k.on("mix_hi", t + 1))
        dve.tensor_tensor(k.xs_lo[:, t], k.k3[:, t], k.xs_hi[:, t].bitcast(F32), ALU.subtract) \
            .then_inc(k.sem("mix_lo"), 1)
    dve_cat_split(k, dve, "1", range(6, DT))
    dve_residual(k, dve, ch, "wo1", None)
    dve_ffn(k, dve, ch, "c", lambda t: pcol(k, "norm2", 8 + t), None, None)
    dve_norm_in_place(k, dve, "fin2", lambda t: pcol(k, "final2", t))


def vector_pair(k, dve, ch, st, s, p):
    j = 2 * s + p
    r, kk, v = k.r3[:, j], k.k3[:, j], k.v3[:, j]
    if s or p:
        st.after("pe", ("BC", s, 0) if p else ("var", s - 1, 1))
        st.after("act", ("natK", s, 0) if p else ("ystd", s - 1, 1))
        st.after("dve", ("CV", s, 0) if p else ("out", s - 1, 1))
    st.done(dve.tensor_scalar(k.t2, kk, pcol(k, "k_k", j), None, ALU.mult), ("kk0", s, p))
    st.after("act", ("sgw", s, p))
    ch.link(dve.tensor_scalar(k.t0, k.t0, -DECAY, None, ALU.mult))
    ch.link(dve.tensor_tensor_scan(k.t1, k.again, k.t0, 0.0, ALU.mult, ALU.add))
    st.done(dve.tensor_tensor(k.t0, k.t1, k.t0, ALU.subtract), ("L", s, p))
    st.after("act", ("a", s, p))
    ch.link(dve.tensor_scalar(k.t4, k.ta, pcol(k, "k_a", j), k.omka[:, j:j + 1], ALU.mult, ALU.add))
    st.after("dve", ("kk0", s, p))
    st.done(dve.tensor_tensor(kk, kk, k.t4, ALU.mult), ("kp", s, p))
    st.after("dve", ("kp", s, p))
    st.done(dve.scalar_tensor_tensor(k.tb, r, pcol(k, "r_k", j), kk, ALU.mult, ALU.mult), ("rk", s, p))
    st.after("act", ("std", s, p))
    ch.link(dve.tensor_scalar(k.t3, k.t3, 1e-12, None, ALU.max))
    ch.link(dve.reciprocal(k.t3, k.t3))
    ch.link(dve.tensor_tensor(k.t2, k.t2, k.t3, ALU.mult))
    st.done(dve.scalar_tensor_tensor(k.at[:, p], k.t2, -1.0, k.t0, ALU.mult, ALU.mult), ("at", s, p))
    st.after("dve", ("at", s, p))
    ch.link(dve.tensor_tensor(k.t2, k.t2, k.ta, ALU.mult))
    ch.link(dve.tensor_tensor(k.t2, k.t2, k.t6, ALU.mult))
    st.done(dve.tensor_tensor(k.t4, kk, k.t6, ALU.mult), ("hats", s, p))
    st.after("act", ("W", s, p))
    st.after("dve", ("rk", s, p))
    st.done(dve.tensor_tensor(r, r, k.t5, ALU.mult), ("rt", s, p))
    ch.link(dve.tensor_copy(k.wc[:, p], chunks(k.t5)[:, :, CHUNK - 1]))
    st.after("pe", ("TV", s, p))
    st.done(dve.tensor_copy(k.nV[:, p], k.ps[:, 6]), ("natV", s, p))
    st.after("pe", ("BON", s, p))
    st.done(dve.tensor_tensor(v, v, k.ps[:, 3], ALU.mult), ("bv", s, p))

    def masked(name, bank, dst, mask, src):
        st.after("pe", (src, s, p))
        st.done(dve.tensor_tensor(chunks(dst), bank,
                                  mask.unsqueeze(1).broadcast_to([P, CH, CHUNK]), ALU.mult), (name, s, p))

    masked("D", chunks(k.ps[:, 7]), k.D_[p], k.m_diag_low, "AA")
    masked("O", chunks(k.ps[:, 7]), k.O_[p], k.m_off_low, "AA")
    masked("DT", twofold(k, 0, 0), k.DT_[p], k.m_diag_up, "AC")
    masked("CP", twofold(k, 0, 1), k.CP[:, p], k.m_up_eq, "AC")
    masked("BT", twofold(k, 2, 0), k.BT[:, p], k.m_up, "BC")
    masked("CV", twofold(k, 2, 1), k.CV[:, p], k.m_up_eq, "BC")


def vector_inverse(k, dve, ch, st, s):
    i64 = k.i64.unsqueeze(1).broadcast_to([P, CH, CHUNK])

    def copy(name, p, bank, dst):
        st.after("pe", (name, s, p))
        st.done(dve.tensor_copy(dst, k.ps[:, 4 * p + bank]), (name, s, p))

    def add(name, p, bank, dst):
        st.after("pe", (name, s, p))
        st.done(dve.tensor_tensor(dst, k.ps[:, 4 * p + bank], dst, ALU.add), (name, s, p))

    for p in range(2):
        st.after("dve", ("DT", s, p))
        st.done(dve.tensor_tensor(chunks(k.XT_[p]), chunks(k.DT_[p]), i64, ALU.add), ("XT", s, p))
        copy("D2", p, 0, k.D2_[p])
    for p in range(2):
        copy("D4", p, 0, k.D_[p])
        st.after("dve", ("XT", s, p))
        st.after("act", ("D4T", s, p))
        x = chunks(k.XT_[p])
        st.done(dve.tensor_tensor(x, twofold(k, 4 * p + 1, 1), x, ALU.add), ("X1", s, p))
    for p in range(2):
        copy("D8", p, 0, k.D2_[p])
        st.after("dve", ("X1", s, p))
        add("X2", p, 1, k.XT_[p])
    for p in range(2):
        st.after("dve", ("X2", s, p))
        add("X3", p, 2, k.XT_[p])
    for p in range(2):
        copy("ZT", p, 0, k.DT_[p])
    for p in range(2):
        st.after("dve", ("ZT", s, p))
        st.done(dve.tensor_tensor(chunks(k.E_[p]), chunks(k.DT_[p]), i64, ALU.add), ("IZ", s, p))
    for p in range(2):
        st.after("dve", ("IZ", s, p))
        add("U2", p, 0, k.E_[p])
    for p in range(2):
        copy("TT", p, 1, k.TT[:, p])


def layer1_map(k, region, h_at, rest_at):
    r = region(h_at)
    r.at[0] += 4 * 2 * S
    k.nB, k.nK, k.nV = (r(n, [P, 2, S]) for n in ("nB", "nK", "nV"))
    k.BT, k.CP, k.CV, k.TT = (r(n, [P, 2, S]) for n in ("BT", "CP", "CV", "TT"))
    k.wide = region(h_at)("wide", [P, 22 * 1024])
    k.at_in_wide, k.r3_in_wide = 0, (rest_at - h_at) // 4
    k.at = k.wide[:, 0:2 * S].rearrange("p (a n) -> p a n", a=2)
    k.r3 = k.wide[:, k.r3_in_wide:k.r3_in_wide + 6 * S].rearrange("p (a n) -> p a n", a=6)
    r = region(h_at)
    hi, lo = r("mix_hi", [P, DT, S], F32R), r("mix_lo", [P, DT, S], F32R)
    mix = (hi, lo)
    r = region(rest_at)
    r.at[0] += 4 * 6 * S
    k.k3, k.v3 = (r(n, [P, 6, S]) for n in ("k3", "v3"))
    mem = (r("mkT1", [P, 2, N_MEM]), r("mv1", [P, 2, N_MEM]), r("mq1", [P, 2, S]))
    z = r("zs", [P, 3, S])
    k.zwa, k.zg0, k.zg1 = (z[:, i] for i in range(3))
    k.wa2, k.g2a, k.g2b = (r(n, [P, 768])[:] for n in ("wa2", "g2a", "g2b"))
    k.omka, k.gn_eps = r("omka", [P, 6]), r("gn_eps", [P, 1])
    k.M, k.Pm, k.G = r("M", [P, 2, 2, DH]), r("Pm", [P, 2, 2, DH]), r("G", [P, 2, DH])
    k.wc = r("wc", [P, 2, CH])
    n_const = 6 * CHUNK + 2 * P
    temps_at = r.at[0] + 4 * n_const
    k.mats = r("mats", [P, n_const + 6 * S])
    k.rconst = k.mats[:, 0:n_const]
    masks = [k.rconst[:, i * CHUNK:(i + 1) * CHUNK] for i in range(6)]
    k.m_up, k.m_up_eq, k.m_diag_low, k.m_diag_up, k.m_off_low, k.i64 = masks
    k.blkm, k.blk1 = k.rconst[:, 384:512], k.rconst[:, 512:640]
    k.i64_in_mats = 5 * CHUNK
    k.O_in_mats = [n_const, n_const + S]
    mats = [k.mats[:, n_const + i * S:n_const + (i + 1) * S] for i in range(6)]
    k.O_, k.D_, k.DT_ = mats[0:2], mats[2:4], mats[4:6]
    tmp = r("tmp", [P, 4, S])
    t = [tmp[:, i] for i in range(4)]
    k.t4, k.t5, k.t6, k.ta = t
    k.again = r("again", [P, S])[:]
    k.t0, k.t1, k.t2, k.t3 = (k.work[:, i] for i in range(4))
    k.tb = k.std[:]
    k.D2_ = [t[0], t[1]]
    k.DX = [tmp[:, 2:4], k.work[:, 0:2]]
    k.D2T_, k.XT_ = [t[2], k.t0], [t[3], k.t1]
    k.E_ = [k.t2, k.t3]
    k.ysq, k.ystd = [k.t0, k.t2], [k.t1, k.t3]
    r = region(temps_at)
    memT, m_hi, m_lo = r("memT1", [P, DT, N_MEM]), r("m_hi1", [P, DT, N_MEM], F32R), None
    k.zbuf = region(temps_at)("zbuf", [P, 2, 1 + S])
    m_lo = region(rest_at)("m_lo1", [P, DT, N_MEM], F32R)
    r = region(temps_at)
    att = (r("cat1", [P, 4, 256]), r("ap1", [P, 4, S]), r("apT1", [P, 3, S]),
           r("azero1", [P, N_MEM]), r("asum1", [P, 3, 6]), r("aw1", [P, 6]), r("amax1", [P, 4]))
    k.layer1_names = (mem, memT, m_hi, m_lo, att, mix, 768)


def layer_names(k, names):
    (k.mkT, k.mv, k.mq), k.memT, k.m_hi, k.m_lo, att, (k.xs_hi, k.xs_lo), k.cat_from = names
    k.cat, k.ap, k.apT, k.azero, k.asum, k.aw, k.amax = att


def build(nc, slots, cols, x, row_bv, sel, mem, pos, w1, w2, wa2, g2, rconst, out):
    with ExitStack() as ctx:
        k = Kernel(nc, ctx)

        def sb(name, shape, dt=F32, stack=ctx):
            return stack.enter_context(nc.sbuf_tensor(name, shape, dt))

        k.n_slots = slots.shape[0]
        k.slots_dram, k.cols_dram, k.x_dram, k.row_bv_dram, k.sel_dram = slots, cols, x, row_bv, sel
        k.out_dram = out
        k.mem_dram, k.pos_dram, k.w1_dram, k.w2_dram = mem, pos, w1, w2
        k.wa2_dram, k.g2_dram, k.rconst_dram = wa2, g2, rconst
        k.ps = ctx.enter_context(nc.psum_tensor("ps", [P, 8, S], F32))
        k.cols = sb("cols", [P, N_COLS])
        k.xT = sb("xT", [P, DT, S])
        k.raw = [sb(f"raw{j}", [P, DT, SLOT_COLS]) for j in range(2)]
        k.w_hi = [sb(f"w_hi{j}", [P, DT, SLOT_COLS], F32R) for j in range(2)]
        k.w_lo = [sb(f"w_lo{j}", [P, DT, SLOT_COLS], F32R) for j in range(2)]
        k.work = sb("work", [P, 4, S])
        k.std = k.rstd = sb("std", [P, S])
        k.inv_d, k.inv_h, k.one = sb("inv_d", [P, P]), sb("inv_h", [P, P]), sb("one", [P, P])
        k.eps, k.zero = sb("eps", [P, 1]), sb("zero", [P, 1])
        k.mod, k.A = sb("mod", [P, 48]), sb("A", [P, 8])
        k.raw_landed = [k.sem("raw_landed_even"), k.sem("raw_landed_odd")]

        h_at = nc.sbuf_base
        rest_at = h_at + 2 * DT * S * 4

        def region(base):
            at = [base]

            def place(name, shape, dt=F32):
                size = 4 * int(np.prod(shape[1:]))
                t = nc.alloc_sbuf_tensor_at(name, shape, dt, offset=at[0])
                at[0] += -(-size // 32) * 32
                return t

            place.at = at
            return place

        h = region(h_at)
        k.h_hi, k.h_lo = h("h_hi", [P, DT, S], F32R), h("h_lo", [P, DT, S], F32R)
        r = region(rest_at)
        k.aT = r("aT", [P, DT, TAPS - 1 + S])
        k.qkT = r("qkT", [P, 2 * DT, S])
        k.qT, k.kT = k.qkT[:, 0:DT], k.qkT[:, DT:2 * DT]
        cs_at = r.at[0] - DT * S * 4
        k.v = r("v", [P, 4, D])
        k.rows = r("rows", [P, 5, S])
        k.gcol = r("gcol", [P, 16])
        k.sel = r("sel", [4, ML_HEADS, P])
        early_at = r.at[0]
        k.row_bv = r("row_bv", [P, 1, D])
        k.row_bv2 = k.row_bv[:].broadcast_to([P, 2, D])
        k.qpre = r("qpre", [P, 2, QK_TAPS - 1 + S])
        k.cb = r("cb", [P, DT, P])
        k.pool_acc, k.pool_tap = r("pool_acc", [P, S]), r("pool_tap", [P, S])
        assert r.at[0] <= SBUF_END
        r = region(early_at)
        k.scT, k.conv_late = r("scT", [P, 1280]), r("conv_late", [P, S])
        k.diag = r("diag", [P, P])
        r = region(cs_at)
        k.cs_hi, k.cs_lo = r("cs_hi", [P, DT, S], F32R), r("cs_lo", [P, DT, S], F32R)
        r = region(rest_at)
        k.hid_hi, k.hid_lo = r("hid_hi", [P, FT, S], F32R), r("hid_lo", [P, FT, S], F32R)
        r = region(rest_at)
        k.nq, k.mq = r("nq", [P, 6, S]), r("mq", [P, 2, S])
        k.kds, k.kdw = r("kds", [P, GROUPS, S]), r("kdw", [P, GROUPS, S])
        k.vs, k.vw = r("vs", [P, 4, 256]), r("vw", [P, 4, 256])
        k.kcb, k.vcb = r("kcb", [P, GROUPS * N_CMP]), r("vcb", [N_CMP, GROUPS, DH])
        k.mkT, k.mv = r("mkT", [P, 2, N_MEM]), r("mv", [P, 2, N_MEM])
        k.gates = r("gates", [P, 4, 36])
        k.hidc = r("hidc", [P, 2, 4 * N_CMP])
        stage_at = r.at[0]
        k.kcT, k.vcT = r("kcT", [P, 2, S]), r("vcT", [P, 2, S])
        k.kT1 = r("kT1", [P, 2, S])
        k.pos, k.w2 = r("pos", [P, 2, 32]), r("w2", [P, P + DH])
        k.blocks = r("blocks", [P, 2, N_CMP, 32])
        k.w1 = r("w1", [P, 32, P])
        k.kT2 = k.kT1
        r = region(stage_at)
        k.memT = r("memT", [P, DT, N_MEM])
        k.m_hi, k.m_lo = r("m_hi", [P, DT, N_MEM], F32R), r("m_lo", [P, DT, N_MEM], F32R)
        r = region(stage_at)
        k.table, k.table_c = r("table", [P, HEADS, S]), r("table_c", [P, HEADS, 4 * N_CMP])
        r = region(stage_at)
        k.xs_hi, k.xs_lo = r("xs_hi", [P, DT, S], F32R), r("xs_lo", [P, DT, S], F32R)
        r = region(h_at)
        k.cat = r("cat", [P, 4, D])
        k.ap, k.apT = r("ap", [P, 4, S]), r("apT", [P, 3, S])
        k.azero = r("azero", [P, N_MEM])
        k.asum, k.aw, k.amax = r("asum", [P, 3, 6]), r("aw", [P, 6]), r("amax", [P, 4])
        assert r.at[0] <= rest_at
        layer1_map(k, region, h_at, rest_at)
        k.layer0_names = ((k.mkT, k.mv, k.mq), k.memT, k.m_hi, k.m_lo,
                          (k.cat, k.ap, k.apT, k.azero, k.asum, k.aw, k.amax), (k.xs_hi, k.xs_lo), 0)

        block = ctx.enter_context(nc.Block())

        @block.sync
        def _(sp):
            sync_program(k, sp)

        @block.gpsimd
        def _(pool):
            gpsimd_program(k, pool)

        @block.scalar
        def _(act):
            layer_names(k, k.layer0_names)
            scalar_block1(k, act)
            scalar_layer0(k, act)
            layer_names(k, k.layer1_names)
            scalar_layer1(k, act)

        @block.vector
        def _(dve):
            ch = Chain(dve, k.sem("vector_step"))
            layer_names(k, k.layer0_names)
            vector_block1(k, dve, ch)
            vector_layer0(k, dve, ch)
            layer_names(k, k.layer1_names)
            vector_layer1(k, dve, ch)

        @block.tensor
        def _(pe):
            layer_names(k, k.layer0_names)
            tensor_block1(k, pe)
            tensor_layer0(k, pe)
            layer_names(k, k.layer1_names)
            tensor_layer1(k, pe)


def layout(inputs):
    a = {name: np.asarray(value) for name, value in inputs.items()}
    pos, w1, w2 = compression_weights(a)
    arrays = {
        "slots": stream_of_weights(a),
        "cols": parameter_columns(a),
        "x": by_tiles(a["x"][0]),
        "row_bv": np.broadcast_to(a["b_in"][0][4096:5120], (P, 1, D)),
        "sel": selectors(),
        "mem": by_tiles(a["mem_2"][0]),
        "pos": pos, "w1": w1, "w2": w2,
        "wa2": np.concatenate([a["rw_w2_2"][0], a["rw_a2_2"][0]]),
        "g2": a["rw_g2_2"][0],
        "rconst": recurrence_constants(),
    }
    return {name + "_dram": np.ascontiguousarray(value) for name, value in arrays.items()}


def kernel(**inputs):
    import concourse.bacc as bacc
    from concourse.bass_utils import run_bass_kernel_spmd

    arrays = layout(inputs)
    nc = bacc.Bacc("TRN2", target_bir_lowering=False, num_devices=1)
    args = [nc.dram_tensor(name, v.shape, F32, kind="ExternalInput").ap() for name, v in arrays.items()]
    args.append(nc.dram_tensor("out_dram", (P, DT, S), F32, kind="ExternalOutput").ap())
    build(nc, *args)
    result = run_bass_kernel_spmd(nc, [arrays], core_ids=[0])
    got = np.asarray(result.results[0]["out_dram"])
    return np.ascontiguousarray(got.transpose(1, 0, 2).reshape(D, S).T)[None]
```
